# Optimizing a Trainium2 kernel written in Bass

```python
import math
import jax, jax.numpy as jnp
from jax import lax
import numpy as np

D_MODEL = 1024
BATCH = 1
SEQ = 256
DEPTH = 2

HEAD_DIM = 64
N_HEADS_DIFF = 4
N_HEADS_DIL = 6
N_HEADS_MOBA = 6
N_HEADS_MIX = N_HEADS_DIFF + N_HEADS_DIL + N_HEADS_MOBA
MIX_WIDTH = N_HEADS_MIX * HEAD_DIM
DIFF_HALF = HEAD_DIM // 2
ROPE_THETA = 500000.0
ROPE_FRACTION = 4
DILATED_PAIRS = ((128, 1), (512, 4), (2048, 16))
MOBA_BLOCK = 256
MOBA_TOPK = 3
MOBA_Q_CHUNK = 64
Q_BLOCK = 128
MEM_LEN = 256
N_HEADS_MEM = 4
MEM_WIDTH = N_HEADS_MEM * HEAD_DIM
D_FF = -(-(8 * D_MODEL) // (3 * 256)) * 256
EPS = 1e-6

kernel_name = "hymba_style_diff_dilated_moba_hybrid"

def rms_norm(x, w):
    xf = x.astype(jnp.float32)
    y = xf * lax.rsqrt(jnp.mean(xf * xf, axis=-1, keepdims=True) + EPS)
    return (y * w.astype(jnp.float32)).astype(x.dtype)

def rotary(x, positions, rot_dim):
    half = rot_dim // 2
    inv_freq = ROPE_THETA ** (-jnp.arange(half, dtype=jnp.float32) / half)
    ang = positions.astype(jnp.float32)[..., None] * inv_freq
    cos = jnp.cos(ang)[:, :, None, :]
    sin = jnp.sin(ang)[:, :, None, :]
    xr = x[..., :rot_dim].astype(jnp.float32)
    x1, x2 = xr[..., :half], xr[..., half:]
    rot = jnp.concatenate([x1 * cos - x2 * sin, x2 * cos + x1 * sin], axis=-1).astype(x.dtype)
    return jnp.concatenate([rot, x[..., rot_dim:]], axis=-1)

def diff_qk_prep(t, gain, positions):
    B, S, H, _ = t.shape
    t = t.reshape(B, S, 2 * H, DIFF_HALF)
    t = rotary(rms_norm(t, gain), positions, DIFF_HALF // ROPE_FRACTION)
    return t.reshape(B, S, H, 2, DIFF_HALF)

def diff_attention(q1, q2, k1, k2, v, lam):
    B, S, H, Dh = q1.shape
    scale = Dh ** -0.5
    key_idx = jnp.arange(S)

    def one_block(start):
        qs1 = lax.dynamic_slice_in_dim(q1, start, Q_BLOCK, axis=1)
        qs2 = lax.dynamic_slice_in_dim(q2, start, Q_BLOCK, axis=1)
        q_idx = start + jnp.arange(Q_BLOCK)
        mask = (key_idx[None, :] <= q_idx[:, None])[None, None]
        s1 = jnp.einsum('bqhd,bkhd->bhqk', qs1, k1, preferred_element_type=jnp.float32) * scale
        s2 = jnp.einsum('bqhd,bkhd->bhqk', qs2, k2, preferred_element_type=jnp.float32) * scale
        p1 = jax.nn.softmax(jnp.where(mask, s1, -jnp.inf), axis=-1)
        p2 = jax.nn.softmax(jnp.where(mask, s2, -jnp.inf), axis=-1)
        p = (p1 - lam * p2).astype(v.dtype)
        return jnp.einsum('bhqk,bkhd->bqhd', p, v)

    out = lax.map(one_block, jnp.arange(S // Q_BLOCK) * Q_BLOCK)
    return jnp.moveaxis(out, 0, 1).reshape(B, S, H, v.shape[-1])

def dilated_branch(q, k, v, window, dilation):
    B, S, H, D = q.shape
    W = window // dilation
    unit = dilation * W
    Sp = -(-S // unit) * unit
    nc = Sp // unit
    pad = Sp - S

    def to_blocks(t):
        t = jnp.pad(t, ((0, 0), (0, pad), (0, 0), (0, 0)))
        return t.reshape(B, nc, W, dilation, H, D)

    def with_prev(t):
        prev = jnp.pad(t, ((0, 0), (1, 0), (0, 0), (0, 0), (0, 0), (0, 0)))[:, :-1]
        return jnp.concatenate([prev, t], axis=2)

    qb = to_blocks(q)
    kw = with_prev(to_blocks(k))
    vw = with_prev(to_blocks(v))
    s = jnp.einsum('bcirhd,bcjrhd->bcrhij', qb, kw, preferred_element_type=jnp.float32) * (D ** -0.5)
    m_q = jnp.arange(nc)[:, None, None] * W + jnp.arange(W)[None, :, None]
    m_k = jnp.arange(nc)[:, None, None] * W + jnp.arange(2 * W)[None, None, :] - W
    delta = m_q - m_k
    valid = (delta >= 0) & (delta <= W) & (m_k >= 0)
    s = jnp.where(valid[None, :, None, None, :, :], s, -jnp.inf)
    lse = jax.nn.logsumexp(s, axis=-1)
    p = jnp.exp(s - lse[..., None]).astype(v.dtype)
    o = jnp.einsum('bcrhij,bcjrhd->bcirhd', p, vw).reshape(B, Sp, H, D)[:, :S]
    lse = jnp.transpose(lse, (0, 1, 4, 2, 3)).reshape(B, Sp, H)[:, :S]
    return o, lse

def dilated_mixture(q, k, v):
    outs, lses = [], []
    for window, dilation in DILATED_PAIRS:
        o, lse = dilated_branch(q, k, v, window, dilation)
        outs.append(o)
        lses.append(lse)
    w = jax.nn.softmax(jnp.stack(lses, axis=0), axis=0)
    o = jnp.sum(w[..., None] * jnp.stack(outs, axis=0).astype(jnp.float32), axis=0)
    return o.astype(v.dtype)

def moba_attention(q, k, v):
    B, S, H, D = q.shape
    scale = D ** -0.5
    Sp = -(-S // MOBA_BLOCK) * MOBA_BLOCK
    nblk = Sp // MOBA_BLOCK
    n_sel = min(MOBA_TOPK, nblk)
    pad = Sp - S
    kp = jnp.pad(k, ((0, 0), (0, pad), (0, 0), (0, 0)))
    vp = jnp.pad(v, ((0, 0), (0, pad), (0, 0), (0, 0)))
    kbt = kp.reshape(B, nblk, MOBA_BLOCK, H, D).transpose(0, 1, 3, 2, 4)
    vbt = vp.reshape(B, nblk, MOBA_BLOCK, H, D).transpose(0, 1, 3, 2, 4)
    k_mean = jnp.mean(kbt.astype(jnp.float32), axis=3)
    b_idx = jnp.arange(B)[:, None, None, None]
    h_idx = jnp.arange(H)[None, None, :, None]
    blk_ids = jnp.arange(nblk)

    def one_chunk(start):
        qs = lax.dynamic_slice_in_dim(q, start, MOBA_Q_CHUNK, axis=1)
        q_pos = start + jnp.arange(MOBA_Q_CHUNK)
        own = start // MOBA_BLOCK
        gate = jnp.einsum('bqhd,bnhd->bqhn', qs.astype(jnp.float32), k_mean)
        gate = jnp.where(blk_ids < own, gate, -jnp.inf)
        _, sel = lax.top_k(gate, n_sel)
        sel_valid = sel < own
        ks = kbt[b_idx, sel, h_idx]
        vs = vbt[b_idx, sel, h_idx]
        s_sel = jnp.einsum('bqhd,bqhnkd->bqhnk', qs, ks, preferred_element_type=jnp.float32) * scale
        s_sel = jnp.where(sel_valid[..., None], s_sel, -jnp.inf).reshape(B, MOBA_Q_CHUNK, H, n_sel * MOBA_BLOCK)
        k_own = lax.dynamic_slice_in_dim(kp, own * MOBA_BLOCK, MOBA_BLOCK, axis=1)
        v_own = lax.dynamic_slice_in_dim(vp, own * MOBA_BLOCK, MOBA_BLOCK, axis=1)
        own_pos = own * MOBA_BLOCK + jnp.arange(MOBA_BLOCK)
        s_own = jnp.einsum('bqhd,bkhd->bqhk', qs, k_own, preferred_element_type=jnp.float32) * scale
        s_own = jnp.where((own_pos[None, :] <= q_pos[:, None])[None, :, None, :], s_own, -jnp.inf)
        p = jax.nn.softmax(jnp.concatenate([s_sel, s_own], axis=-1), axis=-1).astype(v.dtype)
        p_sel = p[..., :n_sel * MOBA_BLOCK].reshape(B, MOBA_Q_CHUNK, H, n_sel, MOBA_BLOCK)
        p_own = p[..., n_sel * MOBA_BLOCK:]
        return (jnp.einsum('bqhnk,bqhnkd->bqhd', p_sel, vs)
                + jnp.einsum('bqhk,bkhd->bqhd', p_own, v_own))

    out = lax.map(one_chunk, jnp.arange(S // MOBA_Q_CHUNK) * MOBA_Q_CHUNK)
    return jnp.moveaxis(out, 0, 1).reshape(B, S, H, D)

def memory_cross_attention(h, mem_n, w_q, w_kv, w_o, q_gain, k_gain):
    B, S, _ = h.shape
    M = mem_n.shape[1]
    q = rms_norm((h @ w_q).reshape(B, S, N_HEADS_MEM, HEAD_DIM), q_gain)
    kv = (mem_n @ w_kv).reshape(B, M, 2, N_HEADS_MEM, HEAD_DIM)
    k = rms_norm(kv[:, :, 0], k_gain)
    v = kv[:, :, 1]
    s = jnp.einsum('bshd,bmhd->bhsm', q, k, preferred_element_type=jnp.float32) * (HEAD_DIM ** -0.5)
    p = jax.nn.softmax(s, axis=-1).astype(v.dtype)
    o = jnp.einsum('bhsm,bmhd->bshd', p, v).reshape(B, S, MEM_WIDTH)
    return o @ w_o

def swiglu(h, w_gate_up, w_down):
    gu = h @ w_gate_up
    g, u = gu[..., :D_FF], gu[..., D_FF:]
    return (jax.nn.silu(g) * u) @ w_down

def setup_inputs(seed: int = 0) -> dict:
    key = jax.random.key(seed)
    ks = iter(jax.random.split(key, 40))

    def nrm(shape, scale):
        return jax.random.normal(next(ks), shape, dtype=jnp.float32) * scale

    def gain(shape):
        return 1.0 + nrm(shape, 0.02)

    L = DEPTH
    return {
        "x": nrm((BATCH, SEQ, D_MODEL), 1.0),
        "mem": nrm((BATCH, MEM_LEN, D_MODEL), 1.0),
        "positions": jnp.broadcast_to(jnp.arange(SEQ, dtype=jnp.int32)[None, :], (BATCH, SEQ)),
        "norm_mix": gain((L, D_MODEL)),
        "w_in": nrm((L, D_MODEL, 3 * MIX_WIDTH), D_MODEL ** -0.5),
        "qn_diff": gain((L, DIFF_HALF)),
        "kn_diff": gain((L, DIFF_HALF)),
        "lambda_q1": nrm((L, DIFF_HALF), 0.1),
        "lambda_k1": nrm((L, DIFF_HALF), 0.1),
        "lambda_q2": nrm((L, DIFF_HALF), 0.1),
        "lambda_k2": nrm((L, DIFF_HALF), 0.1),
        "subln_diff": gain((L, HEAD_DIM)),
        "qn_dil": gain((L, HEAD_DIM)),
        "kn_dil": gain((L, HEAD_DIM)),
        "qn_moba": gain((L, HEAD_DIM)),
        "kn_moba": gain((L, HEAD_DIM)),
        "w_out": nrm((L, MIX_WIDTH, D_MODEL), MIX_WIDTH ** -0.5),
        "norm_cross": gain((L, D_MODEL)),
        "norm_mem": gain((L, D_MODEL)),
        "w_mq": nrm((L, D_MODEL, MEM_WIDTH), D_MODEL ** -0.5),
        "w_mkv": nrm((L, D_MODEL, 2 * MEM_WIDTH), D_MODEL ** -0.5),
        "qn_mem": gain((L, HEAD_DIM)),
        "kn_mem": gain((L, HEAD_DIM)),
        "w_mo": nrm((L, MEM_WIDTH, D_MODEL), MEM_WIDTH ** -0.5),
        "norm_ffn": gain((L, D_MODEL)),
        "w_gate_up": nrm((L, D_MODEL, 2 * D_FF), D_MODEL ** -0.5),
        "w_down": nrm((L, D_FF, D_MODEL), D_FF ** -0.5),
    }

def reference(x, mem, positions, norm_mix, w_in, qn_diff, kn_diff, lambda_q1, lambda_k1,
              lambda_q2, lambda_k2, subln_diff, qn_dil, kn_dil, qn_moba, kn_moba, w_out,
              norm_cross, norm_mem, w_mq, w_mkv, qn_mem, kn_mem, w_mo, norm_ffn,
              w_gate_up, w_down):
    B, S, _ = x.shape
    a_end = N_HEADS_DIFF
    b_end = N_HEADS_DIFF + N_HEADS_DIL
    rot = HEAD_DIM // ROPE_FRACTION
    for l in range(DEPTH):
        h = rms_norm(x, norm_mix[l])
        qkv = (h @ w_in[l]).reshape(B, S, 3, N_HEADS_MIX, HEAD_DIM)
        q, k, v = qkv[:, :, 0], qkv[:, :, 1], qkv[:, :, 2]

        lam_init = 0.8 - 0.6 * math.exp(-0.3 * l)
        lam = (jnp.exp(jnp.sum(lambda_q1[l].astype(jnp.float32) * lambda_k1[l].astype(jnp.float32)))
               - jnp.exp(jnp.sum(lambda_q2[l].astype(jnp.float32) * lambda_k2[l].astype(jnp.float32)))
               + lam_init)
        qa = diff_qk_prep(q[:, :, :a_end], qn_diff[l], positions)
        ka = diff_qk_prep(k[:, :, :a_end], kn_diff[l], positions)
        o_a = diff_attention(qa[:, :, :, 0], qa[:, :, :, 1], ka[:, :, :, 0], ka[:, :, :, 1],
                             v[:, :, :a_end], lam)
        o_a = rms_norm(o_a, subln_diff[l]) * (1.0 - lam_init)

        qb = rotary(rms_norm(q[:, :, a_end:b_end], qn_dil[l]), positions, rot)
        kb = rotary(rms_norm(k[:, :, a_end:b_end], kn_dil[l]), positions, rot)
        o_b = dilated_mixture(qb, kb, v[:, :, a_end:b_end])

        qc = rotary(rms_norm(q[:, :, b_end:], qn_moba[l]), positions, rot)
        kc = rotary(rms_norm(k[:, :, b_end:], kn_moba[l]), positions, rot)
        o_c = moba_attention(qc, kc, v[:, :, b_end:])

        mix = jnp.concatenate([o_a, o_b.astype(o_a.dtype), o_c.astype(o_a.dtype)], axis=2)
        x = x + mix.reshape(B, S, MIX_WIDTH) @ w_out[l]

        x = x + memory_cross_attention(rms_norm(x, norm_cross[l]), rms_norm(mem, norm_mem[l]),
                                       w_mq[l], w_mkv[l], w_mo[l], qn_mem[l], kn_mem[l])

        x = x + swiglu(rms_norm(x, norm_ffn[l]), w_gate_up[l], w_down[l])
    return x


_drawn_inputs = setup_inputs


def setup_inputs(seed=0):
    import zlib

    import numpy as np

    out = dict(_drawn_inputs(seed))
    spreads = {}
    factors = {'norm_mix': 2.747,
     'qn_diff': 6.413,
     'kn_diff': 6.077,
     'lambda_q1': 8.0,
     'subln_diff': 4.376,
     'qn_dil': 8.0,
     'kn_dil': 8.0,
     'qn_moba': 8.0,
     'kn_moba': 8.0,
     'norm_cross': 8.0,
     'norm_mem': 8.0,
     'qn_mem': 8.0,
     'kn_mem': 8.0,
     'norm_ffn': 2.97}
    for name, (base, spread) in spreads.items():
        noise = np.random.default_rng([zlib.crc32(name.encode()), seed]).standard_normal(out[name].shape)
        drawn = base * np.exp(spread * noise) if base else spread * noise
        out[name] = __import__('jax').numpy.asarray(drawn.astype(out[name].dtype))
    for name, factor in factors.items():
        out[name] = (out[name] * factor).astype(out[name].dtype)
    return out
```

```python
import math
from contextlib import ExitStack

import numpy as np

import concourse.bass as bass
from concourse import mybir

P = 128
F32 = mybir.dt.float32
F32R = mybir.dt.float32r
I32 = mybir.dt.int32
ALU = mybir.AluOpType
ACT = mybir.ActivationFunctionType
AX_X = mybir.AxisListType.X

D = 1024
SEQ = 256
DEPTH = 2
HD = 64
HEADS = 16
DIFF, DIL, MOBA = 4, 6, 6
MEM_HEADS = 4
MEM_W = MEM_HEADS * HD
FF = 2816
EPS = 1e-6
THETA = 500000.0

T = SEQ // P
KC = D // P
HALF = KC // 2
NCHUNK = 3 * D // 512
FCH = FF // P
PAIRS = FCH // 2

RING = 3
U_QKV, U_MKV, U_OUT, U_MQ, U_MO, U_FFN = 0, 12, 14, 18, 20, 21
UNITS = U_FFN + 3 * PAIRS
FILLS = UNITS // RING
assert UNITS % RING == 0 and U_FFN % RING == 0

B_MIX, B_MEM, B_HEADS, B_CROSS, B_FFN = range(5)
BUILDS = 5

SOFTMAXES = [(h, (h % 2) * HD + a * 32, 32) for h in range(DIFF) for a in range(2)]
SOFTMAXES += [(h, (h % 2) * HD, HD) for h in range(DIFF, HEADS)]
NS = len(SOFTMAXES)
LAST_OF = [max(n for n in range(NS) if SOFTMAXES[n][0] == h) for h in range(HEADS)]

NEG = -1.0e30
GROUPS = 2 * DIFF + DIL + MOBA
ROT = ((2 * DIFF, 32, 4, 0, 0), (DIL + MOBA, 64, 8, DIFF * HD, 4))
NFREQ = 12


class Signal:

    def __init__(self, sem, per_layer, before=0):
        self.sem, self.per_layer, self.before = sem, per_layer, before

    def at(self, layer, k):
        return self.before + layer * self.per_layer + k


def trunk(nc, x, mem, positions, w, gains, consts, out):
    with ExitStack() as ctx:
        def sb(name, shape, dt=F32):
            return ctx.enter_context(nc.sbuf_tensor(name, shape, dt))

        def signal(name, per_layer=1, before=0):
            return Signal(ctx.enter_context(nc.semaphore(name)), per_layer, before)

        raw = [sb(f"raw{s}", [P, 2048]) for s in range(RING)]
        whi = [sb(f"whi{s}", [P, 2048], F32R) for s in range(RING)]
        wlo = [sb(f"wlo{s}", [P, 2048], F32R) for s in range(RING)]
        xs = sb("xs", [P, T, D])
        xn = sb("xn", [P, T, D])
        thi = sb("thi", [P, KC, SEQ], F32R)
        tlo = sb("tlo", [P, KC, SEQ], F32R)
        qkv = sb("qkv", [P, T, 3 * D])
        qT = sb("qT", [P, KC, SEQ])
        kT = sb("kT", [P, KC, SEQ])
        sq = sb("sq", [P, T * D])
        prob = [sq[:, 512 * b:512 * b + 512] for b in range(4)]
        probT_all = sb("probT", [P, 3 * 512])
        probT = [probT_all[:, 512 * b:512 * b + 512] for b in range(3)]
        kvm = sb("kvm", [P, T, 2 * MEM_W])
        kmT = sb("kmT", [P, 2, SEQ])
        qm = sb("qm", [P, T, MEM_W])
        qmT = sb("qmT", [P, 2, SEQ])
        om = sb("om", [P, T, MEM_W])
        ahi = [sb(f"ahi{b}", [P, SEQ], F32R) for b in range(2)]
        alo = [sb(f"alo{b}", [P, SEQ], F32R) for b in range(2)]
        silu_g = [qkv[:, 0, 256 * b:256 * b + 256] for b in range(2)]
        act_f = [qkv[:, 0, 512 + 256 * b:768 + 256 * b] for b in range(2)]
        rope = probT_all[:, 0:4 * 192].rearrange("p (i n) -> p i n", i=4)
        g_mix = sb("g_mix", [P, D])
        g_mem, g_cross, g_ffn = sb("g_mem", [P, D]), sb("g_cross", [P, D]), sb("g_ffn", [P, D])
        g_qk = [sb("g_q", [P, D]), sb("g_k", [P, D])]
        g_sub = sb("g_sub", [P, DEPTH, HD])
        g_qm, g_km = sb("g_qm", [P, DEPTH, HD]), sb("g_km", [P, DEPTH, HD])
        ident = sb("ident", [P, P])
        masks = sb("masks", [P, 2, 3 * P])
        freqs = sb("freqs", [P, NFREQ])
        lam_in = sb("lam_in", [P, 4, DEPTH, 32])
        lam_dot = sb("lam_dot", [P, 2, DEPTH])
        lam_exp = sb("lam_exp", [P, 2, DEPTH])
        neg_lam = sb("neg_lam", [P, DEPTH])
        pos_i = sb("pos_i", [P, T], I32)
        pos_f = sb("pos_f", [P, T])
        ang = sb("ang", [P, 2, T, NFREQ])
        turns = sb("turns", [P, 2, T, NFREQ])
        cs = sb("cs", [P, 2, T, NFREQ])
        ss = sb("ss", [P, T])
        mem_r = sb("mem_r", [P, T])
        g32 = sb("g32", [P, T, 32])
        nv, nh, ny, nt = (sb(n, [P, 40]) for n in ("nv", "nh", "ny", "nt"))
        mx = sb("mx", [P, NS, T])
        nm = sb("nm", [P, NS, T])
        zs = sb("zs", [P, NS, T])
        rz = sb("rz", [P, NS, T])

        ps = ctx.enter_context(nc.psum_tensor("ps", [P, 8, 512], F32))

        def banks(a, b):
            return ps[:, a:b, :].rearrange("p b n -> p (b n)")

        s_x = signal("x_loaded")
        s_mem = signal("mem_loaded")
        s_const = signal("consts_loaded")
        s_lam = signal("lambda_ready")
        s_cs = signal("angles_ready")
        s_sin = signal("sines_ready")
        s_memss = signal("mem_squares")
        s_memn = signal("mem_normalised")
        s_out = signal("stored")
        s_gain = signal("gains_loaded", 16 * 5)
        s_gmix = signal("mix_gain_loaded", 16)
        mem_in = signal("mem_in", 16)
        raw_in = [signal(f"raw_in{s}") for s in range(RING)]
        hi_done = [signal(f"hi_done{s}", FILLS) for s in range(RING)]
        lo_done = [signal(f"lo_done{s}", FILLS) for s in range(RING)]
        used = [signal(f"used{s}", FILLS) for s in range(RING)]
        x_new = signal("x_new", 3)
        ss_done = signal("ss_done", 3)
        xn_ready = signal("xn_ready", 2 * (BUILDS - 1))
        xm_ready = signal("xm_ready", 1)
        t_ps = signal("t_ps", 2 * BUILDS)
        t_hi = signal("t_hi", 2 * BUILDS)
        t_lo = signal("t_lo", 2 * BUILDS)
        proj_out = signal("proj_out", NCHUNK)
        mkv_out = signal("mkv_out", 1)
        km_ready = signal("km_ready", 1)
        mq_out = signal("mq_out", 1)
        qm_ready = signal("qm_ready", 1)
        sqr = signal("sqr", 2)
        scaled = signal("scaled", 2)
        roped = signal("roped", 2)
        qkT_ps = signal("qkT_ps", 4)
        qkT_act = signal("qkT_act", 2)
        qkT_dve = signal("qkT_dve", 2)
        scores = signal("scores", NS)
        masked = signal("masked", NS)
        nmax = signal("nmax", NS)
        probs = signal("probs", NS)
        combined = signal("combined", DIFF)
        pT_ps = signal("pT_ps", HEADS)
        pT_act = signal("pT_act", HEADS // 2)
        pT_dve = signal("pT_dve", HEADS // 2)
        pv = signal("pv", HEADS)
        kmT_ps, kmT_out = signal("kmT_ps", 1), signal("kmT_out", 1)
        qmT_ps, qmT_out = signal("qmT_ps", 1), signal("qmT_out", 1)
        m_scores, m_max, m_probs = (signal(n, MEM_HEADS) for n in ("m_scores", "m_max", "m_probs"))
        m_pT_ps, m_pT, m_pv = (signal(n, MEM_HEADS) for n in ("m_pT_ps", "m_pT", "m_pv"))
        om_ready, omT_ps, om_hi, om_lo = (signal(n, 1) for n in ("om_ready", "omT_ps", "om_hi", "om_lo"))
        silu_done = signal("silu_done", FCH)
        glu = signal("glu", FCH)
        act_hi = signal("act_hi", FCH)
        act_lo = signal("act_lo", FCH)
        down_even = signal("down_even", PAIRS)
        dve_chain = signal("dve_chain")
        pool_chain = signal("pool_chain")

        def dmas_before_ffn(s, upto=U_FFN):
            return sum(1 for u in range(upto) if u % RING == s)

        per_layer_dmas = [dmas_before_ffn(s) + PAIRS * (2 if s < 2 else 1) for s in range(RING)]

        def raw_level(layer, u, pair=0):
            s = u % RING
            if u < U_FFN:
                n = dmas_before_ffn(s, u + 1)
            else:
                n = dmas_before_ffn(s) + (pair + 1) * (2 if s < 2 else 1)
            return 16 * (layer * per_layer_dmas[s] + n)

        def fill(u, pair=0):
            return u // RING + pair

        def used_before(layer, u, pair=0):
            return used[u % RING].at(layer, fill(u, pair))

        def used_after(layer, u, pair=0):
            return used[u % RING].at(layer, fill(u, pair) + 1)

        block = ctx.enter_context(nc.Block())

        @block.sync
        def _(sp):
            sp.dma_start(xs[:], x.rearrange("b (t p) d -> p (b t) d", p=P)).then_inc(s_x.sem, 16)

            def load(layer, u, src, pair=0, count=True):
                s = u % RING
                sp.wait_ge(hi_done[s].sem, hi_done[s].at(layer, fill(u, pair)))
                sp.wait_ge(lo_done[s].sem, lo_done[s].at(layer, fill(u, pair)))
                for dst, part in src:
                    sp.dma_start(dst, part).then_inc(raw_in[s].sem, 16)

            def view(u, k):
                return raw[u % RING][:].rearrange("p (k n) -> p k n", k=k)

            for layer in range(DEPTH):
                w_in = w["w_in"][layer].rearrange("(k p) n -> p k n", p=P)
                w_mkv = w["w_mkv"][layer].rearrange("(k p) n -> p k n", p=P)
                w_out = w["w_out"][layer].rearrange("(k p) n -> p k n", p=P)
                w_mq = w["w_mq"][layer].rearrange("(k p) n -> p k n", p=P)
                w_mo = w["w_mo"][layer].rearrange("(k p) n -> p k n", p=P)
                w_gu = w["w_gate_up"][layer].rearrange("(k p) (j n) -> p k j n", p=P, j=2)
                w_down = w["w_down"][layer].rearrange("(k p) n -> p k n", p=P)
                for c in range(NCHUNK):
                    for h in range(2):
                        u = U_QKV + 2 * c + h
                        load(layer, u, [(view(u, 4), w_in[:, 4 * h:4 * h + 4, 512 * c:512 * c + 512])])
                for h in range(2):
                    load(layer, U_MKV + h, [(view(U_MKV + h, 4), w_mkv[:, 4 * h:4 * h + 4, :])])
                for c in range(2):
                    for h in range(2):
                        u = U_OUT + 2 * c + h
                        load(layer, u, [(view(u, 4), w_out[:, 4 * h:4 * h + 4, 512 * c:512 * c + 512])])
                for h in range(2):
                    u = U_MQ + h
                    load(layer, u, [(raw[u % RING][:, 0:1024].rearrange("p (k n) -> p k n", k=4),
                                     w_mq[:, 4 * h:4 * h + 4, :])])
                load(layer, U_MO, [(view(U_MO, 2), w_mo)])
                with sp.Fori(0, PAIRS) as i:
                    for b in range(2):
                        u = U_FFN + b
                        dst = raw[u % RING][:].rearrange("p (k j n) -> p k j n", k=KC, j=2)
                        load(layer, u, [(dst[:, :, j, :], w_gu[:, :, j, bass.ds(i * 256 + b * 128, 128)])
                                        for j in range(2)], i)
                    u = U_FFN + 2
                    load(layer, u, [(view(u, 2), w_down[:, bass.ds(i * 2, 2), :])], i)
            sp.wait_ge(x_new.sem, x_new.at(DEPTH - 1, 3))
            sp.dma_start(out.rearrange("b (t p) d -> p (b t) d", p=P), xs[:]).then_inc(s_out.sem, 16)
            sp.wait_ge(s_out.sem, 16)

        @block.gpsimd
        def _(pool):
            pool.dma_start(g_mix[:], gains["norm_mix"][0:1, :].to_broadcast((P, D))).then_inc(s_gmix.sem, 16)
            pool.dma_start(qkv[:, :, 0:D], mem.rearrange("b (t p) d -> p (b t) d", p=P)).then_inc(s_mem.sem, 16)
            loads = [
                (pos_i[:], positions.rearrange("b (t p) -> p (b t)", p=P)),
                (freqs[:], consts["freqs"].to_broadcast((P, NFREQ))),
                (ident[:], consts["ident"]),
                (masks[:], consts["masks"]),
            ]
            for l in range(DEPTH):
                for tile, name in ((g_sub, "subln_diff"), (g_qm, "qn_mem"), (g_km, "kn_mem")):
                    loads.append((tile[:, l, :], gains[name][l:l + 1, :].to_broadcast((P, HD))))
                for n, name in enumerate(("lambda_q1", "lambda_k1", "lambda_q2", "lambda_k2")):
                    loads.append((lam_in[:, n, l, :], gains[name][l:l + 1, :].to_broadcast((P, 32))))
            assert len(loads) == N_CONST
            for dst, src in loads:
                with nc.allow_non_contiguous_dma(reason="256 positions"):
                    pool.dma_start(dst, src).then_inc(s_const.sem, 16)

            links = [0]

            def link(ins):
                links[0] += 1
                ins.then_inc(pool_chain.sem, 1)
                pool.wait_ge(pool_chain.sem, links[0])

            for layer in range(DEPTH):
                if layer:
                    pool.wait_ge(xn_ready.sem, xn_ready.at(layer - 1, 2 * (BUILDS - 1)))
                for tile, name in ((g_mem, "norm_mem"), (g_qk[0], "q_gain"), (g_qk[1], "k_gain"),
                                   (g_cross, "norm_cross"), (g_ffn, "norm_ffn")):
                    pool.dma_start(tile[:], gains[name][layer:layer + 1, :].to_broadcast((P, D)))\
                        .then_inc(s_gain.sem, 16)
                pool.wait_ge(s_gain.sem, s_gain.at(layer, 16 * 5))
                pool.wait_ge(t_ps.sem, t_ps.at(layer, 2 * B_MIX + 2))
                if layer + 1 < DEPTH:
                    pool.dma_start(g_mix[:], gains["norm_mix"][layer + 1:layer + 2, :].to_broadcast((P, D)))\
                        .then_inc(s_gmix.sem, 16)
                pool.dma_start(xn[:], mem.rearrange("b (t p) d -> p (b t) d", p=P)).then_inc(mem_in.sem, 16)
                pool.wait_ge(mem_in.sem, mem_in.at(layer, 16))
                if layer == 0:
                    pool.wait_ge(s_memn.sem, 1)
                for t in range(T):
                    ins = pool.tensor_scalar(xn[:, t, :], xn[:, t, :], mem_r[:, t:t + 1], None, ALU.mult)
                link(ins)
                pool.tensor_tensor(xn[:], xn[:], g_mem[:].unsqueeze(1).to_broadcast((P, T, D)), ALU.mult)\
                    .then_inc(xm_ready.sem, 1)
                for part in range(2):
                    y = qkv[:, :, part * D:(part + 1) * D]
                    pool.wait_ge(scaled.sem, scaled.at(layer, part + 1))
                    if layer == 0 and part == 0:
                        pool.wait_ge(s_sin.sem, 1)
                    link(pool.tensor_tensor(y, y, g_qk[part][:].unsqueeze(1).to_broadcast((P, T, D)), ALU.mult))
                    todo = []
                    for n, (groups, width, half, col, tab) in enumerate(ROT):
                        v = y[:, :, col:col + groups * width].rearrange("p t (g w) -> p t g w", w=width)
                        x1, x2 = v[:, :, :, 0:half], v[:, :, :, half:2 * half]
                        size = T * groups * half
                        m = [rope[:, i, 0:size].rearrange("p (t g f) -> p t g f", t=T, f=half)
                             for i in range(4)]
                        cos, sin = (cs[:, i, :, tab:tab + half].unsqueeze(2).to_broadcast((P, T, groups, half))
                                    for i in range(2))
                        for i, (a, b) in enumerate(((x1, cos), (x2, sin), (x2, cos), (x1, sin))):
                            ins = pool.tensor_tensor(m[i], a, b, ALU.mult)
                            if i == 3:
                                link(ins)
                        pool.tensor_tensor(x1, m[0], m[1], ALU.subtract)
                        ins = pool.tensor_tensor(x2, m[2], m[3], ALU.add)
                        if n == 0:
                            link(ins)
                        else:
                            ins.then_inc(roped.sem, 1)

        @block.scalar
        def _(act):
            def split_hi(layer, u, pair=0):
                s = u % RING
                act.wait_ge(raw_in[s].sem, raw_level(layer, u, pair))
                act.wait_ge(used[s].sem, used_before(layer, u, pair))
                act.activation(whi[s][:], raw[s][:], ACT.Copy).then_inc(hi_done[s].sem, 1)

            def build_hi(layer, b):
                for h in range(2):
                    act.wait_ge(t_ps.sem, t_ps.at(layer, 2 * b + h + 1))
                    act.activation(thi[:, 4 * h:4 * h + 4, :].rearrange("p k n -> p (k n)"),
                                   banks(2 * h, 2 * h + 2), ACT.Copy).then_inc(t_hi.sem, 1)

            def squares_of_x(layer, n):
                if layer == 0 and n == 0:
                    act.wait_ge(s_x.sem, 16)
                else:
                    act.wait_ge(x_new.sem, x_new.at(layer, n))
                for t in range(T):
                    ins = act.activation(sq[:, t * D:(t + 1) * D], xs[:, t, :], ACT.Square,
                                         accum_out=ss[:, t:t + 1])
                ins.then_inc(ss_done.sem, 1)

            act.wait_ge(s_cs.sem, 1)
            act.activation(cs[:], ang[:], ACT.Sin).then_inc(s_sin.sem, 1)
            act.wait_ge(s_lam.sem, 1)
            act.activation(lam_exp[:], lam_dot[:], ACT.Exp).then_inc(s_lam.sem, 1)
            act.wait_ge(s_mem.sem, 16)
            for t in range(T):
                ins = act.activation(sq[:, t * D:(t + 1) * D], qkv[:, t, 0:D], ACT.Square,
                                     accum_out=ss[:, t:t + 1])
            ins.then_inc(s_memss.sem, 1)
            act.wait_ge(s_memn.sem, 1)
            split_hi(0, 0)
            split_hi(0, 1)

            for layer in range(DEPTH):
                squares_of_x(layer, 0)
                split_hi(layer, 2)
                build_hi(layer, B_MIX)
                for c in range(NCHUNK):
                    split_hi(layer, 2 * c + 3)
                    act.wait_ge(used[(2 * c + 1) % RING].sem, used_after(layer, 2 * c + 1))
                    act.activation(qkv[:, :, 512 * c:512 * c + 512],
                                   ps[:, 4 + 2 * (c % 2):6 + 2 * (c % 2), :], ACT.Copy)\
                        .then_inc(proj_out.sem, 1)
                    split_hi(layer, 2 * c + 4)
                    if c in (1, 3):
                        part = c // 2
                        if part:
                            act.wait_ge(scaled.sem, scaled.at(layer, part))
                        act.wait_ge(proj_out.sem, proj_out.at(layer, c + 1))
                        act.activation(sq[:], qkv[:, :, part * D:(part + 1) * D], ACT.Square)\
                            .then_inc(sqr.sem, 1)
                build_hi(layer, B_MEM)
                act.wait_ge(qkT_ps.sem, qkT_ps.at(layer, 1))
                act.activation(qT[:, 0:4, :], banks(6, 8), ACT.Copy).then_inc(qkT_act.sem, 1)
                split_hi(layer, 15)
                act.wait_ge(used[(U_MKV + 1) % RING].sem, used_after(layer, U_MKV + 1))
                act.activation(kvm[:], ps[:, 4:6, :], ACT.Copy).then_inc(mkv_out.sem, 1)
                split_hi(layer, 16)
                act.wait_ge(qkT_ps.sem, qkT_ps.at(layer, 3))
                act.activation(kT[:, 0:4, :], banks(2, 4), ACT.Copy).then_inc(qkT_act.sem, 1)

                def exps(n):
                    _, _, rows = SOFTMAXES[n]
                    act.wait_ge(nmax.sem, nmax.at(layer, n + 1))
                    for t, (a, b) in enumerate(((0, P), (P, 3 * P))):
                        ins = act.activation(prob[n % 4][:, a:b], prob[n % 4][:, a:b], ACT.Exp,
                                             bias=nm[:, n, t:t + 1], scale=float(rows) ** -0.5,
                                             accum_out=zs[:, n, t:t + 1])
                    ins.then_inc(probs.sem, 1)

                def probT_out(m):
                    act.wait_ge(pT_ps.sem, pT_ps.at(layer, m + 1))
                    if m >= 3:
                        act.wait_ge(pv.sem, pv.at(layer, m - 2))
                    act.activation(probT[m % 3][:, 0:384], ps[:, 2 + m % 2, 0:384], ACT.Copy)\
                        .then_inc(pT_act.sem, 1)

                for n in range(NS + 2):
                    if n < NS:
                        exps(n)
                    for m in range(0, HEADS, 2):
                        if LAST_OF[m] + 2 == n:
                            probT_out(m)
                build_hi(layer, B_HEADS)
                split_hi(layer, 17)
                split_hi(layer, 18)
                split_hi(layer, 19)
                squares_of_x(layer, 1)
                build_hi(layer, B_CROSS)
                split_hi(layer, 20)
                act.wait_ge(kmT_ps.sem, kmT_ps.at(layer, 1))
                act.activation(kmT[:].rearrange("p j n -> p (j n)"), ps[:, 6, :], ACT.Copy)\
                    .then_inc(kmT_out.sem, 1)
                act.wait_ge(used[(U_MQ + 1) % RING].sem, used_after(layer, U_MQ + 1))
                act.activation(qm[:], ps[:, 4:6, 0:MEM_W], ACT.Copy).then_inc(mq_out.sem, 1)
                split_hi(layer, 21)
                split_hi(layer, 22)
                for g in range(MEM_HEADS):
                    act.wait_ge(m_max.sem, m_max.at(layer, g + 1))
                    for t in range(T):
                        ins = act.activation(prob[g][:, 256 * t:256 * t + 256],
                                             ps[:, g % 2, 256 * t:256 * t + 256], ACT.Exp,
                                             bias=nm[:, g, t:t + 1], scale=float(HD) ** -0.5,
                                             accum_out=zs[:, g, t:t + 1])
                    ins.then_inc(m_probs.sem, 1)
                act.wait_ge(omT_ps.sem, omT_ps.at(layer, 1))
                act.activation(thi[:, 0:2, :].rearrange("p k n -> p (k n)"), ps[:, 0, :], ACT.Copy)\
                    .then_inc(om_hi.sem, 1)
                squares_of_x(layer, 2)
                build_hi(layer, B_FFN)

                def silu_step(pair, b):
                    act.wait_ge(used[(U_FFN + b) % RING].sem, used_after(layer, U_FFN + b, pair))
                    if not_first(pair):
                        act.wait_ge(glu.sem, glu.at(layer, pair * 2 + b - 1))
                    act.activation(silu_g[b], ps[:, b, 0:256], ACT.Silu).then_inc(silu_done.sem, 1)

                silu_step(0, 0)
                split_hi(layer, U_FFN + 2, 0)
                split_hi(layer, U_FFN, 1)
                silu_step(0, 1)
                split_hi(layer, U_FFN + 1, 1)
                with act.Fori(1, PAIRS - 1) as i:
                    silu_step(i, 0)
                    split_hi(layer, U_FFN + 2, i)
                    split_hi(layer, U_FFN, i + 1)
                    silu_step(i, 1)
                    split_hi(layer, U_FFN + 1, i + 1)
                silu_step(PAIRS - 1, 0)
                split_hi(layer, U_FFN + 2, PAIRS - 1)
                if layer + 1 < DEPTH:
                    split_hi(layer + 1, 0)
                silu_step(PAIRS - 1, 1)
                if layer + 1 < DEPTH:
                    split_hi(layer + 1, 1)

        @block.vector
        def _(dve):
            links = [0]

            def link(ins):
                links[0] += 1
                ins.then_inc(dve_chain.sem, 1)
                dve.wait_ge(dve_chain.sem, links[0])

            def split_lo(layer, u, pair=0):
                s = u % RING
                dve.wait_ge(hi_done[s].sem, hi_done[s].at(layer, fill(u, pair) + 1))
                dve.tensor_tensor(wlo[s][:], raw[s][:], whi[s][:].bitcast(F32), ALU.subtract)\
                   .then_inc(lo_done[s].sem, 1)

            def rsqrt(n):
                v, h, y, t = (a[:, 0:n] for a in (nv, nh, ny, nt))
                link(dve.tensor_scalar(y.bitcast(I32), v.bitcast(I32), -0.5, 1597463007.0, ALU.mult, ALU.add))
                link(dve.tensor_scalar(h, v, -0.5, None, ALU.mult))
                for _ in range(3):
                    link(dve.tensor_tensor(t, y, h, ALU.mult))
                    link(dve.tensor_tensor(t, t, y, ALU.mult))
                    link(dve.scalar_tensor_tensor(y, t, 1.5, y, ALU.add, ALU.mult))

            def mean_eps(dst, sums, width):
                link(dve.tensor_scalar(dst, sums, 1.0 / width, EPS, ALU.mult, ALU.add))

            def norm_x(layer, n, gain, ready):
                dve.wait_ge(ss_done.sem, ss_done.at(layer, n + 1))
                mean_eps(nv[:, 0:T], ss[:], D)
                rsqrt(T)
                for t in range(T):
                    dve.scalar_tensor_tensor(xn[:, t, :], xs[:, t, :], ny[:, t:t + 1], gain, ALU.mult, ALU.mult)\
                       .then_inc(ready.sem, 1)

            def build_lo(layer, b):
                for h in range(2):
                    dve.wait_ge(t_hi.sem, t_hi.at(layer, 2 * b + h + 1))
                    part = (slice(None), slice(4 * h, 4 * h + 4), slice(None))
                    dve.tensor_tensor(tlo[part].rearrange("p k n -> p (k n)"), banks(2 * h, 2 * h + 2),
                                      thi[part].rearrange("p k n -> p (k n)").bitcast(F32), ALU.subtract)\
                       .then_inc(t_lo.sem, 1)

            def head_norm(y, squares, heads, gain, ready):
                link(dve.tensor_tensor(squares, y, y, ALU.mult))
                link(dve.tensor_reduce(nh[:, 0:T * heads], squares, AX_X, ALU.add))
                mean_eps(nv[:, 0:T * heads], nh[:, 0:T * heads], HD)
                rsqrt(T * heads)
                r = ny[:, 0:T * heads].rearrange("p (t h) -> p t h", t=T).unsqueeze(3).to_broadcast((P, T, heads, HD))
                link(dve.tensor_tensor(y, y, r, ALU.mult))
                return y, gain.unsqueeze(1).unsqueeze(1).to_broadcast((P, T, heads, HD))

            dve.wait_ge(s_const.sem, 16 * N_CONST)
            link(dve.tensor_copy(pos_f[:], pos_i[:]))
            for t in range(T):
                for i in range(2):
                    ins = dve.tensor_scalar(ang[:, i, t, :], freqs[:], pos_f[:, t:t + 1], None, ALU.mult)
            link(ins)
            magic = 12582912.0
            for i, quarter in ((0, 0.25), (1, 0.0)):
                ins = dve.tensor_scalar(turns[:, i], ang[:, i], 1.0 / (2.0 * math.pi), quarter, ALU.mult, ALU.add)
            link(ins)
            link(dve.tensor_scalar(turns[:], turns[:], magic, None, ALU.add))
            link(dve.tensor_scalar(turns[:], turns[:], -magic, None, ALU.add))
            for c in TWO_PI:
                link(dve.scalar_tensor_tensor(ang[:].rearrange("p i t f -> p (i t f)"),
                                              turns[:].rearrange("p i t f -> p (i t f)"), -c,
                                              ang[:].rearrange("p i t f -> p (i t f)"), ALU.mult, ALU.add))
            link(dve.tensor_scalar(ang[:, 0], ang[:, 0], math.pi / 2, None, ALU.add))
            dve.tensor_scalar(ang[:], ang[:], 3.1415925, -3.1415925, ALU.min, ALU.max).then_inc(s_cs.sem, 1)
            for i in range(2):
                for l in range(DEPTH):
                    ins = dve.tensor_tensor_reduce(nt[:, 0:32], lam_in[:, 2 * i, l, :], lam_in[:, 2 * i + 1, l, :],
                                                   1.0, 0.0, ALU.mult, ALU.add, lam_dot[:, i, l:l + 1])
                    link(ins)
            ins = dve.tensor_scalar(g_sub[:, 0, :], g_sub[:, 0, :], 1.0 - lam_init(0), None, ALU.mult)
            for l in range(1, DEPTH):
                ins = dve.tensor_scalar(g_sub[:, l, :], g_sub[:, l, :], 1.0 - lam_init(l), None, ALU.mult)
            ins.then_inc(s_lam.sem, 1)
            dve.wait_ge(s_lam.sem, 2)
            link(dve.tensor_tensor(neg_lam[:], lam_exp[:, 1, :], lam_exp[:, 0, :], ALU.subtract))
            for l in range(DEPTH):
                ins = dve.tensor_scalar(neg_lam[:, l:l + 1], neg_lam[:, l:l + 1], -lam_init(l), None, ALU.add)
            link(ins)
            dve.wait_ge(s_memss.sem, 1)
            mean_eps(nv[:, 0:T], ss[:], D)
            rsqrt(T)
            dve.tensor_copy(mem_r[:], ny[:, 0:T]).then_inc(s_memn.sem, 1)
            split_lo(0, 0)
            split_lo(0, 1)

            for layer in range(DEPTH):
                dve.wait_ge(s_gmix.sem, s_gmix.at(layer, 16))
                norm_x(layer, 0, g_mix[:], xn_ready)
                split_lo(layer, 2)
                build_lo(layer, B_MIX)

                def scale_qk(part):
                    y = qkv[:, :, part * D:(part + 1) * D]
                    dve.wait_ge(sqr.sem, sqr.at(layer, part + 1))
                    link(dve.tensor_reduce(g32[:], sq[:].rearrange("p (t g w) -> p t g w", t=T, w=32), AX_X, ALU.add))
                    v = nv[:, 0:T * GROUPS].rearrange("p (t g) -> p t g", t=T)
                    dve.tensor_scalar(v[:, :, 0:8], g32[:, :, 0:8], 1.0 / 32, EPS, ALU.mult, ALU.add)
                    two = g32[:, :, 8:32].rearrange("p t (g w) -> p t g w", w=2)
                    link(dve.tensor_tensor(v[:, :, 8:20], two[:, :, :, 0], two[:, :, :, 1], ALU.add))
                    mean_eps(v[:, :, 8:20], v[:, :, 8:20], HD)
                    rsqrt(T * GROUPS)
                    r = ny[:, 0:T * GROUPS].rearrange("p (t g) -> p t g", t=T)
                    for n, (groups, width, _, col, _) in enumerate(ROT):
                        z = y[:, :, col:col + groups * width].rearrange("p t (g w) -> p t g w", w=width)
                        rg = r[:, :, 8 * n:8 * n + groups].unsqueeze(3).to_broadcast((P, T, groups, width))
                        ins = dve.tensor_tensor(z, z, rg, ALU.mult)
                    ins.then_inc(scaled.sem, 1)

                for c in range(NCHUNK):
                    split_lo(layer, 2 * c + 3)
                    split_lo(layer, 2 * c + 4)
                    if c in (2, 4):
                        scale_qk(c // 2 - 1)
                build_lo(layer, B_MEM)
                dve.wait_ge(qkT_ps.sem, qkT_ps.at(layer, 2))
                dve.tensor_copy(qT[:, 4:8, :].rearrange("p k n -> p (k n)"), banks(0, 2)).then_inc(qkT_dve.sem, 1)
                split_lo(layer, 15)
                dve.wait_ge(mkv_out.sem, mkv_out.at(layer, 1))
                km = kvm[:, :, 0:MEM_W].rearrange("p t (h d) -> p t h d", d=HD)
                y, gain = head_norm(km, sq[:, 0:T * MEM_W].rearrange("p (t h d) -> p t h d", t=T, d=HD),
                                    MEM_HEADS, g_km[:, layer, :], None)
                dve.tensor_tensor(y, y, gain, ALU.mult).then_inc(km_ready.sem, 1)
                split_lo(layer, 16)
                dve.wait_ge(qkT_ps.sem, qkT_ps.at(layer, 4))
                dve.tensor_copy(kT[:, 4:8, :].rearrange("p k n -> p (k n)"), banks(6, 8)).then_inc(qkT_dve.sem, 1)

                def mask_max(n):
                    head, _, rows = SOFTMAXES[n]
                    kind = 1 if DIFF <= head < DIFF + DIL else 0
                    dve.wait_ge(scores.sem, scores.at(layer, n + 1))
                    if n >= 4:
                        dve.wait_ge(pT_ps.sem, pT_ps.at(layer, SOFTMAXES[n - 4][0] + 1))
                    for t, (a, b) in enumerate(((0, P), (P, 3 * P))):
                        ins = dve.tensor_tensor_reduce(prob[n % 4][:, a:b], ps[:, n % 2, a:b], masks[:, kind, a:b],
                                                       1.0, 3.0 * NEG, ALU.add, ALU.max, mx[:, n, t:t + 1])
                    ins.then_inc(masked.sem, 1)
                    dve.wait_ge(masked.sem, masked.at(layer, n + 1))
                    dve.tensor_scalar(nm[:, n, :], mx[:, n, :], -float(rows) ** -0.5, None, ALU.mult)\
                       .then_inc(nmax.sem, 1)

                def combine(h):
                    n = 2 * h
                    dve.wait_ge(probs.sem, probs.at(layer, n + 2))
                    link(dve.reciprocal(rz[:, n:n + 2, :], zs[:, n:n + 2, :]))
                    link(dve.tensor_scalar(rz[:, n + 1, :], rz[:, n + 1, :], neg_lam[:, layer:layer + 1], None, ALU.mult))
                    p1, p2 = prob[n % 4], prob[(n + 1) % 4]
                    for t, (a, b) in enumerate(((0, P), (P, 3 * P))):
                        ins = dve.tensor_scalar(p1[:, a:b], p1[:, a:b], rz[:, n, t:t + 1], None, ALU.mult)
                    link(ins)
                    for t, (a, b) in enumerate(((0, P), (P, 3 * P))):
                        ins = dve.scalar_tensor_tensor(p1[:, a:b], p2[:, a:b], rz[:, n + 1, t:t + 1], p1[:, a:b],
                                                       ALU.mult, ALU.add)
                    ins.then_inc(combined.sem, 1)

                def probT_out(m):
                    dve.wait_ge(pT_ps.sem, pT_ps.at(layer, m + 1))
                    if m >= 3:
                        dve.wait_ge(pv.sem, pv.at(layer, m - 2))
                    dve.tensor_copy(probT[m % 3][:, 0:384], ps[:, 2 + m % 2, 0:384]).then_inc(pT_dve.sem, 1)

                def by_head(a, heads):
                    return a.rearrange("p t (h d) -> p t h d", h=heads)

                def heads_out(first, heads, half):
                    n = first + DIFF
                    link(dve.reciprocal(rz[:, n:n + heads, :], zs[:, n:n + heads, :]))
                    col = (first % 8) * HD
                    o = by_head(ps[:, 4 + 2 * half:6 + 2 * half, col:col + heads * HD], heads)
                    r = rz[:, n:n + heads, :].rearrange("p h t -> p t h").unsqueeze(3).to_broadcast((P, T, heads, HD))
                    return dve.tensor_tensor(by_head(xn[:, :, first * HD:(first + heads) * HD], heads), o, r, ALU.mult)

                def first_heads_out():
                    dve.wait_ge(pv.sem, pv.at(layer, 8))
                    dve.wait_ge(probs.sem, probs.at(layer, 8 + DIFF))
                    heads_out(DIFF, 8 - DIFF, 0)
                    o = by_head(xn[:, :, 0:DIFF * HD], DIFF)
                    link(dve.tensor_copy(o, by_head(ps[:, 4:6, 0:DIFF * HD], DIFF)))
                    y, gain = head_norm(o, om[:].rearrange("p t (h d) -> p t h d", d=HD), DIFF, g_sub[:, layer, :], None)
                    dve.tensor_tensor(y, y, gain, ALU.mult).then_inc(xn_ready.sem, 1)

                for n in range(NS + 3):
                    if n < NS:
                        mask_max(n)
                    for h in range(HEADS):
                        if h < DIFF and LAST_OF[h] + 1 == n:
                            combine(h)
                        if h % 2 and LAST_OF[h] + 2 == n:
                            probT_out(h)
                    if n == 8 + DIFF + 3:
                        first_heads_out()
                dve.wait_ge(pv.sem, pv.at(layer, HEADS))
                heads_out(8, 8, 1).then_inc(xn_ready.sem, 1)

                build_lo(layer, B_HEADS)
                split_lo(layer, 17)
                split_lo(layer, 18)

                def add_to_x(units):
                    for c in range(2):
                        dve.wait_ge(used[units[c][0] % RING].sem, used_after(layer, *units[c]))
                        ins = dve.tensor_tensor(xs[:, :, 512 * c:512 * c + 512], ps[:, 4 + 2 * c:6 + 2 * c, :],
                                                xs[:, :, 512 * c:512 * c + 512], ALU.add)
                    ins.then_inc(x_new.sem, 1)
                    return ins

                add_to_x([(U_OUT + 1,), (U_OUT + 3,)])
                split_lo(layer, 19)
                dve.wait_ge(s_gain.sem, s_gain.at(layer, 16 * 5))
                norm_x(layer, 1, g_cross[:], xn_ready)
                build_lo(layer, B_CROSS)
                split_lo(layer, 20)
                dve.wait_ge(mq_out.sem, mq_out.at(layer, 1))
                y, gain = head_norm(qm[:].rearrange("p t (h d) -> p t h d", d=HD),
                                    om[:].rearrange("p t (h d) -> p t h d", d=HD), MEM_HEADS, g_qm[:, layer, :], None)
                dve.tensor_tensor(y, y, gain, ALU.mult).then_inc(qm_ready.sem, 1)
                dve.wait_ge(qmT_ps.sem, qmT_ps.at(layer, 1))
                dve.tensor_copy(qmT[:].rearrange("p j n -> p (j n)"), ps[:, 7, :]).then_inc(qmT_out.sem, 1)
                split_lo(layer, 21)
                split_lo(layer, 22)

                def mem_probT(g):
                    dve.wait_ge(m_pT_ps.sem, m_pT_ps.at(layer, g + 1))
                    if g >= 3:
                        dve.wait_ge(m_pv.sem, m_pv.at(layer, g - 2))
                    dve.tensor_copy(probT[g % 3], ps[:, 2 + g % 2, :]).then_inc(m_pT.sem, 1)

                for g in range(MEM_HEADS):
                    dve.wait_ge(m_scores.sem, m_scores.at(layer, g + 1))
                    link(dve.tensor_reduce(mx[:, g, :], ps[:, g % 2, :].rearrange("p (t n) -> p t n", t=T), AX_X, ALU.max))
                    dve.tensor_scalar(nm[:, g, :], mx[:, g, :], -float(HD) ** -0.5, None, ALU.mult)\
                       .then_inc(m_max.sem, 1)
                    if g >= 2:
                        mem_probT(g - 2)
                for g in range(MEM_HEADS - 2, MEM_HEADS):
                    mem_probT(g)
                link(dve.reciprocal(rz[:, 0:MEM_HEADS, :], zs[:, 0:MEM_HEADS, :]))
                dve.wait_ge(m_pv.sem, m_pv.at(layer, MEM_HEADS))
                r = rz[:, 0:MEM_HEADS, :].rearrange("p h t -> p t h").unsqueeze(3).to_broadcast((P, T, MEM_HEADS, HD))
                dve.tensor_tensor(by_head(om[:], MEM_HEADS),
                                  ps[:, 4, :].rearrange("p (t h d) -> p t h d", t=T, d=HD), r, ALU.mult)\
                   .then_inc(om_ready.sem, 1)
                dve.wait_ge(om_hi.sem, om_hi.at(layer, 1))
                dve.tensor_tensor(tlo[:, 0:2, :].rearrange("p k n -> p (k n)"), ps[:, 0, :],
                                  thi[:, 0:2, :].rearrange("p k n -> p (k n)").bitcast(F32), ALU.subtract)\
                   .then_inc(om_lo.sem, 1)
                add_to_x([(U_MO,)] * 2)

                norm_x(layer, 2, g_ffn[:], xn_ready)
                build_lo(layer, B_FFN)

                def glu_step(pair, b):
                    f = pair * 2 + b
                    dve.wait_ge(silu_done.sem, silu_done.at(layer, f + 1))
                    dve.tensor_tensor(act_f[b], ps[:, b, 256:512], silu_g[b], ALU.mult).then_inc(glu.sem, 1)
                    dve.wait_ge(glu.sem, glu.at(layer, f + 1))
                    if not_first(pair):
                        if b == 0:
                            dve.wait_ge(down_even.sem, down_even.at(layer, pair))
                        else:
                            dve.wait_ge(used[(U_FFN + 2) % RING].sem, used_after(layer, U_FFN + 2, pair - 1))
                    dve.tensor_copy(ahi[b][:], act_f[b]).then_inc(act_hi.sem, 1)
                    dve.wait_ge(act_hi.sem, act_hi.at(layer, f + 1))
                    dve.tensor_tensor(alo[b][:], act_f[b], ahi[b][:].bitcast(F32), ALU.subtract)\
                       .then_inc(act_lo.sem, 1)

                glu_step(0, 0)
                split_lo(layer, U_FFN + 2, 0)
                split_lo(layer, U_FFN, 1)
                glu_step(0, 1)
                split_lo(layer, U_FFN + 1, 1)
                with dve.Fori(1, PAIRS - 1) as i:
                    glu_step(i, 0)
                    split_lo(layer, U_FFN + 2, i)
                    split_lo(layer, U_FFN, i + 1)
                    glu_step(i, 1)
                    split_lo(layer, U_FFN + 1, i + 1)
                glu_step(PAIRS - 1, 0)
                split_lo(layer, U_FFN + 2, PAIRS - 1)
                if layer + 1 < DEPTH:
                    split_lo(layer + 1, 0)
                glu_step(PAIRS - 1, 1)
                if layer + 1 < DEPTH:
                    split_lo(layer + 1, 1)
                add_to_x([(U_FFN + 2, PAIRS - 1)] * 2)

        @block.tensor
        def _(pe):
            def three(acc, x_hi, x_lo, w_hi, w_lo, start, stop):
                pe.matmul(acc, x_hi, w_hi, start=start, stop=False)
                pe.matmul(acc, x_hi, w_lo, start=False, stop=False)
                return pe.matmul(acc, x_lo, w_hi, start=False, stop=stop)

            def build(layer, b, src):
                for h in range(2):
                    for k in range(4 * h, 4 * h + 4):
                        for t in range(T):
                            col = (k % 2) * SEQ + t * P
                            ins = pe.transpose(ps[:, k // 2, col:col + P], src[:, t, k * P:(k + 1) * P], ident[:])
                    ins.then_inc(t_ps.sem, 1)
                    if b == B_HEADS and h == 0:
                        pe.wait_ge(xn_ready.sem, xn_ready.at(layer, 4))

            def token_major(layer, u0, units, chunks, cols, bank_of):
                for i in range(units):
                    u = u0 + i
                    pe.wait_ge(lo_done[u % RING].sem, lo_done[u % RING].at(layer, fill(u) + 1))
                    s = u % RING
                    for kk in range(chunks):
                        k = chunks * i + kk
                        for t in range(T):
                            for c in range(max(1, cols // 512)):
                                n = min(cols, 512)
                                a = kk * cols + c * 512
                                ins = three(ps[:, bank_of(t, c), 0:n], thi[:, k, t * P:(t + 1) * P],
                                            tlo[:, k, t * P:(t + 1) * P], whi[s][:, a:a + n], wlo[s][:, a:a + n],
                                            k == 0, i == units - 1 and kk == chunks - 1)
                    ins.then_inc(used[s].sem, 1)

            pe.wait_ge(s_const.sem, 16 * N_CONST)
            for layer in range(DEPTH):
                pe.wait_ge(xn_ready.sem, xn_ready.at(layer, 2))
                build(layer, B_MIX, xn)
                pe.wait_ge(t_lo.sem, t_lo.at(layer, 2 * B_MIX + 2))
                for c in range(NCHUNK):
                    if c >= 2:
                        pe.wait_ge(proj_out.sem, proj_out.at(layer, c - 1))
                    elif layer and c == 0:
                        pe.wait_ge(x_new.sem, x_new.at(layer - 1, 3))
                    token_major(layer, U_QKV + 2 * c, 2, 4, 512, lambda t, _: 4 + 2 * (c % 2) + t)
                pe.wait_ge(xm_ready.sem, xm_ready.at(layer, 1))
                build(layer, B_MEM, xn)

                def transpose_qk(part, half, bank):
                    for j in range(4 * half, 4 * half + 4):
                        for t in range(T):
                            a = (j % 4) * SEQ + t * P
                            ins = pe.transpose(ps[:, bank + a // 512, a % 512:a % 512 + P],
                                               qkv[:, t, part * D + j * P:part * D + (j + 1) * P], ident[:])
                    ins.then_inc(qkT_ps.sem, 1)

                pe.wait_ge(roped.sem, roped.at(layer, 1))
                pe.wait_ge(proj_out.sem, proj_out.at(layer, NCHUNK))
                transpose_qk(0, 0, 6)
                pe.wait_ge(t_lo.sem, t_lo.at(layer, 2 * B_MEM + 1))
                transpose_qk(0, 1, 0)
                pe.wait_ge(t_lo.sem, t_lo.at(layer, 2 * B_MEM + 2))
                token_major(layer, U_MKV, 2, 4, 512, lambda t, _: 4 + t)
                pe.wait_ge(roped.sem, roped.at(layer, 2))
                transpose_qk(1, 0, 2)
                pe.wait_ge(qkT_act.sem, qkT_act.at(layer, 1))
                transpose_qk(1, 1, 6)

                def score(n):
                    h, base, rows = SOFTMAXES[n]
                    if n >= 2:
                        pe.wait_ge(masked.sem, masked.at(layer, n - 1))
                    j = h // 2
                    q, k = qT[base:base + rows, j, :], kT[base:base + rows, j, :]
                    pe.matmul(ps[:, n % 2, 0:P], q[:, 0:P], k[:, 0:P], start=True, stop=True)
                    pe.matmul(ps[:, n % 2, P:3 * P], q[:, P:2 * P], k, start=True, stop=True)\
                      .then_inc(scores.sem, 1)

                def transpose_p(m):
                    n = 2 * m if m < DIFF else m + DIFF
                    if m < DIFF:
                        pe.wait_ge(combined.sem, combined.at(layer, m + 1))
                    else:
                        pe.wait_ge(probs.sem, probs.at(layer, n + 1))
                    if m >= 2:
                        pe.wait_ge((pT_act, pT_dve)[m % 2].sem, (pT_act, pT_dve)[m % 2].at(layer, m // 2))
                    for b in range(3):
                        ins = pe.transpose(ps[:, 2 + m % 2, b * P:(b + 1) * P], prob[n % 4][:, b * P:(b + 1) * P], ident[:])
                    ins.then_inc(pT_ps.sem, 1)

                def weigh_v(m):
                    pe.wait_ge((pT_act, pT_dve)[m % 2].sem, (pT_act, pT_dve)[m % 2].at(layer, m // 2 + 1))
                    p = probT[m % 3]
                    a, bank = (m % 8) * HD, 4 + 2 * (m // 8)
                    v = qkv[:, :, 2 * D + m * HD:2 * D + (m + 1) * HD]
                    pe.matmul(ps[:, bank, a:a + HD], p[:, 0:P], v[:, 0, :], start=True, stop=True)
                    pe.matmul(ps[:, bank + 1, a:a + HD], p[:, P:2 * P], v[:, 0, :], start=True, stop=False)
                    pe.matmul(ps[:, bank + 1, a:a + HD], p[:, 2 * P:3 * P], v[:, 1, :], start=False, stop=True)\
                      .then_inc(pv.sem, 1)

                pe.wait_ge(qkT_act.sem, qkT_act.at(layer, 2))
                pe.wait_ge(qkT_dve.sem, qkT_dve.at(layer, 2))
                pe.wait_ge(mkv_out.sem, mkv_out.at(layer, 1))
                for n in range(NS + 4):
                    if n < NS:
                        score(n)
                    for m in range(HEADS):
                        if LAST_OF[m] + 2 == n:
                            transpose_p(m)
                        if LAST_OF[m] + 3 == n:
                            weigh_v(m)

                pe.wait_ge(xn_ready.sem, xn_ready.at(layer, 3))
                pe.wait_ge(masked.sem, masked.at(layer, NS))
                pe.wait_ge(pT_dve.sem, pT_dve.at(layer, HEADS // 2))
                build(layer, B_HEADS, xn)
                pe.wait_ge(t_lo.sem, t_lo.at(layer, 2 * B_HEADS + 2))
                for c in range(2):
                    token_major(layer, U_OUT + 2 * c, 2, 4, 512, lambda t, _: 4 + 2 * c + t)

                pe.wait_ge(xn_ready.sem, xn_ready.at(layer, 6))
                build(layer, B_CROSS, xn)

                def transpose_small(src, bank, sig):
                    for j in range(2):
                        for t in range(T):
                            a = j * SEQ + t * P
                            ins = pe.transpose(ps[:, bank, a:a + P], src[:, t, j * P:(j + 1) * P], ident[:])
                    ins.then_inc(sig.sem, 1)

                pe.wait_ge(km_ready.sem, km_ready.at(layer, 1))
                transpose_small(kvm, 6, kmT_ps)
                pe.wait_ge(t_lo.sem, t_lo.at(layer, 2 * B_CROSS + 2))
                token_major(layer, U_MQ, 2, 4, MEM_W, lambda t, _: 4 + t)
                pe.wait_ge(qm_ready.sem, qm_ready.at(layer, 1))
                transpose_small(qm, 7, qmT_ps)
                pe.wait_ge(kmT_out.sem, kmT_out.at(layer, 1))
                pe.wait_ge(qmT_out.sem, qmT_out.at(layer, 1))

                def mem_score(g):
                    base, j = (g % 2) * HD, g // 2
                    if g >= 2:
                        pe.wait_ge(m_probs.sem, m_probs.at(layer, g - 1))
                    for t in range(T):
                        ins = pe.matmul(ps[:, g % 2, 256 * t:256 * t + 256], qmT[base:base + HD, j, t * P:(t + 1) * P],
                                        kmT[base:base + HD, j, :], start=True, stop=True)
                    ins.then_inc(m_scores.sem, 1)

                def mem_transpose_p(g):
                    pe.wait_ge(m_probs.sem, m_probs.at(layer, g + 1))
                    if g >= 2:
                        pe.wait_ge(m_pT.sem, m_pT.at(layer, g - 1))
                    for t in range(T):
                        for k in range(T):
                            a = k * SEQ + t * P
                            ins = pe.transpose(ps[:, 2 + g % 2, a:a + P],
                                               prob[g][:, 256 * t + k * P:256 * t + (k + 1) * P], ident[:])
                    ins.then_inc(m_pT_ps.sem, 1)

                def mem_weigh_v(g):
                    pe.wait_ge(m_pT.sem, m_pT.at(layer, g + 1))
                    for t in range(T):
                        for k in range(T):
                            ins = pe.matmul(ps[:, 4, t * 256 + g * HD:t * 256 + (g + 1) * HD],
                                            probT[g % 3][:, k * SEQ + t * P:k * SEQ + (t + 1) * P],
                                            kvm[:, k, MEM_W + g * HD:MEM_W + (g + 1) * HD],
                                            start=(k == 0), stop=(k == T - 1))
                    ins.then_inc(m_pv.sem, 1)

                for g in range(MEM_HEADS + 2):
                    if g < MEM_HEADS:
                        mem_score(g)
                    if 1 <= g <= MEM_HEADS:
                        mem_transpose_p(g - 1)
                    if g >= 2:
                        mem_weigh_v(g - 2)
                pe.wait_ge(om_ready.sem, om_ready.at(layer, 1))
                transpose_small(om, 0, omT_ps)
                pe.wait_ge(om_lo.sem, om_lo.at(layer, 1))
                token_major(layer, U_MO, 1, 2, D, lambda t, c: 4 + 2 * c + t)

                pe.wait_ge(xn_ready.sem, xn_ready.at(layer, 8))
                build(layer, B_FFN, xn)
                pe.wait_ge(t_lo.sem, t_lo.at(layer, 2 * B_FFN + 2))

                def gate_up(pair, b):
                    s = (U_FFN + b) % RING
                    pe.wait_ge(lo_done[(U_FFN + b) % RING].sem, lo_done[(U_FFN + b) % RING].at(layer, fill(U_FFN + b, pair) + 1))
                    if not_first(pair):
                        pe.wait_ge(glu.sem, glu.at(layer, pair * 2 + b - 1))
                    for j in range(2):
                        acc = ps[:, b, 256 * j:256 * j + 256]
                        for k in range(KC):
                            a = (2 * k + j) * P
                            pe.matmul(acc, whi[s][:, a:a + P], thi[:, k, :], start=(k == 0), stop=False)
                            pe.matmul(acc, whi[s][:, a:a + P], tlo[:, k, :], start=False, stop=False)
                            ins = pe.matmul(acc, wlo[s][:, a:a + P], thi[:, k, :], start=False, stop=(k == KC - 1))
                    ins.then_inc(used[s].sem, 1)

                def down(pair, b, first=False, last=False):
                    s = (U_FFN + 2) % RING
                    if b == 0:
                        pe.wait_ge(lo_done[(U_FFN + 2) % RING].sem, lo_done[(U_FFN + 2) % RING].at(layer, fill(U_FFN + 2, pair) + 1))
                    pe.wait_ge(act_lo.sem, act_lo.at(layer, pair * 2 + b + 1))
                    for t in range(T):
                        for c in range(2):
                            a = b * D + c * 512
                            ins = three(ps[:, 4 + 2 * c + t, :], ahi[b][:, t * P:(t + 1) * P],
                                        alo[b][:, t * P:(t + 1) * P], whi[s][:, a:a + 512], wlo[s][:, a:a + 512],
                                        first, last)
                    ins.then_inc((down_even.sem, used[s].sem)[b], 1)

                gate_up(0, 0)
                gate_up(0, 1)
                down(0, 0, first=True)
                with pe.Fori(1, PAIRS) as i:
                    gate_up(i, 0)
                    down(i - 1, 1)
                    gate_up(i, 1)
                    down(i, 0)
                down(PAIRS - 1, 1, last=True)


N_CONST = 4 + DEPTH * (3 + 4)


def not_first(pair):
    return not isinstance(pair, int) or pair > 0


def lam_init(layer):
    return 0.8 - 0.6 * math.exp(-0.3 * layer)


def split_two_pi():
    parts, left = [], 2.0 * math.pi
    for bits in (5, 13, 21):
        c = math.floor(left * 2.0 ** bits) / 2.0 ** bits
        parts.append(c)
        left -= c
    return parts + [left]


TWO_PI = split_two_pi()


def mask_table():
    q = np.arange(SEQ)[:, None]
    k = np.arange(SEQ)[None, :]
    d = q - k
    count = [(d >= 0).astype(np.float64),
             (((d >= 0) & (d <= 128)).astype(np.float64) + ((d >= 0) & (d % 4 == 0)) + ((d >= 0) & (d % 16 == 0)))]
    table = np.full((P, 2, 3 * P), NEG, np.float32)
    for kind, c in enumerate(count):
        m = np.where(c > 0, np.log(np.maximum(c, 1.0)) * math.sqrt(HD), NEG).astype(np.float32)
        table[:, kind, 0:P] = m[0:P, 0:P]
        table[:, kind, P:3 * P] = m[P:2 * P, :]
    return table


def freq_table():
    parts = [THETA ** (-np.arange(half, dtype=np.float32) / np.float32(half)) for half in (4, 8)]
    return np.concatenate(parts).astype(np.float32)[None, :]


WEIGHTS = ("w_in", "w_out", "w_mq", "w_mkv", "w_mo", "w_gate_up", "w_down")
GAINS = ("norm_mix", "norm_cross", "norm_mem", "norm_ffn", "subln_diff", "qn_mem", "kn_mem",
         "lambda_q1", "lambda_k1", "lambda_q2", "lambda_k2")


def kernel(**inputs):
    import concourse.bacc as bacc
    from concourse.bass_utils import run_bass_kernel_spmd

    nc = bacc.Bacc("TRN2", target_bir_lowering=False, num_devices=1)
    arrays = {}

    def put(name, a):
        a = np.ascontiguousarray(a)
        arrays[f"in_{name}"] = a
        return nc.dram_tensor(f"in_{name}", a.shape, mybir.dt.from_np(a.dtype), kind="ExternalInput").ap()

    def tiled(kind):
        parts = [np.tile(np.asarray(inputs[f"{kind}_{n}"]), (1, reps))
                 for n, reps in (("diff", 2 * DIFF), ("dil", DIL), ("moba", MOBA))]
        return np.concatenate(parts, axis=1)

    x = put("x", inputs["x"])
    mem = put("mem", inputs["mem"])
    positions = put("positions", inputs["positions"])
    w = {n: put(n, inputs[n]) for n in WEIGHTS}
    gains = {n: put(n, inputs[n]) for n in GAINS}
    gains["q_gain"] = put("q_gain", tiled("qn"))
    gains["k_gain"] = put("k_gain", tiled("kn"))
    consts = {"ident": put("ident", np.eye(P, dtype=np.float32)), "masks": put("masks", mask_table()),
              "freqs": put("freqs", freq_table())}
    out = nc.dram_tensor("out", (1, SEQ, D), F32, kind="ExternalOutput").ap()
    trunk(nc, x, mem, positions, w, gains, consts, out)
    r = run_bass_kernel_spmd(nc, [arrays], core_ids=[0])
    return r.results[0]["out"]
```

```python
import math
from contextlib import ExitStack

import numpy as np

import concourse.bass as bass
from concourse import mybir

P = 128
F32 = mybir.dt.float32
F32R = mybir.dt.float32r
I32 = mybir.dt.int32
ALU = mybir.AluOpType
ACT = mybir.ActivationFunctionType
AX_X = mybir.AxisListType.X

D = 1024
SEQ = 256
DEPTH = 2
HD = 64
HEADS = 16
DIFF, DIL, MOBA = 4, 6, 6
MEM_HEADS = 4
MEM_W = MEM_HEADS * HD
FF = 2816
EPS = 1e-6
THETA = 500000.0

T = SEQ // P
KC = D // P
HALF = KC // 2
NCHUNK = 3 * D // 512
FCH = FF // P
PAIRS = FCH // 2

RING = 3
U_QKV, U_MKV, U_OUT, U_MQ, U_MO, U_FFN = 0, 12, 14, 18, 20, 21
UNITS = U_FFN + 3 * PAIRS
FILLS = UNITS // RING
assert UNITS % RING == 0 and U_FFN % RING == 0

B_MIX, B_MEM, B_HEADS, B_CROSS, B_FFN = range(5)
BUILDS = 5

SOFTMAXES = [(h, (h % 2) * HD + a * 32, 32) for h in range(DIFF) for a in range(2)]
SOFTMAXES += [(h, (h % 2) * HD, HD) for h in range(DIFF, HEADS)]
NS = len(SOFTMAXES)
LAST_OF = [max(n for n in range(NS) if SOFTMAXES[n][0] == h) for h in range(HEADS)]

NEG = -1.0e30
GROUPS = 2 * DIFF + DIL + MOBA
ROT = ((2 * DIFF, 32, 4, 0, 0), (DIL + MOBA, 64, 8, DIFF * HD, 4))
NFREQ = 12


class Signal:

    def __init__(self, sem, per_layer):
        self.sem, self.per_layer = sem, per_layer

    def at(self, layer, k):
        return layer * self.per_layer + k


def trunk(nc, x, mem, positions, w, gains, consts, out):
    with ExitStack() as ctx:
        def sb(name, shape, dt=F32):
            return ctx.enter_context(nc.sbuf_tensor(name, shape, dt))

        def signal(name, per_layer=1):
            return Signal(ctx.enter_context(nc.semaphore(name)), per_layer)

        raw = [sb(f"raw{s}", [P, 2048]) for s in range(RING)]
        whi = [sb(f"whi{s}", [P, 2048], F32R) for s in range(RING)]
        wlo = [sb(f"wlo{s}", [P, 2048], F32R) for s in range(RING)]
        xs = sb("xs", [P, T, D])
        xn = sb("xn", [P, T, D])
        thi = sb("thi", [P, KC, SEQ], F32R)
        tlo = sb("tlo", [P, KC, SEQ], F32R)
        qkv = sb("qkv", [P, T, 3 * D])
        qT = sb("qT", [P, KC, SEQ])
        kT = sb("kT", [P, KC, SEQ])
        sq = sb("sq", [P, T * D])
        prob = [sq[:, 512 * b:512 * b + 512] for b in range(4)]
        probT_all = sb("probT", [P, 3 * 512])
        probT = [probT_all[:, 512 * b:512 * b + 512] for b in range(3)]
        kvm = sb("kvm", [P, T, 2 * MEM_W])
        kmT = sb("kmT", [P, 2, SEQ])
        qm = sb("qm", [P, T, MEM_W])
        qmT = sb("qmT", [P, 2, SEQ])
        om = sb("om", [P, T, MEM_W])
        ahi = [sb(f"ahi{b}", [P, SEQ], F32R) for b in range(2)]
        alo = [sb(f"alo{b}", [P, SEQ], F32R) for b in range(2)]
        gate_n = [qkv[:, 0, 256 * b:256 * b + 256] for b in range(2)]
        silu_g = [qkv[:, 0, 512 + 256 * b:768 + 256 * b] for b in range(2)]
        act_f = [qkv[:, 0, 1024 + 256 * b:1280 + 256 * b] for b in range(2)]
        rs_diag = qkv[:, 1, 0:SEQ]
        rs_row = qkv[:, 1, SEQ:2 * SEQ]
        rope = probT_all[:, 0:4 * 192].rearrange("p (i n) -> p i n", i=4)
        g_mix = sb("g_mix", [P, D])
        g_mem, g_cross, g_ffn = sb("g_mem", [P, D]), sb("g_cross", [P, D]), sb("g_ffn", [P, D])
        g_qk = [sb("g_q", [P, D]), sb("g_k", [P, D])]
        table = sb("table", [P, N_TABLE])
        ident = table[:, 0:P]
        masks = table[:, P:P + 6 * P].rearrange("p (c n) -> p c n", c=2)
        freqs = table[:, 7 * P:7 * P + NFREQ]
        small = sb("small", [P, DEPTH, N_SMALL])
        g_sub, g_qm, g_km = (small[:, :, HD * i:HD * i + HD] for i in range(3))
        lam_in = [small[:, :, 3 * HD + 32 * i:3 * HD + 32 * i + 32] for i in range(4)]
        ones = sb("ones", [P, P])
        lam_dot = sb("lam_dot", [P, 2, DEPTH])
        lam_exp = sb("lam_exp", [P, 2, DEPTH])
        neg_lam = sb("neg_lam", [P, DEPTH])
        pos_i = sb("pos_i", [P, T], I32)
        pos_f = sb("pos_f", [P, T])
        ang = sb("ang", [P, 2, T, NFREQ])
        turns = sb("turns", [P, 2, T, NFREQ])
        cs = sb("cs", [P, 2, T, NFREQ])
        ss = sb("ss", [P, T])
        rs = sb("rs", [P, 3, T])
        mem_ss = sb("mem_ss", [P, T])
        mem_r = sb("mem_r", [P, T])
        g32 = sb("g32", [P, T, 32])
        nv, nh, ny, nt = (sb(n, [P, 40]) for n in ("nv", "nh", "ny", "nt"))
        mx = sb("mx", [P, NS, T])
        nm = sb("nm", [P, NS, T])
        zs = sb("zs", [P, NS, T])
        rz = sb("rz", [P, HEADS, T])
        lam_z = sb("lam_z", [P, 2, T])
        qscale = sb("qscale", [P, T, MEM_HEADS])

        ps = ctx.enter_context(nc.psum_tensor("ps", [P, 8, 512], F32))

        def banks(a, b):
            return ps[:, a:b, :].rearrange("p b n -> p (b n)")

        def half_of(a, h):
            return a[:, 4 * h:4 * h + 4, :].rearrange("p k n -> p (k n)")

        s_x = [signal(f"x_loaded{h}") for h in range(2)]
        s_mem = signal("mem_loaded")
        s_table = signal("table_loaded")
        s_small = signal("small_gains_loaded")
        s_pos = signal("positions_loaded")
        s_gmix0 = signal("first_gain_loaded")
        s_ones = signal("ones_set")
        s_lam = signal("lambda_ready")
        s_cs = signal("angles_ready")
        s_sin = signal("sines_ready")
        s_memss = signal("mem_squares")
        s_memr = signal("mem_roots")
        s_out = signal("stored")
        s_gain = signal("gains_loaded", 16 * 5)
        s_gmix = signal("mix_gain_loaded", 16)
        mem_in = signal("mem_in", 16)
        raw_in = [signal(f"raw_in{s}") for s in range(RING)]
        hi_done = [signal(f"hi_done{s}", FILLS) for s in range(RING)]
        lo_done = [signal(f"lo_done{s}", FILLS) for s in range(RING)]
        used = [signal(f"used{s}", FILLS) for s in range(RING)]
        x_new = signal("x_new", 3)
        ss_done = signal("ss_done", 3)
        rs_ready = signal("rs_ready", 3)
        xn_ready = signal("xn_ready", 2 * (BUILDS - 1))
        xm_ready = signal("xm_ready", 1)
        t_ps = signal("t_ps", 2 * BUILDS)
        t_hi = signal("t_hi", 2 * BUILDS)
        t_lo = signal("t_lo", 2 * BUILDS)
        proj_out = signal("proj_out", NCHUNK)
        mkv_out = signal("mkv_out", 1)
        km_ready = signal("km_ready", 1)
        mq_out = signal("mq_out", 1)
        sqr = signal("sqr", 2)
        scaled = signal("scaled", 2)
        roped = signal("roped", 2)
        qkT_ps = signal("qkT_ps", 4)
        qkT_act = signal("qkT_act", 2)
        qkT_dve = signal("qkT_dve", 2)
        scores = signal("scores", NS)
        masked = signal("masked", NS)
        nmax = signal("nmax", NS)
        probs = signal("probs", NS)
        combined = signal("combined", DIFF)
        pT_ps = signal("pT_ps", HEADS)
        pT_act = signal("pT_act", HEADS // 2)
        pT_dve = signal("pT_dve", HEADS // 2)
        pv = signal("pv", HEADS)
        o_read = signal("o_read", 1)
        kmT_ps, kmT_out = signal("kmT_ps", 1), signal("kmT_out", 1)
        qmT_ps, qmT_out = signal("qmT_ps", 1), signal("qmT_out", 1)
        m_scores, m_max, m_probs = (signal(n, MEM_HEADS) for n in ("m_scores", "m_max", "m_probs"))
        m_pT_ps, m_pT, m_pv = (signal(n, MEM_HEADS) for n in ("m_pT_ps", "m_pT", "m_pv"))
        om_ready, omT_ps, om_hi, om_lo = (signal(n, 1) for n in ("om_ready", "omT_ps", "om_hi", "om_lo"))
        diag_ready, row_ps, row_out = (signal(n, 1) for n in ("diag_ready", "row_ps", "row_out"))
        gate_done = signal("gate_done", FCH)
        silu_done = signal("silu_done", FCH)
        glu = signal("glu", FCH)
        act_hi = signal("act_hi", FCH)
        act_lo = signal("act_lo", FCH)
        down_even = signal("down_even", PAIRS)
        dve_chain = signal("dve_chain")
        pool_chain = signal("pool_chain")

        def dmas_before_ffn(s, upto=U_FFN):
            return sum(1 for u in range(upto) if u % RING == s)

        per_layer_dmas = [dmas_before_ffn(s) + PAIRS * (2 if s < 2 else 1) for s in range(RING)]

        def raw_level(layer, u, pair=0):
            s = u % RING
            if u < U_FFN:
                n = dmas_before_ffn(s, u + 1)
            else:
                n = dmas_before_ffn(s) + (pair + 1) * (2 if s < 2 else 1)
            return 16 * (layer * per_layer_dmas[s] + n)

        def fill(u, pair=0):
            return u // RING + pair

        def used_before(layer, u, pair=0):
            return used[u % RING].at(layer, fill(u, pair))

        def used_after(layer, u, pair=0):
            return used[u % RING].at(layer, fill(u, pair) + 1)

        block = ctx.enter_context(nc.Block())

        @block.sync
        def _(sp):
            x_in = x.rearrange("b (t p) d -> p (b t) d", p=P)
            for h in range(2):
                sp.dma_start(xs[:, :, 512 * h:512 * h + 512], x_in[:, :, 512 * h:512 * h + 512]).then_inc(s_x[h].sem, 16)

            def load(layer, u, src, pair=0):
                s = u % RING
                if layer or u >= RING:
                    sp.wait_ge(hi_done[s].sem, hi_done[s].at(layer, fill(u, pair)))
                    sp.wait_ge(lo_done[s].sem, lo_done[s].at(layer, fill(u, pair)))
                for dst, part in src:
                    sp.dma_start(dst, part).then_inc(raw_in[s].sem, 16)

            def view(u, k):
                return raw[u % RING][:].rearrange("p (k n) -> p k n", k=k)

            for layer in range(DEPTH):
                w_in = w["w_in"][layer].rearrange("(k p) n -> p k n", p=P)
                w_mkv = w["w_mkv"][layer].rearrange("(k p) n -> p k n", p=P)
                w_out = w["w_out"][layer].rearrange("(k p) n -> p k n", p=P)
                w_mq = w["w_mq"][layer].rearrange("(k p) n -> p k n", p=P)
                w_mo = w["w_mo"][layer].rearrange("(k p) n -> p k n", p=P)
                w_gu = w["w_gate_up"][layer].rearrange("(k p) (j n) -> p k j n", p=P, j=2)
                w_down = w["w_down"][layer].rearrange("(k p) n -> p k n", p=P)
                for c in range(NCHUNK):
                    for h in range(2):
                        u = U_QKV + 2 * c + h
                        load(layer, u, [(view(u, 4), w_in[:, 4 * h:4 * h + 4, 512 * c:512 * c + 512])])
                for h in range(2):
                    load(layer, U_MKV + h, [(view(U_MKV + h, 4), w_mkv[:, 4 * h:4 * h + 4, :])])
                for h in range(2):
                    for c in range(2):
                        u = U_OUT + 2 * h + c
                        load(layer, u, [(view(u, 4), w_out[:, 4 * h:4 * h + 4, 512 * c:512 * c + 512])])
                for h in range(2):
                    u = U_MQ + h
                    load(layer, u, [(raw[u % RING][:, 0:1024].rearrange("p (k n) -> p k n", k=4),
                                     w_mq[:, 4 * h:4 * h + 4, :])])
                load(layer, U_MO, [(view(U_MO, 2), w_mo)])
                with sp.Fori(0, PAIRS) as i:
                    for b in range(2):
                        u = U_FFN + b
                        dst = raw[u % RING][:].rearrange("p (k j n) -> p k j n", k=KC, j=2)
                        load(layer, u, [(dst[:, :, j, :], w_gu[:, :, j, bass.ds(i * 256 + b * 128, 128)])
                                        for j in range(2)], i)
                    u = U_FFN + 2
                    load(layer, u, [(view(u, 2), w_down[:, bass.ds(i * 2, 2), :])], i)
            sp.wait_ge(x_new.sem, x_new.at(DEPTH - 1, 3))
            sp.dma_start(out.rearrange("b (t p) d -> p (b t) d", p=P), xs[:]).then_inc(s_out.sem, 16)
            sp.wait_ge(s_out.sem, 16)

        @block.gpsimd
        def _(pool):
            mem_rows = mem.rearrange("b (t p) d -> p (b t) d", p=P)
            pool.dma_start(qkv[:, :, 0:D], mem_rows).then_inc(s_mem.sem, 16)
            with nc.allow_non_contiguous_dma(reason="256 positions"):
                pool.dma_start(pos_i[:], positions.rearrange("b (t p) -> p (b t)", p=P)).then_inc(s_pos.sem, 16)

            links = [0]

            def link(ins):
                links[0] += 1
                ins.then_inc(pool_chain.sem, 1)
                pool.wait_ge(pool_chain.sem, links[0])

            def split_lo(layer, u):
                s = u % RING
                pool.wait_ge(hi_done[s].sem, hi_done[s].at(layer, fill(u) + 1))
                pool.tensor_tensor(wlo[s][:], raw[s][:], whi[s][:].bitcast(F32), ALU.subtract)\
                    .then_inc(lo_done[s].sem, 1)

            for layer in range(DEPTH):
                if layer:
                    pool.wait_ge(xn_ready.sem, xn_ready.at(layer - 1, 8))
                for tile, name in ((g_mem, "norm_mem"), (g_qk[0], "q_gain"), (g_qk[1], "k_gain"),
                                   (g_cross, "norm_cross"), (g_ffn, "norm_ffn")):
                    pool.dma_start(tile[:], gains[name][layer:layer + 1, :].to_broadcast((P, D)))\
                        .then_inc(s_gain.sem, 16)
                pool.wait_ge(s_gain.sem, s_gain.at(layer, 16 * 5))
                pool.wait_ge(t_ps.sem, t_ps.at(layer, 2 * B_MIX + 2))
                if layer + 1 < DEPTH:
                    pool.dma_start(g_mix[:], gains["norm_mix"][layer + 1:layer + 2, :].to_broadcast((P, D)))\
                        .then_inc(s_gmix.sem, 16)
                pool.dma_start(xn[:], mem_rows).then_inc(mem_in.sem, 16)
                pool.wait_ge(mem_in.sem, mem_in.at(layer, 16))
                if layer == 0:
                    pool.wait_ge(s_memr.sem, 1)
                for t in range(T):
                    ins = pool.tensor_scalar(xn[:, t, :], xn[:, t, :], mem_r[:, t:t + 1], None, ALU.mult)
                link(ins)
                pool.tensor_tensor(xn[:], xn[:], g_mem[:].unsqueeze(1).to_broadcast((P, T, D)), ALU.mult)\
                    .then_inc(xm_ready.sem, 1)
                for part in range(2):
                    y = qkv[:, :, part * D:(part + 1) * D]
                    pool.wait_ge(scaled.sem, scaled.at(layer, part + 1))
                    if layer == 0 and part == 0:
                        pool.wait_ge(s_sin.sem, 1)
                    link(pool.tensor_tensor(y, y, g_qk[part][:].unsqueeze(1).to_broadcast((P, T, D)), ALU.mult))
                    for n, (groups, width, half, col, tab) in enumerate(ROT):
                        v = y[:, :, col:col + groups * width].rearrange("p t (g w) -> p t g w", w=width)
                        x1, x2 = v[:, :, :, 0:half], v[:, :, :, half:2 * half]
                        size = T * groups * half
                        m = [rope[:, i, 0:size].rearrange("p (t g f) -> p t g f", t=T, f=half) for i in range(4)]
                        cos, sin = (cs[:, i, :, tab:tab + half].unsqueeze(2).to_broadcast((P, T, groups, half))
                                    for i in range(2))
                        for i, (a, b) in enumerate(((x1, cos), (x2, sin), (x2, cos), (x1, sin))):
                            ins = pool.tensor_tensor(m[i], a, b, ALU.mult)
                        link(ins)
                        pool.tensor_tensor(x1, m[0], m[1], ALU.subtract)
                        ins = pool.tensor_tensor(x2, m[2], m[3], ALU.add)
                        if n == 0:
                            link(ins)
                        else:
                            ins.then_inc(roped.sem, 1)
                for u in range(U_OUT, U_OUT + 4):
                    split_lo(layer, u)

        @block.scalar
        def _(act):
            act.dma_start(g_mix[:], gains["norm_mix"][0:1, :].to_broadcast((P, D))).then_inc(s_gmix0.sem, 16)
            act.dma_start(table[:], consts["table"]).then_inc(s_table.sem, 16)
            act.dma_start(small[:].rearrange("p l n -> p (l n)"),
                          gains["small"].to_broadcast((P, DEPTH * N_SMALL))).then_inc(s_small.sem, 16)

            def split_hi(layer, u, pair=0):
                s = u % RING
                act.wait_ge(raw_in[s].sem, raw_level(layer, u, pair))
                if layer or u >= RING:
                    act.wait_ge(used[s].sem, used_before(layer, u, pair))
                act.activation(whi[s][:], raw[s][:], ACT.Copy).then_inc(hi_done[s].sem, 1)

            def build_hi(layer, b, h, bank):
                act.wait_ge(t_ps.sem, t_ps.at(layer, 2 * b + h + 1))
                act.activation(half_of(thi, h), banks(bank, bank + 2), ACT.Copy).then_inc(t_hi.sem, 1)

            def squares_of_x(layer, n):
                if layer == 0 and n == 0:
                    for h in range(2):
                        act.wait_ge(s_x[h].sem, 16)
                else:
                    act.wait_ge(x_new.sem, x_new.at(layer, n))
                for t in range(T):
                    ins = act.activation(sq[:, t * D:(t + 1) * D], xs[:, t, :], ACT.Square,
                                         accum_out=ss[:, t:t + 1])
                ins.then_inc(ss_done.sem, 1)

            split_hi(0, 0)
            split_hi(0, 1)
            for layer in range(DEPTH):
                for h in range(2):
                    build_hi(layer, B_MIX, h, 2 * h)
                if layer:
                    act.wait_ge(x_new.sem, x_new.at(layer, 0))
                squares_of_x(layer, 0)
                split_hi(layer, 2)
                if layer == 0:
                    act.wait_ge(s_mem.sem, 16)
                    act.wait_ge(rs_ready.sem, 1)
                    for t in range(T):
                        ins = act.activation(sq[:, t * D:(t + 1) * D], qkv[:, t, 0:D], ACT.Square,
                                             accum_out=mem_ss[:, t:t + 1])
                    ins.then_inc(s_memss.sem, 1)
                for c in range(NCHUNK):
                    split_hi(layer, 2 * c + 3)
                    act.wait_ge(used[(2 * c + 1) % RING].sem, used_after(layer, 2 * c + 1))
                    if c == 0:
                        act.wait_ge(rs_ready.sem, rs_ready.at(layer, 1))
                        if layer == 0:
                            act.wait_ge(s_memss.sem, 1)
                    for t in range(T):
                        ins = act.activation(qkv[:, t, 512 * c:512 * c + 512], ps[:, 4 + 2 * (c % 2) + t, :],
                                             ACT.Copy, scale=rs[:, 0, t:t + 1])
                    ins.then_inc(proj_out.sem, 1)
                    if c in (1, 3):
                        part = c // 2
                        act.wait_ge(proj_out.sem, proj_out.at(layer, c + 1))
                        if part:
                            act.wait_ge(scaled.sem, scaled.at(layer, part))
                        act.activation(sq[:], qkv[:, :, part * D:(part + 1) * D], ACT.Square)\
                            .then_inc(sqr.sem, 1)
                    split_hi(layer, 2 * c + 4)
                    if layer == 0 and c == 0:
                        act.wait_ge(s_cs.sem, 1)
                        act.activation(cs[:], ang[:], ACT.Sin).then_inc(s_sin.sem, 1)
                        act.wait_ge(s_lam.sem, 1)
                        act.activation(lam_exp[:], lam_dot[:], ACT.Exp).then_inc(s_lam.sem, 1)
                    if c == 4:
                        act.wait_ge(qkT_ps.sem, qkT_ps.at(layer, 1))
                        act.activation(half_of(qT, 0), banks(0, 2), ACT.Copy).then_inc(qkT_act.sem, 1)
                act.wait_ge(qkT_ps.sem, qkT_ps.at(layer, 3))
                act.activation(half_of(kT, 0), banks(0, 2), ACT.Copy).then_inc(qkT_act.sem, 1)

                def exps(n):
                    _, _, rows = SOFTMAXES[n]
                    act.wait_ge(nmax.sem, nmax.at(layer, n + 1))
                    for t, (a, b) in enumerate(((0, P), (P, 3 * P))):
                        ins = act.activation(prob[n % 4][:, a:b], prob[n % 4][:, a:b], ACT.Exp,
                                             bias=nm[:, n, t:t + 1], scale=float(rows) ** -0.5,
                                             accum_out=zs[:, n, t:t + 1])
                    ins.then_inc(probs.sem, 1)

                def probT_out(m):
                    act.wait_ge(pT_ps.sem, pT_ps.at(layer, m + 1))
                    if m >= 3:
                        act.wait_ge(pv.sem, pv.at(layer, m - 2))
                    act.activation(probT[m % 3][:, 0:384], ps[:, 2 + m % 2, 0:384], ACT.Copy)\
                        .then_inc(pT_act.sem, 1)

                for n in range(NS + 2):
                    if n < NS:
                        exps(n)
                    for m in range(0, HEADS, 2):
                        if LAST_OF[m] + 2 == n:
                            probT_out(m)
                    if n in (MEM_BUILD_AT[0], MEM_BUILD_AT[1]):
                        build_hi(layer, B_MEM, MEM_BUILD_AT.index(n), 6)
                    if n == 13:
                        split_hi(layer, 15)
                act.wait_ge(used[(U_MKV + 1) % RING].sem, used_after(layer, U_MKV + 1))
                act.activation(kvm[:], ps[:, 6:8, :], ACT.Copy).then_inc(mkv_out.sem, 1)
                split_hi(layer, 16)
                build_hi(layer, B_HEADS, 0, 0)
                split_hi(layer, 17)
                build_hi(layer, B_HEADS, 1, 2)
                split_hi(layer, 18)
                split_hi(layer, 19)
                split_hi(layer, 20)
                for h in range(2):
                    build_hi(layer, B_CROSS, h, 2 * h)
                squares_of_x(layer, 1)
                act.wait_ge(kmT_ps.sem, kmT_ps.at(layer, 1))
                act.activation(kmT[:].rearrange("p j n -> p (j n)"), ps[:, 6, :], ACT.Copy)\
                    .then_inc(kmT_out.sem, 1)
                act.wait_ge(used[(U_MQ + 1) % RING].sem, used_after(layer, U_MQ + 1))
                act.activation(qm[:], ps[:, 4:6, 0:MEM_W], ACT.Copy).then_inc(mq_out.sem, 1)
                act.wait_ge(qmT_ps.sem, qmT_ps.at(layer, 1))
                act.activation(qmT[:].rearrange("p j n -> p (j n)"), ps[:, 7, :], ACT.Copy)\
                    .then_inc(qmT_out.sem, 1)
                split_hi(layer, 21)
                for g in range(MEM_HEADS):
                    act.wait_ge(m_max.sem, m_max.at(layer, g + 1))
                    for t in range(T):
                        ins = act.activation(prob[g][:, 256 * t:256 * t + 256],
                                             ps[:, g, 256 * t:256 * t + 256], ACT.Exp,
                                             bias=nm[:, g, t:t + 1], scale=qscale[:, t, g:g + 1],
                                             accum_out=zs[:, g, t:t + 1])
                    ins.then_inc(m_probs.sem, 1)
                act.wait_ge(omT_ps.sem, omT_ps.at(layer, 1))
                act.activation(thi[:, 0:2, :].rearrange("p k n -> p (k n)"), ps[:, 7, :], ACT.Copy)\
                    .then_inc(om_hi.sem, 1)
                split_hi(layer, 22)
                for h in range(2):
                    build_hi(layer, B_FFN, h, 2 * h)
                squares_of_x(layer, 2)

                def silu_step(pair, b):
                    act.wait_ge(gate_done.sem, gate_done.at(layer, pair * 2 + b + 1))
                    if not_first(pair):
                        act.wait_ge(glu.sem, glu.at(layer, pair * 2 + b - 1))
                    act.activation(silu_g[b], gate_n[b], ACT.Silu).then_inc(silu_done.sem, 1)

                silu_step(0, 0)
                split_hi(layer, U_FFN, 1)
                split_hi(layer, U_FFN + 2, 0)
                silu_step(0, 1)
                split_hi(layer, U_FFN + 1, 1)
                with act.Fori(1, PAIRS - 1) as i:
                    silu_step(i, 0)
                    split_hi(layer, U_FFN, i + 1)
                    split_hi(layer, U_FFN + 2, i)
                    silu_step(i, 1)
                    split_hi(layer, U_FFN + 1, i + 1)
                silu_step(PAIRS - 1, 0)
                if layer + 1 < DEPTH:
                    split_hi(layer + 1, 0)
                split_hi(layer, U_FFN + 2, PAIRS - 1)
                silu_step(PAIRS - 1, 1)
                if layer + 1 < DEPTH:
                    split_hi(layer + 1, 1)

        @block.vector
        def _(dve):
            links = [0]

            def link(ins):
                links[0] += 1
                ins.then_inc(dve_chain.sem, 1)
                dve.wait_ge(dve_chain.sem, links[0])

            def split_lo(layer, u, pair=0):
                s = u % RING
                dve.wait_ge(hi_done[s].sem, hi_done[s].at(layer, fill(u, pair) + 1))
                dve.tensor_tensor(wlo[s][:], raw[s][:], whi[s][:].bitcast(F32), ALU.subtract)\
                   .then_inc(lo_done[s].sem, 1)

            def rsqrt(n):
                v, h, y, t = (a[:, 0:n] for a in (nv, nh, ny, nt))
                dve.tensor_scalar(h, v, -0.5, None, ALU.mult)
                link(dve.tensor_scalar(y.bitcast(I32), v.bitcast(I32), -0.5, 1597463007.0, ALU.mult, ALU.add))
                for _ in range(3):
                    link(dve.tensor_tensor(t, y, h, ALU.mult))
                    link(dve.tensor_tensor(t, t, y, ALU.mult))
                    link(dve.scalar_tensor_tensor(y, t, 1.5, y, ALU.add, ALU.mult))

            def mean_eps(dst, sums, width):
                link(dve.tensor_scalar(dst, sums, 1.0 / width, EPS, ALU.mult, ALU.add))

            def roots_of_x(layer, n):
                dve.wait_ge(ss_done.sem, ss_done.at(layer, n + 1))
                mean_eps(nv[:, 0:T], ss[:], D)
                rsqrt(T)
                dve.tensor_copy(rs[:, n, :], ny[:, 0:T]).then_inc(rs_ready.sem, 1)

            def gain_x(gain, h):
                cols = slice(512 * h, 512 * h + 512)
                dve.tensor_tensor(xn[:, :, cols], xs[:, :, cols], gain[:, cols].unsqueeze(1).to_broadcast((P, T, 512)),
                                  ALU.mult).then_inc(xn_ready.sem, 1)

            def build_lo(layer, b, h, bank):
                dve.wait_ge(t_hi.sem, t_hi.at(layer, 2 * b + h + 1))
                dve.tensor_tensor(half_of(tlo, h), banks(bank, bank + 2), half_of(thi, h).bitcast(F32), ALU.subtract)\
                   .then_inc(t_lo.sem, 1)

            def by_head(a, heads):
                return a.rearrange("p t (h d) -> p t h d", h=heads)

            def head_roots(y, squares, heads):
                link(dve.tensor_tensor(squares, y, y, ALU.mult))
                link(dve.tensor_reduce(nh[:, 0:T * heads], squares, AX_X, ALU.add))
                mean_eps(nv[:, 0:T * heads], nh[:, 0:T * heads], HD)
                rsqrt(T * heads)
                return ny[:, 0:T * heads].rearrange("p (t h) -> p t h", t=T)

            def per_head(r, heads):
                return r.unsqueeze(3).to_broadcast((P, T, heads, HD))

            def every_head(gain, heads):
                return gain.unsqueeze(1).unsqueeze(1).to_broadcast((P, T, heads, HD))

            def add_to_x(layer, units, first_bank, gain, scale=None):
                for c in range(2):
                    cols = slice(512 * c, 512 * c + 512)
                    dve.wait_ge(used[units[c][0] % RING].sem, used_after(layer, *units[c]))
                    b = first_bank[c]
                    if scale is None:
                        ins = dve.tensor_tensor(xs[:, :, cols], ps[:, b:b + 2, :], xs[:, :, cols], ALU.add)
                    else:
                        for t in range(T):
                            ins = dve.scalar_tensor_tensor(xs[:, t, cols], ps[:, b + t, :], scale[:, t:t + 1],
                                                           xs[:, t, cols], ALU.mult, ALU.add)
                    if c == 0:
                        if gain is not None:
                            link(ins)
                            gain_x(gain, 0)
                    else:
                        ins.then_inc(x_new.sem, 1)
                        x_news[0] += 1
                        if gain is not None:
                            dve.wait_ge(x_new.sem, x_news[0])
                            gain_x(gain, 1)

            x_news = [0]

            dve.memset(ones[:], 1.0).then_inc(s_ones.sem, 1)
            dve.wait_ge(s_gmix0.sem, 16)
            for h in range(2):
                dve.wait_ge(s_x[h].sem, 16)
                gain_x(g_mix, h)
            split_lo(0, 0)
            split_lo(0, 1)

            def tables():
                dve.wait_ge(s_pos.sem, 16)
                dve.wait_ge(s_table.sem, 16)
                dve.wait_ge(s_small.sem, 16)
                link(dve.tensor_copy(pos_f[:], pos_i[:]))
                for t in range(T):
                    for i in range(2):
                        ins = dve.tensor_scalar(ang[:, i, t, :], freqs, pos_f[:, t:t + 1], None, ALU.mult)
                link(ins)
                magic = 12582912.0
                for i, quarter in ((0, 0.25), (1, 0.0)):
                    ins = dve.tensor_scalar(turns[:, i], ang[:, i], 1.0 / (2.0 * math.pi), quarter, ALU.mult, ALU.add)
                link(ins)
                link(dve.tensor_scalar(turns[:], turns[:], magic, None, ALU.add))
                link(dve.tensor_scalar(turns[:], turns[:], -magic, None, ALU.add))
                for c in TWO_PI:
                    link(dve.scalar_tensor_tensor(ang[:].rearrange("p i t f -> p (i t f)"),
                                                  turns[:].rearrange("p i t f -> p (i t f)"), -c,
                                                  ang[:].rearrange("p i t f -> p (i t f)"), ALU.mult, ALU.add))
                link(dve.tensor_scalar(ang[:, 0], ang[:, 0], math.pi / 2, None, ALU.add))
                dve.tensor_scalar(ang[:], ang[:], 3.1415925, -3.1415925, ALU.min, ALU.max).then_inc(s_cs.sem, 1)
                for i in range(2):
                    for l in range(DEPTH):
                        link(dve.tensor_tensor_reduce(nt[:, 0:32], lam_in[2 * i][:, l, :], lam_in[2 * i + 1][:, l, :],
                                                      1.0, 0.0, ALU.mult, ALU.add, lam_dot[:, i, l:l + 1]))
                for l in range(DEPTH):
                    ins = dve.tensor_scalar(g_sub[:, l, :], g_sub[:, l, :], 1.0 - lam_init(l), None, ALU.mult)
                    dve.tensor_tensor(g_km[:, l, :], g_km[:, l, :], g_qm[:, l, :], ALU.mult)
                ins = dve.memset(nt[:, 0:32], 0.0)
                ins.then_inc(s_lam.sem, 1)
                dve.wait_ge(s_lam.sem, 2)
                link(dve.tensor_tensor(neg_lam[:], lam_exp[:, 1, :], lam_exp[:, 0, :], ALU.subtract))
                for l in range(DEPTH):
                    ins = dve.tensor_scalar(neg_lam[:, l:l + 1], neg_lam[:, l:l + 1], -lam_init(l), None, ALU.add)
                link(ins)

            for layer in range(DEPTH):
                for h in range(2):
                    build_lo(layer, B_MIX, h, 2 * h)
                roots_of_x(layer, 0)
                split_lo(layer, 2)
                if layer == 0:
                    dve.wait_ge(s_memss.sem, 1)
                    mean_eps(nv[:, 0:T], mem_ss[:], D)
                    rsqrt(T)
                    dve.tensor_copy(mem_r[:], ny[:, 0:T]).then_inc(s_memr.sem, 1)

                def scale_qk(part):
                    y = qkv[:, :, part * D:(part + 1) * D]
                    dve.wait_ge(sqr.sem, sqr.at(layer, part + 1))
                    link(dve.tensor_reduce(g32[:], sq[:].rearrange("p (t g w) -> p t g w", t=T, w=32), AX_X, ALU.add))
                    v = nv[:, 0:T * GROUPS].rearrange("p (t g) -> p t g", t=T)
                    dve.tensor_scalar(v[:, :, 0:8], g32[:, :, 0:8], 1.0 / 32, EPS, ALU.mult, ALU.add)
                    two = g32[:, :, 8:32].rearrange("p t (g w) -> p t g w", w=2)
                    link(dve.tensor_tensor(v[:, :, 8:20], two[:, :, :, 0], two[:, :, :, 1], ALU.add))
                    mean_eps(v[:, :, 8:20], v[:, :, 8:20], HD)
                    rsqrt(T * GROUPS)
                    r = ny[:, 0:T * GROUPS].rearrange("p (t g) -> p t g", t=T)
                    for n, (groups, width, _, col, _) in enumerate(ROT):
                        z = y[:, :, col:col + groups * width].rearrange("p t (g w) -> p t g w", w=width)
                        rg = r[:, :, 8 * n:8 * n + groups].unsqueeze(3).to_broadcast((P, T, groups, width))
                        ins = dve.tensor_tensor(z, z, rg, ALU.mult)
                    ins.then_inc(scaled.sem, 1)

                for c in range(NCHUNK):
                    if c == 4:
                        scale_qk(1)
                    split_lo(layer, 2 * c + 3)
                    if c == 2:
                        scale_qk(0)
                    if c < 5:
                        split_lo(layer, 2 * c + 4)
                    if layer == 0 and c == 0:
                        tables()
                    if c == 4:
                        dve.wait_ge(qkT_ps.sem, qkT_ps.at(layer, 2))
                        dve.tensor_copy(half_of(qT, 1), banks(2, 4)).then_inc(qkT_dve.sem, 1)
                dve.wait_ge(qkT_ps.sem, qkT_ps.at(layer, 4))
                dve.tensor_copy(half_of(kT, 1), banks(2, 4)).then_inc(qkT_dve.sem, 1)

                def mask_max(n):
                    head, _, rows = SOFTMAXES[n]
                    kind = 1 if DIFF <= head < DIFF + DIL else 0
                    dve.wait_ge(scores.sem, scores.at(layer, n + 1))
                    if n >= 4:
                        dve.wait_ge(pT_ps.sem, pT_ps.at(layer, SOFTMAXES[n - 4][0] + 1))
                    for t, (a, b) in enumerate(((0, P), (P, 3 * P))):
                        ins = dve.tensor_tensor_reduce(prob[n % 4][:, a:b], ps[:, n % 2, a:b], masks[:, kind, a:b],
                                                       1.0, 3.0 * NEG, ALU.add, ALU.max, mx[:, n, t:t + 1])
                    ins.then_inc(masked.sem, 1)
                    dve.wait_ge(masked.sem, masked.at(layer, n + 1))
                    dve.tensor_scalar(nm[:, n, :], mx[:, n, :], -float(rows) ** -0.5, None, ALU.mult)\
                       .then_inc(nmax.sem, 1)

                def combine(h):
                    n = 2 * h
                    dve.wait_ge(probs.sem, probs.at(layer, n + 2))
                    link(dve.reciprocal(lam_z[:, 0, :], zs[:, n + 1, :]))
                    link(dve.scalar_tensor_tensor(lam_z[:, 1, :], lam_z[:, 0, :], neg_lam[:, layer:layer + 1],
                                                  zs[:, n, :], ALU.mult, ALU.mult))
                    p1, p2 = prob[n % 4], prob[(n + 1) % 4]
                    for t, (a, b) in enumerate(((0, P), (P, 3 * P))):
                        ins = dve.scalar_tensor_tensor(p1[:, a:b], p2[:, a:b], lam_z[:, 1, t:t + 1], p1[:, a:b],
                                                       ALU.mult, ALU.add)
                    ins.then_inc(combined.sem, 1)

                def probT_out(m):
                    dve.wait_ge(pT_ps.sem, pT_ps.at(layer, m + 1))
                    if m >= 3:
                        dve.wait_ge(pv.sem, pv.at(layer, m - 2))
                    dve.tensor_copy(probT[m % 3][:, 0:384], ps[:, 2 + m % 2, 0:384]).then_inc(pT_dve.sem, 1)

                def heads_out(half):
                    dve.wait_ge(pv.sem, pv.at(layer, 8 * half + 8))
                    dve.wait_ge(probs.sem, probs.at(layer, LAST_OF[8 * half + 7] + 1))
                    r = rz[:, 8 * half:8 * half + 8, :]
                    if half == 0:
                        dve.reciprocal(r[:, 0:4, :], zs[:, 0:8:2, :])
                        link(dve.reciprocal(r[:, 4:8, :], zs[:, 8:12, :]))
                    else:
                        link(dve.reciprocal(r, zs[:, 12:20, :]))
                    return dve.tensor_tensor(by_head(xn[:, :, 512 * half:512 * half + 512], 8), by_head(ps[:, 4:6, :], 8),
                                             per_head(r.rearrange("p h t -> p t h"), 8), ALU.mult)

                for n in range(NS + 3):
                    if n < NS:
                        mask_max(n)
                    for h in range(HEADS):
                        if h < DIFF and LAST_OF[h] + 1 == n:
                            combine(h)
                        if h % 2 and LAST_OF[h] + 2 == n:
                            probT_out(h)
                    if n in MEM_BUILD_AT:
                        build_lo(layer, B_MEM, MEM_BUILD_AT.index(n), 6)
                    if n == HALF_AT:
                        heads_out(0).then_inc(o_read.sem, 1)
                    if n == NS:
                        dve.wait_ge(o_read.sem, o_read.at(layer, 1))
                        y = by_head(xn[:, :, 0:DIFF * HD], DIFF)
                        r = head_roots(y, by_head(om[:], DIFF), DIFF)
                        link(dve.tensor_tensor(y, y, per_head(r, DIFF), ALU.mult))
                        dve.tensor_tensor(y, y, every_head(g_sub[:, layer, :], DIFF), ALU.mult)\
                           .then_inc(xn_ready.sem, 1)
                heads_out(1).then_inc(xn_ready.sem, 1)
                build_lo(layer, B_HEADS, 0, 0)
                build_lo(layer, B_HEADS, 1, 2)
                dve.wait_ge(mkv_out.sem, mkv_out.at(layer, 1))
                y = by_head(kvm[:, :, 0:MEM_W], MEM_HEADS)
                r = head_roots(y, by_head(om[:], MEM_HEADS), MEM_HEADS)
                link(dve.tensor_tensor(y, y, per_head(r, MEM_HEADS), ALU.mult))
                dve.tensor_tensor(y, y, every_head(g_km[:, layer, :], MEM_HEADS), ALU.mult).then_inc(km_ready.sem, 1)
                split_lo(layer, 18)
                dve.wait_ge(s_gain.sem, s_gain.at(layer, 16 * 5))
                add_to_x(layer, [(U_OUT + 2,), (U_OUT + 3,)], (6, 4), g_cross)
                split_lo(layer, 19)
                for h in range(2):
                    build_lo(layer, B_CROSS, h, 2 * h)
                roots_of_x(layer, 1)
                split_lo(layer, 20)

                dve.wait_ge(rs_ready.sem, rs_ready.at(layer, 2))
                dve.tensor_tensor(nm[:, NS - 1, :], rs[:, 1, :], rs[:, 1, :], ALU.mult)
                dve.wait_ge(mq_out.sem, mq_out.at(layer, 1))
                y, squares = by_head(qm[:], MEM_HEADS), by_head(om[:], MEM_HEADS)
                link(dve.tensor_tensor(squares, y, y, ALU.mult))
                link(dve.tensor_reduce(nh[:, 0:8], squares, AX_X, ALU.add))
                link(dve.tensor_scalar(nt[:, 0:8], nh[:, 0:8], 1.0 / HD, None, ALU.mult))
                for t in range(T):
                    ins = dve.tensor_scalar(nv[:, 4 * t:4 * t + 4], nt[:, 4 * t:4 * t + 4], nm[:, NS - 1, t:t + 1],
                                            EPS, ALU.mult, ALU.add)
                link(ins)
                rsqrt(8)
                for t in range(T):
                    ins = dve.tensor_scalar(qscale[:, t, :], ny[:, 4 * t:4 * t + 4], rs[:, 1, t:t + 1],
                                            float(HD) ** -0.5, ALU.mult, ALU.mult)
                link(ins)

                def mem_probT(g):
                    dve.wait_ge(m_pT_ps.sem, m_pT_ps.at(layer, g + 1))
                    if g >= 3:
                        dve.wait_ge(m_pv.sem, m_pv.at(layer, g - 2))
                    dve.tensor_copy(probT[g % 3], ps[:, 5 + g % 2, :]).then_inc(m_pT.sem, 1)

                for g in range(MEM_HEADS):
                    dve.wait_ge(m_scores.sem, m_scores.at(layer, g + 1))
                    link(dve.tensor_reduce(mx[:, g, :], ps[:, g, :].rearrange("p (t n) -> p t n", t=T), AX_X, ALU.max))
                    dve.scalar_tensor_tensor(nm[:, g, :], mx[:, g, :], -1.0, qscale[:, :, g], ALU.mult, ALU.mult)\
                       .then_inc(m_max.sem, 1)
                    if g >= 2:
                        mem_probT(g - 2)
                for g in range(MEM_HEADS - 2, MEM_HEADS):
                    mem_probT(g)
                dve.wait_ge(m_probs.sem, m_probs.at(layer, MEM_HEADS))
                link(dve.reciprocal(rz[:, 0:MEM_HEADS, :], zs[:, 0:MEM_HEADS, :]))
                dve.wait_ge(m_pv.sem, m_pv.at(layer, MEM_HEADS))
                dve.tensor_tensor(by_head(om[:], MEM_HEADS),
                                  ps[:, 4, :].rearrange("p (t h d) -> p t h d", t=T, d=HD),
                                  per_head(rz[:, 0:MEM_HEADS, :].rearrange("p h t -> p t h"), MEM_HEADS), ALU.mult)\
                   .then_inc(om_ready.sem, 1)
                dve.wait_ge(om_hi.sem, om_hi.at(layer, 1))
                dve.tensor_tensor(tlo[:, 0:2, :].rearrange("p k n -> p (k n)"), ps[:, 7, :],
                                  thi[:, 0:2, :].rearrange("p k n -> p (k n)").bitcast(F32), ALU.subtract)\
                   .then_inc(om_lo.sem, 1)
                split_lo(layer, 21)
                add_to_x(layer, [(U_MO,)] * 2, (0, 2), g_ffn)

                split_lo(layer, 22)
                for h in range(2):
                    build_lo(layer, B_FFN, h, 2 * h)
                roots_of_x(layer, 2)
                dve.wait_ge(rs_ready.sem, rs_ready.at(layer, 3))
                for t in range(T):
                    ins = dve.tensor_scalar(rs_diag[:, t * P:(t + 1) * P], ident, rs[:, 2, t:t + 1], None, ALU.mult)
                ins.then_inc(diag_ready.sem, 1)
                dve.wait_ge(row_ps.sem, row_ps.at(layer, 1))
                dve.tensor_copy(rs_row, ps[:, 2, 0:SEQ]).then_inc(row_out.sem, 1)
                dve.wait_ge(row_out.sem, row_out.at(layer, 1))

                def gate_step(pair, b):
                    dve.wait_ge(used[(U_FFN + b) % RING].sem, used_after(layer, U_FFN + b, pair))
                    if not_first(pair):
                        dve.wait_ge(silu_done.sem, silu_done.at(layer, pair * 2 + b - 1))
                    dve.tensor_tensor(gate_n[b], ps[:, b, 0:256], rs_row, ALU.mult).then_inc(gate_done.sem, 1)

                def glu_step(pair, b):
                    f = pair * 2 + b
                    dve.wait_ge(silu_done.sem, silu_done.at(layer, f + 1))
                    dve.tensor_tensor(act_f[b], ps[:, b, 256:512], silu_g[b], ALU.mult).then_inc(glu.sem, 1)
                    dve.wait_ge(glu.sem, glu.at(layer, f + 1))
                    if not_first(pair):
                        if b == 0:
                            dve.wait_ge(down_even.sem, down_even.at(layer, pair))
                        else:
                            dve.wait_ge(used[(U_FFN + 2) % RING].sem, used_after(layer, U_FFN + 2, pair - 1))
                    dve.tensor_copy(ahi[b][:], act_f[b]).then_inc(act_hi.sem, 1)
                    dve.wait_ge(act_hi.sem, act_hi.at(layer, f + 1))
                    dve.tensor_tensor(alo[b][:], act_f[b], ahi[b][:].bitcast(F32), ALU.subtract)\
                       .then_inc(act_lo.sem, 1)

                gate_step(0, 0)
                glu_step(0, 0)
                split_lo(layer, U_FFN, 1)
                split_lo(layer, U_FFN + 2, 0)
                gate_step(0, 1)
                glu_step(0, 1)
                split_lo(layer, U_FFN + 1, 1)
                with dve.Fori(1, PAIRS - 1) as i:
                    gate_step(i, 0)
                    glu_step(i, 0)
                    split_lo(layer, U_FFN, i + 1)
                    split_lo(layer, U_FFN + 2, i)
                    gate_step(i, 1)
                    glu_step(i, 1)
                    split_lo(layer, U_FFN + 1, i + 1)
                gate_step(PAIRS - 1, 0)
                glu_step(PAIRS - 1, 0)
                if layer + 1 < DEPTH:
                    split_lo(layer + 1, 0)
                split_lo(layer, U_FFN + 2, PAIRS - 1)
                gate_step(PAIRS - 1, 1)
                glu_step(PAIRS - 1, 1)
                if layer + 1 < DEPTH:
                    split_lo(layer + 1, 1)
                    dve.wait_ge(s_gmix.sem, s_gmix.at(layer, 16))
                add_to_x(layer, [(U_FFN + 2, PAIRS - 1)] * 2, (4, 6), g_mix if layer + 1 < DEPTH else None, rs[:, 2, :])

        @block.tensor
        def _(pe):
            def build(layer, b, h, bank, src):
                for k in range(4 * h, 4 * h + 4):
                    for t in range(T):
                        a = (k - 4 * h) * SEQ + t * P
                        ins = pe.transpose(ps[:, bank + a // 512, a % 512:a % 512 + P],
                                           src[:, t, k * P:(k + 1) * P], ident)
                ins.then_inc(t_ps.sem, 1)

            def build_of_x(layer, b):
                for h in range(2):
                    pe.wait_ge(xn_ready.sem, xn_ready.at(layer, XN_OF[b] + h + 1))
                    build(layer, b, h, 2 * h, xn)

            def with_unit(layer, u, chunks, cols, acc, k0, first, last, built=None):
                s = u % RING
                pe.wait_ge(lo_done[s].sem, lo_done[s].at(layer, fill(u) + 1))
                n = min(cols, 512)
                if built is not None:
                    pe.wait_ge(t_hi.sem, t_hi.at(layer, built))
                for part in (thi, tlo):
                    if part is tlo and built is not None:
                        pe.wait_ge(t_lo.sem, t_lo.at(layer, built))
                    for k in range(chunks):
                        for t in range(T):
                            for c in range(cols // n):
                                a = k * cols + c * n
                                x_t = part[:, k0 + k, t * P:(t + 1) * P]
                                end = last and k == chunks - 1
                                if part is thi:
                                    pe.matmul(acc(t, c), x_t, whi[s][:, a:a + n], start=first and k == 0, stop=False)
                                    pe.matmul(acc(t, c), x_t, wlo[s][:, a:a + n], start=False, stop=False)
                                else:
                                    ins = pe.matmul(acc(t, c), x_t, whi[s][:, a:a + n], start=False, stop=end)
                ins.then_inc(used[s].sem, 1)

            pe.wait_ge(s_table.sem, 16)
            for layer in range(DEPTH):
                build_of_x(layer, B_MIX)

                def transpose_qk(part, half, bank):
                    for j in range(4 * half, 4 * half + 4):
                        for t in range(T):
                            a = (j % 4) * SEQ + t * P
                            ins = pe.transpose(ps[:, bank + a // 512, a % 512:a % 512 + P],
                                               qkv[:, t, part * D + j * P:part * D + (j + 1) * P], ident)
                    ins.then_inc(qkT_ps.sem, 1)

                for c in range(NCHUNK):
                    if c >= 2:
                        pe.wait_ge(proj_out.sem, proj_out.at(layer, c - 1))
                    if c == 5:
                        pe.wait_ge(roped.sem, roped.at(layer, 1))
                        for half in range(2):
                            transpose_qk(0, half, 2 * half)

                    def acc(t, _):
                        return ps[:, 4 + 2 * (c % 2) + t, :]

                    for h in range(2):
                        with_unit(layer, U_QKV + 2 * c + h, 4, 512, acc, 4 * h, h == 0, h == 1,
                                  2 * B_MIX + h + 1 if c == 0 else None)
                pe.wait_ge(roped.sem, roped.at(layer, 2))
                pe.wait_ge(qkT_act.sem, qkT_act.at(layer, 1))
                pe.wait_ge(qkT_dve.sem, qkT_dve.at(layer, 1))
                for half in range(2):
                    transpose_qk(1, half, 2 * half)

                def score(n):
                    h, base, rows = SOFTMAXES[n]
                    if n >= 2:
                        pe.wait_ge(masked.sem, masked.at(layer, n - 1))
                    j = h // 2
                    q, k = qT[base:base + rows, j, :], kT[base:base + rows, j, :]
                    pe.matmul(ps[:, n % 2, 0:P], q[:, 0:P], k[:, 0:P], start=True, stop=True)
                    pe.matmul(ps[:, n % 2, P:3 * P], q[:, P:2 * P], k, start=True, stop=True)\
                      .then_inc(scores.sem, 1)

                def transpose_p(m):
                    n = 2 * m if m < DIFF else m + DIFF
                    if m < DIFF:
                        pe.wait_ge(combined.sem, combined.at(layer, m + 1))
                    else:
                        pe.wait_ge(probs.sem, probs.at(layer, n + 1))
                    if m >= 2:
                        if m % 2:
                            pe.wait_ge(pT_dve.sem, pT_dve.at(layer, m // 2))
                        else:
                            pe.wait_ge(pT_act.sem, pT_act.at(layer, m // 2))
                    for b in range(3):
                        ins = pe.transpose(ps[:, 2 + m % 2, b * P:(b + 1) * P], prob[n % 4][:, b * P:(b + 1) * P], ident)
                    ins.then_inc(pT_ps.sem, 1)

                def weigh_v(m):
                    if m % 2:
                        pe.wait_ge(pT_dve.sem, pT_dve.at(layer, m // 2 + 1))
                    else:
                        pe.wait_ge(pT_act.sem, pT_act.at(layer, m // 2 + 1))
                    if m == 8:
                        pe.wait_ge(o_read.sem, o_read.at(layer, 1))
                    p = probT[m % 3]
                    a = (m % 8) * HD
                    v = qkv[:, :, 2 * D + m * HD:2 * D + (m + 1) * HD]
                    pe.matmul(ps[:, 4, a:a + HD], p[:, 0:P], v[:, 0, :], start=True, stop=True)
                    pe.matmul(ps[:, 5, a:a + HD], p[:, P:2 * P], v[:, 0, :], start=True, stop=False)
                    pe.matmul(ps[:, 5, a:a + HD], p[:, 2 * P:3 * P], v[:, 1, :], start=False, stop=True)\
                      .then_inc(pv.sem, 1)

                def mem_piece(i):
                    k, t = i // 2, i % 2
                    u = U_MKV + k // 4
                    s = u % RING
                    if i % 8 == 0:
                        pe.wait_ge(lo_done[s].sem, lo_done[s].at(layer, fill(u) + 1))
                    if i == 0:
                        pe.wait_ge(t_lo.sem, t_lo.at(layer, 2 * B_MEM + 2))
                    cols = slice((k % 4) * 512, (k % 4) * 512 + 512)
                    tok = slice(t * P, (t + 1) * P)
                    acc = ps[:, 6 + t, :]
                    pe.matmul(acc, thi[:, k, tok], whi[s][:, cols], start=(k == 0), stop=False)
                    pe.matmul(acc, thi[:, k, tok], wlo[s][:, cols], start=False, stop=False)
                    ins = pe.matmul(acc, tlo[:, k, tok], whi[s][:, cols], start=False, stop=(k == KC - 1))
                    if i % 8 == 7:
                        ins.then_inc(used[s].sem, 1)

                pe.wait_ge(qkT_act.sem, qkT_act.at(layer, 2))
                pe.wait_ge(qkT_dve.sem, qkT_dve.at(layer, 2))
                for n in range(NS + 5):
                    if n < NS:
                        score(n)
                    if n in MEM_TRANSPOSE_AT:
                        h = MEM_TRANSPOSE_AT.index(n)
                        if h == 0:
                            pe.wait_ge(xm_ready.sem, xm_ready.at(layer, 1))
                            pe.wait_ge(proj_out.sem, proj_out.at(layer, NCHUNK))
                        else:
                            pe.wait_ge(t_lo.sem, t_lo.at(layer, 2 * B_MEM + 1))
                        build(layer, B_MEM, h, 6, xn)
                    if MEM_PIECES_FROM <= n < MEM_PIECES_FROM + 16:
                        mem_piece(n - MEM_PIECES_FROM)
                    for m in range(HEADS):
                        if LAST_OF[m] + 2 == n:
                            transpose_p(m)
                        if LAST_OF[m] + (3 if m < 8 else 4) == n:
                            weigh_v(m)

                def out_acc(c):
                    return lambda t, _: ps[:, (6, 4)[c] + t, :]

                pe.wait_ge(xn_ready.sem, xn_ready.at(layer, 3))
                pe.wait_ge(masked.sem, masked.at(layer, NS))
                build(layer, B_HEADS, 0, 0, xn)
                pe.wait_ge(mkv_out.sem, mkv_out.at(layer, 1))
                with_unit(layer, U_OUT, 4, 512, out_acc(0), 0, True, False, 2 * B_HEADS + 1)
                pe.wait_ge(xn_ready.sem, xn_ready.at(layer, 4))
                pe.wait_ge(pT_dve.sem, pT_dve.at(layer, HEADS // 2))
                build(layer, B_HEADS, 1, 2, xn)
                with_unit(layer, U_OUT + 1, 4, 512, out_acc(1), 0, True, False)
                with_unit(layer, U_OUT + 2, 4, 512, out_acc(0), 4, False, True, 2 * B_HEADS + 2)
                with_unit(layer, U_OUT + 3, 4, 512, out_acc(1), 4, False, True)

                def transpose_small(src, bank, sig):
                    for j in range(2):
                        for t in range(T):
                            a = j * SEQ + t * P
                            ins = pe.transpose(ps[:, bank, a:a + P], src[:, t, j * P:(j + 1) * P], ident)
                    ins.then_inc(sig.sem, 1)

                build_of_x(layer, B_CROSS)
                pe.wait_ge(km_ready.sem, km_ready.at(layer, 1))
                transpose_small(kvm, 6, kmT_ps)
                for h in range(2):
                    with_unit(layer, U_MQ + h, 4, MEM_W, lambda t, _: ps[:, 4 + t, 0:MEM_W], 4 * h, h == 0, h == 1,
                              2 * B_CROSS + h + 1)
                pe.wait_ge(mq_out.sem, mq_out.at(layer, 1))
                transpose_small(qm, 7, qmT_ps)
                pe.wait_ge(kmT_out.sem, kmT_out.at(layer, 1))
                pe.wait_ge(qmT_out.sem, qmT_out.at(layer, 1))

                def mem_transpose_p(g):
                    pe.wait_ge(m_probs.sem, m_probs.at(layer, g + 1))
                    if g >= 2:
                        pe.wait_ge(m_pT.sem, m_pT.at(layer, g - 1))
                    for t in range(T):
                        for k in range(T):
                            a = k * SEQ + t * P
                            ins = pe.transpose(ps[:, 5 + g % 2, a:a + P],
                                               prob[g][:, 256 * t + k * P:256 * t + (k + 1) * P], ident)
                    ins.then_inc(m_pT_ps.sem, 1)

                def mem_weigh_v(g):
                    pe.wait_ge(m_pT.sem, m_pT.at(layer, g + 1))
                    for t in range(T):
                        for k in range(T):
                            ins = pe.matmul(ps[:, 4, t * 256 + g * HD:t * 256 + (g + 1) * HD],
                                            probT[g % 3][:, k * SEQ + t * P:k * SEQ + (t + 1) * P],
                                            kvm[:, k, MEM_W + g * HD:MEM_W + (g + 1) * HD],
                                            start=(k == 0), stop=(k == T - 1))
                    ins.then_inc(m_pv.sem, 1)

                for g in range(MEM_HEADS):
                    base, j = (g % 2) * HD, g // 2
                    for t in range(T):
                        ins = pe.matmul(ps[:, g, 256 * t:256 * t + 256], qmT[base:base + HD, j, t * P:(t + 1) * P],
                                        kmT[base:base + HD, j, :], start=True, stop=True)
                    ins.then_inc(m_scores.sem, 1)
                for g in range(MEM_HEADS + 1):
                    if g < MEM_HEADS:
                        mem_transpose_p(g)
                    if g >= 1:
                        mem_weigh_v(g - 1)
                pe.wait_ge(om_ready.sem, om_ready.at(layer, 1))
                transpose_small(om, 7, omT_ps)
                pe.wait_ge(om_lo.sem, om_lo.at(layer, 1))
                with_unit(layer, U_MO, 2, D, lambda t, c: ps[:, 2 * c + t, :], 0, True, True)

                build_of_x(layer, B_FFN)

                def gate_up(pair, b, lo_of=None):
                    s = (U_FFN + b) % RING
                    pe.wait_ge(lo_done[s].sem, lo_done[s].at(layer, fill(U_FFN + b, pair) + 1))
                    if not_first(pair):
                        pe.wait_ge(glu.sem, glu.at(layer, pair * 2 + b - 1))
                    for j in range(2):
                        acc = ps[:, b, 256 * j:256 * j + 256]
                        for k in range(KC):
                            a = (2 * k + j) * P
                            pe.matmul(acc, whi[s][:, a:a + P], thi[:, k, :], start=(k == 0), stop=False)
                            pe.matmul(acc, whi[s][:, a:a + P], tlo[:, k, :], start=False, stop=False)
                            ins = pe.matmul(acc, wlo[s][:, a:a + P], thi[:, k, :], start=False, stop=(k == KC - 1))
                    ins.then_inc(used[s].sem, 1)

                def down(pair, b, first=False, last=False):
                    s = (U_FFN + 2) % RING
                    if b == 0:
                        pe.wait_ge(lo_done[s].sem, lo_done[s].at(layer, fill(U_FFN + 2, pair) + 1))
                    pe.wait_ge(act_lo.sem, act_lo.at(layer, pair * 2 + b + 1))
                    for c in range(2):
                        for t in range(T):
                            a = b * D + c * 512
                            acc = ps[:, 4 + 2 * c + t, :]
                            tok = slice(t * P, (t + 1) * P)
                            pe.matmul(acc, ahi[b][:, tok], whi[s][:, a:a + 512], start=first, stop=False)
                            pe.matmul(acc, ahi[b][:, tok], wlo[s][:, a:a + 512], start=False, stop=False)
                            ins = pe.matmul(acc, alo[b][:, tok], whi[s][:, a:a + 512], start=False, stop=last)
                    ins.then_inc((down_even.sem, used[s].sem)[b], 1)

                pe.wait_ge(t_lo.sem, t_lo.at(layer, 2 * B_FFN + 2))
                gate_up(0, 0)
                if layer == 0:
                    pe.wait_ge(s_ones.sem, 1)
                pe.wait_ge(diag_ready.sem, diag_ready.at(layer, 1))
                pe.matmul(ps[:, 2, 0:SEQ], ones[:], rs_diag, start=True, stop=True).then_inc(row_ps.sem, 1)
                gate_up(0, 1)
                down(0, 0, first=True)
                with pe.Fori(1, PAIRS) as i:
                    gate_up(i, 0)
                    down(i - 1, 1)
                    gate_up(i, 1)
                    down(i, 0)
                down(PAIRS - 1, 1, last=True)


MEM_TRANSPOSE_AT = (1, 3)
MEM_BUILD_AT = (2, 4)
MEM_PIECES_FROM = 6
HALF_AT = LAST_OF[7] + 4
XN_OF = {B_MIX: 0, B_HEADS: 2, B_CROSS: 4, B_FFN: 6}
N_SMALL = 3 * HD + 4 * 32
N_TABLE = 7 * P + NFREQ


def not_first(pair):
    return not isinstance(pair, int) or pair > 0


def lam_init(layer):
    return 0.8 - 0.6 * math.exp(-0.3 * layer)


def split_two_pi():
    parts, left = [], 2.0 * math.pi
    for bits in (5, 13, 21):
        c = math.floor(left * 2.0 ** bits) / 2.0 ** bits
        parts.append(c)
        left -= c
    return parts + [left]


TWO_PI = split_two_pi()


def mask_table():
    q = np.arange(SEQ)[:, None]
    k = np.arange(SEQ)[None, :]
    d = q - k
    count = [(d >= 0).astype(np.float64),
             (((d >= 0) & (d <= 128)).astype(np.float64) + ((d >= 0) & (d % 4 == 0)) + ((d >= 0) & (d % 16 == 0)))]
    table = np.full((P, 2, 3 * P), NEG, np.float32)
    for kind, c in enumerate(count):
        m = np.where(c > 0, np.log(np.maximum(c, 1.0)) * math.sqrt(HD), NEG).astype(np.float32)
        table[:, kind, 0:P] = m[0:P, 0:P]
        table[:, kind, P:3 * P] = m[P:2 * P, :]
    return table


def freq_table():
    parts = [THETA ** (-np.arange(half, dtype=np.float32) / np.float32(half)) for half in (4, 8)]
    return np.concatenate(parts).astype(np.float32)[None, :]


def const_table():
    return np.concatenate([np.eye(P, dtype=np.float32), mask_table().reshape(P, -1),
                           np.tile(freq_table(), (P, 1))], axis=1)


WEIGHTS = ("w_in", "w_out", "w_mq", "w_mkv", "w_mo", "w_gate_up", "w_down")
GAINS = ("norm_mix", "norm_cross", "norm_mem", "norm_ffn")
SMALL = ("subln_diff", "qn_mem", "kn_mem", "lambda_q1", "lambda_k1", "lambda_q2", "lambda_k2")


def kernel(**inputs):
    import concourse.bacc as bacc
    from concourse.bass_utils import run_bass_kernel_spmd

    nc = bacc.Bacc("TRN2", target_bir_lowering=False, num_devices=1)
    arrays = {}

    def put(name, a):
        a = np.ascontiguousarray(a)
        arrays[f"in_{name}"] = a
        return nc.dram_tensor(f"in_{name}", a.shape, mybir.dt.from_np(a.dtype), kind="ExternalInput").ap()

    def tiled(kind):
        parts = [np.tile(np.asarray(inputs[f"{kind}_{n}"]), (1, reps))
                 for n, reps in (("diff", 2 * DIFF), ("dil", DIL), ("moba", MOBA))]
        return np.concatenate(parts, axis=1)

    x = put("x", inputs["x"])
    mem = put("mem", inputs["mem"])
    positions = put("positions", inputs["positions"])
    w = {n: put(n, inputs[n]) for n in WEIGHTS}
    gains = {n: put(n, inputs[n]) for n in GAINS}
    gains["q_gain"] = put("q_gain", tiled("qn"))
    gains["k_gain"] = put("k_gain", tiled("kn"))
    gains["small"] = put("small", np.concatenate([np.asarray(inputs[n]) for n in SMALL], axis=1).reshape(1, -1))
    consts = {"table": put("table", const_table())}
    out = nc.dram_tensor("out", (1, SEQ, D), F32, kind="ExternalOutput").ap()
    trunk(nc, x, mem, positions, w, gains, consts, out)
    r = run_bass_kernel_spmd(nc, [arrays], core_ids=[0])
    return r.results[0]["out"]
```

```python
import math
from contextlib import ExitStack

import numpy as np

import concourse.bass as bass
from concourse import mybir

P = 128
F32 = mybir.dt.float32
F32R = mybir.dt.float32r
I32 = mybir.dt.int32
ALU = mybir.AluOpType
ACT = mybir.ActivationFunctionType
AX_X = mybir.AxisListType.X

D = 1024
SEQ = 256
DEPTH = 2
HD = 64
HEADS = 16
DIFF, DIL, MOBA = 4, 6, 6
MEM_HEADS = 4
MEM_W = MEM_HEADS * HD
FF = 2816
EPS = 1e-6
THETA = 500000.0

T = SEQ // P
KC = D // P
HALF = KC // 2
NCHUNK = 3 * D // 512
FCH = FF // P
PAIRS = FCH // 2

RING = 3
U_QKV, U_MKV, U_OUT, U_MQ, U_MO, U_FFN = 0, 12, 14, 18, 20, 21
UNITS = U_FFN + 3 * PAIRS
FILLS = UNITS // RING
assert UNITS % RING == 0 and U_FFN % RING == 0

X_MIX, X_CROSS, X_FFN = range(3)
X_BUILDS = 3
B_MEM, B_HEADS = range(2)
BUILDS = 2

SOFTMAXES = [(h, (h % 2) * HD + a * 32, 32) for h in range(DIFF) for a in range(2)]
SOFTMAXES += [(h, (h % 2) * HD, HD) for h in range(DIFF, HEADS)]
NS = len(SOFTMAXES)
LAST_OF = [max(n for n in range(NS) if SOFTMAXES[n][0] == h) for h in range(HEADS)]

NEG = -1.0e30
GROUPS = 2 * DIFF + DIL + MOBA
ROT = ((2 * DIFF, 32, 4, 0, 0), (DIL + MOBA, 64, 8, DIFF * HD, 4))
NFREQ = 12


class Signal:

    def __init__(self, sem, per_layer):
        self.sem, self.per_layer = sem, per_layer

    def at(self, layer, k):
        return layer * self.per_layer + k


def trunk(nc, x, mem, positions, w, gains, consts, out):
    with ExitStack() as ctx:
        def sb(name, shape, dt=F32):
            return ctx.enter_context(nc.sbuf_tensor(name, shape, dt))

        def signal(name, per_layer=1):
            return Signal(ctx.enter_context(nc.semaphore(name)), per_layer)

        raw = [sb(f"raw{s}", [P, 2048]) for s in range(RING)]
        whi = [sb(f"whi{s}", [P, 2048], F32R) for s in range(RING)]
        wlo = [sb(f"wlo{s}", [P, 2048], F32R) for s in range(RING)]
        xs = sb("xs", [P, T, D])
        xn = sb("xn", [P, T, D])
        thi = sb("thi", [P, KC, SEQ], F32R)
        tlo = sb("tlo", [P, KC, SEQ], F32R)
        qkv = sb("qkv", [P, T, 3 * D])
        qT = sb("qT", [P, KC, SEQ])
        kT = sb("kT", [P, KC, SEQ])
        sq = sb("sq", [P, T * D])
        prob = [sq[:, 512 * b:512 * b + 512] for b in range(4)]
        probT_all = sb("probT", [P, 3 * 512])
        probT = [probT_all[:, 512 * b:512 * b + 512] for b in range(3)]
        kvm = sb("kvm", [P, T, 2 * MEM_W])
        kmT = sb("kmT", [P, 2, SEQ])
        qm = sb("qm", [P, T, MEM_W])
        qmT = sb("qmT", [P, 2, SEQ])
        om = sb("om", [P, T, MEM_W])
        ahi = [sb(f"ahi{b}", [P, SEQ], F32R) for b in range(2)]
        alo = [sb(f"alo{b}", [P, SEQ], F32R) for b in range(2)]
        gate_n = [qkv[:, 0, 256 * b:256 * b + 256] for b in range(2)]
        silu_g = [qkv[:, 0, 512 + 256 * b:768 + 256 * b] for b in range(2)]
        act_f = [qkv[:, 0, 1024 + 256 * b:1280 + 256 * b] for b in range(2)]
        rs_diag = qkv[:, 1, 0:SEQ]
        rs_row = qkv[:, 1, SEQ:2 * SEQ]
        m_probT = [qkv[:, 0, 512 * i:512 * i + 512] for i in range(4)]
        rope, rope_dve = (probT_all[:, 768 * e:768 * e + 768].rearrange("p (i n) -> p i n", i=4) for e in range(2))
        g_mix = sb("g_mix", [P, D])
        g_mem, g_cross, g_ffn = sb("g_mem", [P, D]), sb("g_cross", [P, D]), sb("g_ffn", [P, D])
        g_qk = [sb("g_q", [P, D]), sb("g_k", [P, D])]
        ident_sb = sb("ident_sb", [P, P])
        ident = ident_sb[:]
        table = sb("table", [P, N_TABLE])
        masks = table[:, 0:6 * P].rearrange("p (c n) -> p c n", c=2)
        freqs = sb("freqs", [P, NFREQ])
        small = sb("small", [P, DEPTH, N_SMALL])
        g_sub, g_qm, g_km = (small[:, :, HD * i:HD * i + HD] for i in range(3))
        lam_in = [small[:, :, 3 * HD + 32 * i:3 * HD + 32 * i + 32] for i in range(4)]
        ones = sb("ones", [P, P])
        lam_dot = sb("lam_dot", [P, 2, DEPTH])
        lam_exp = sb("lam_exp", [P, 2, DEPTH])
        neg_lam = sb("neg_lam", [P, DEPTH])
        pos_i = sb("pos_i", [P, T], I32)
        pos_f = sb("pos_f", [P, T])
        ang = sb("ang", [P, 2, T, NFREQ])
        turns = sb("turns", [P, 2, T, NFREQ])
        cs = sb("cs", [P, 2, T, NFREQ])
        ss = sb("ss", [P, T])
        rs = sb("rs", [P, 2, T])
        mem_ss = sb("mem_ss", [P, T])
        mem_r = sb("mem_r", [P, T])
        g32 = sb("g32", [P, T, 32])
        nv, nh, ny, nt = (sb(n, [P, 40]) for n in ("nv", "nh", "ny", "nt"))
        mx = sb("mx", [P, NS, T])
        nm = sb("nm", [P, NS, T])
        zs = sb("zs", [P, NS, T])
        rz = sb("rz", [P, HEADS, T])
        lam_z = sb("lam_z", [P, 2, T])
        var_x = sb("var_x", [P, T])
        qscale = sb("qscale", [P, T, MEM_HEADS])

        ps = ctx.enter_context(nc.psum_tensor("ps", [P, 8, 512], F32))

        def banks(a, b):
            return ps[:, a:b, :].rearrange("p b n -> p (b n)")

        def half_of(a, h):
            return a[:, 4 * h:4 * h + 4, :].rearrange("p k n -> p (k n)")

        def quarter(a, q):
            t, h = divmod(q, 2)
            return a[:, 4 * h:4 * h + 4, t * P:(t + 1) * P]

        def bank_as_chunks(b):
            return ps[:, b, :].rearrange("p (k n) -> p k n", k=4)

        s_x = [signal(f"x_loaded{t}") for t in range(T)]
        s_ident = signal("identity_loaded")
        s_freq = signal("frequencies_loaded")
        s_table = signal("table_loaded")
        s_small = signal("small_gains_loaded")
        s_pos = signal("positions_loaded")
        s_gmix0 = signal("first_gain_loaded")
        s_ones = signal("ones_set")
        s_lam = signal("lambda_ready")
        s_cs = signal("angles_ready")
        s_sin = signal("sines_ready")
        s_memss = signal("mem_squares")
        s_memr = signal("mem_roots")
        s_out = signal("stored")
        s_gain = signal("gains_loaded", 16 * 3)
        s_gain_x = signal("later_gains_loaded", 16 * 2)
        s_gmix = signal("mix_gain_loaded", 16)
        mem_in = signal("mem_in", 16)
        raw_in = [signal(f"raw_in{s}") for s in range(RING)]
        hi_done = [signal(f"hi_done{s}", FILLS) for s in range(RING)]
        lo_done = [signal(f"lo_done{s}", FILLS) for s in range(RING)]
        used = [signal(f"used{s}", FILLS) for s in range(RING)]
        t0_done = signal("first_tile_summed", 3)
        x_new = signal("x_new", 3 * T)
        ss_done = signal("ss_done", 3)
        rs_ready = signal("rs_ready", 2)
        xn_ready = signal("xn_ready", 4 * X_BUILDS)
        t_ps = signal("t_ps", 4 * X_BUILDS)
        t_hi = signal("t_hi", 4 * X_BUILDS)
        t_lo = signal("t_lo", 4 * X_BUILDS)
        xm_scaled = signal("xm_scaled", 1)
        xm_ready = signal("xm_ready", 1)
        heads_ready = signal("heads_ready", 2)
        h_ps = signal("h_ps", 2 * BUILDS)
        h_hi = signal("h_hi", 2 * BUILDS)
        h_lo = signal("h_lo", 2 * BUILDS)
        proj_out = signal("proj_out", NCHUNK)
        mkv_out = signal("mkv_out", 1)
        km_ready = signal("km_ready", 1)
        mq_sum = signal("mq_sum", 1)
        mq_out = signal("mq_out", T)
        sqr = signal("sqr", 4)
        scaled = signal("scaled", 2)
        roped = signal("roped", 2)
        roped_dve = signal("roped_dve", 1)
        qkT_ps = signal("qkT_ps", 4)
        qkT_act = signal("qkT_act", 2)
        qkT_dve = signal("qkT_dve", 2)
        scores = signal("scores", NS)
        masked = signal("masked", NS)
        nmax = signal("nmax", NS)
        probs = signal("probs", NS)
        combined = signal("combined", DIFF)
        pT_ps = signal("pT_ps", HEADS)
        pT_act = signal("pT_act", HEADS // 2)
        pT_dve = signal("pT_dve", HEADS // 2)
        pv = signal("pv", HEADS)
        o_read = signal("o_read", 1)
        kmT_ps, kmT_out = signal("kmT_ps", 1), signal("kmT_out", 1)
        qmT_ps, qmT_out = signal("qmT_ps", T), signal("qmT_out", T)
        m_scores, m_max, m_probs = (signal(n, 4) for n in ("m_scores", "m_max", "m_probs"))
        m_pT_act, m_pT_dve = signal("m_pT_act", 2), signal("m_pT_dve", 2)
        m_pT_ps, m_pv = (signal(n, 4) for n in ("m_pT_ps", "m_pv"))
        om_ready, omT_ps, om_hi, om_lo = (signal(n, T) for n in ("om_ready", "omT_ps", "om_hi", "om_lo"))
        diag_ready, row_ps, row_out = (signal(n, 1) for n in ("diag_ready", "row_ps", "row_out"))
        gate_done = signal("gate_done", FCH)
        silu_done = signal("silu_done", FCH)
        glu = signal("glu", FCH)
        act_hi = signal("act_hi", FCH)
        act_lo = signal("act_lo", FCH)
        down_even = signal("down_even", PAIRS)
        dve_chain = signal("dve_chain")
        pool_chain = signal("pool_chain")

        def rotary(y, rot, scratch):
            groups, width, half, col, tab = rot
            v = y[:, :, col:col + groups * width].rearrange("p t (g w) -> p t g w", w=width)
            x1, x2 = v[:, :, :, 0:half], v[:, :, :, half:2 * half]
            size = T * groups * half
            m = [scratch[:, i, 0:size].rearrange("p (t g f) -> p t g f", t=T, f=half) for i in range(4)]
            cos, sin = (cs[:, i, :, tab:tab + half].unsqueeze(2).to_broadcast((P, T, groups, half)) for i in range(2))
            return x1, x2, ((x1, cos), (x2, sin), (x2, cos), (x1, sin)), m

        def dmas_before_ffn(s, upto=U_FFN):
            return sum(1 for u in range(upto) if u % RING == s)

        per_layer_dmas = [dmas_before_ffn(s) + PAIRS * (2 if s < 2 else 1) for s in range(RING)]

        def raw_level(layer, u, pair=0):
            s = u % RING
            if u < U_FFN:
                n = dmas_before_ffn(s, u + 1)
            else:
                n = dmas_before_ffn(s) + (pair + 1) * (2 if s < 2 else 1)
            return 16 * (layer * per_layer_dmas[s] + n)

        def fill(u, pair=0):
            return u // RING + pair

        def used_before(layer, u, pair=0):
            return used[u % RING].at(layer, fill(u, pair))

        def used_after(layer, u, pair=0):
            return used[u % RING].at(layer, fill(u, pair) + 1)

        block = ctx.enter_context(nc.Block())

        @block.sync
        def _(sp):
            x_in = x.rearrange("b (t p) d -> p (b t) d", p=P)
            for t in range(T):
                sp.dma_start(xs[:, t, :], x_in[:, t, :]).then_inc(s_x[t].sem, 16)

            def load(layer, u, src, pair=0):
                s = u % RING
                if layer or u >= RING:
                    sp.wait_ge(hi_done[s].sem, hi_done[s].at(layer, fill(u, pair)))
                    sp.wait_ge(lo_done[s].sem, lo_done[s].at(layer, fill(u, pair)))
                for dst, part in src:
                    sp.dma_start(dst, part).then_inc(raw_in[s].sem, 16)

            def view(u, k):
                return raw[u % RING][:].rearrange("p (k n) -> p k n", k=k)

            for layer in range(DEPTH):
                w_in = w["w_in"][layer].rearrange("(k p) n -> p k n", p=P)
                w_mkv = w["w_mkv"][layer].rearrange("(k p) n -> p k n", p=P)
                w_out = w["w_out"][layer].rearrange("(k p) n -> p k n", p=P)
                w_mq = w["w_mq"][layer].rearrange("(k p) n -> p k n", p=P)
                w_mo = w["w_mo"][layer].rearrange("(k p) n -> p k n", p=P)
                w_gu = w["w_gate_up"][layer].rearrange("(k p) (j n) -> p k j n", p=P, j=2)
                w_down = w["w_down"][layer].rearrange("(k p) n -> p k n", p=P)
                for c in range(NCHUNK):
                    for h in range(2):
                        u = U_QKV + 2 * c + h
                        load(layer, u, [(view(u, 4), w_in[:, 4 * h:4 * h + 4, 512 * c:512 * c + 512])])
                for h in range(2):
                    load(layer, U_MKV + h, [(view(U_MKV + h, 4), w_mkv[:, 4 * h:4 * h + 4, :])])
                for h in range(2):
                    for c in range(2):
                        u = U_OUT + 2 * h + c
                        load(layer, u, [(view(u, 4), w_out[:, 4 * h:4 * h + 4, 512 * c:512 * c + 512])])
                for h in range(2):
                    u = U_MQ + h
                    load(layer, u, [(raw[u % RING][:, 0:1024].rearrange("p (k n) -> p k n", k=4),
                                     w_mq[:, 4 * h:4 * h + 4, :])])
                load(layer, U_MO, [(view(U_MO, 2), w_mo)])
                with sp.Fori(0, PAIRS) as i:
                    for b in range(2):
                        u = U_FFN + b
                        dst = raw[u % RING][:].rearrange("p (k j n) -> p k j n", k=KC, j=2)
                        load(layer, u, [(dst[:, :, j, :], w_gu[:, :, j, bass.ds(i * 256 + b * 128, 128)])
                                        for j in range(2)], i)
                    u = U_FFN + 2
                    load(layer, u, [(view(u, 2), w_down[:, bass.ds(i * 2, 2), :])], i)
            for t in range(T):
                sp.wait_ge(x_new.sem, x_new.at(DEPTH - 1, 2 * T + t + 1))
                sp.dma_start(out.rearrange("b (t p) d -> p (b t) d", p=P)[:, t, :], xs[:, t, :]).then_inc(s_out.sem, 16)
            sp.wait_ge(s_out.sem, 16 * T)

        @block.gpsimd
        def _(pool):
            mem_rows = mem.rearrange("b (t p) d -> p (b t) d", p=P)
            with nc.allow_non_contiguous_dma(reason="256 positions"):
                pool.dma_start(pos_i[:], positions.rearrange("b (t p) -> p (b t)", p=P)).then_inc(s_pos.sem, 16)

            links = [0]

            def link(ins):
                links[0] += 1
                ins.then_inc(pool_chain.sem, 1)
                pool.wait_ge(pool_chain.sem, links[0])

            def angles():
                pool.wait_ge(s_pos.sem, 16)
                pool.wait_ge(s_freq.sem, 16)
                link(pool.tensor_copy(pos_f[:], pos_i[:]))
                for t in range(T):
                    for i in range(2):
                        ins = pool.tensor_scalar(ang[:, i, t, :], freqs[:], pos_f[:, t:t + 1], None, ALU.mult)
                link(ins)
                magic = 12582912.0
                for i, quarter in ((0, 0.25), (1, 0.0)):
                    ins = pool.tensor_scalar(turns[:, i], ang[:, i], 1.0 / (2.0 * math.pi), quarter, ALU.mult, ALU.add)
                link(ins)
                link(pool.tensor_scalar(turns[:], turns[:], magic, None, ALU.add))
                link(pool.tensor_scalar(turns[:], turns[:], -magic, None, ALU.add))
                flat, size = ang[:].rearrange("p i t f -> p (i t f)"), 2 * T * NFREQ
                for n, part in enumerate(TWO_PI):
                    ins = pool.tensor_scalar(rope[:, n, 0:size], turns[:].rearrange("p i t f -> p (i t f)"),
                                             -part, None, ALU.mult)
                link(ins)
                for n in range(len(TWO_PI)):
                    link(pool.tensor_tensor(flat, flat, rope[:, n, 0:size], ALU.add))
                link(pool.tensor_scalar(ang[:, 0], ang[:, 0], math.pi / 2, None, ALU.add))
                pool.tensor_scalar(ang[:], ang[:], 3.1415925, -3.1415925, ALU.min, ALU.max).then_inc(s_cs.sem, 1)

            angles()

            def split_lo(layer, u, n=2048):
                s = u % RING
                pool.wait_ge(hi_done[s].sem, hi_done[s].at(layer, fill(u) + 1))
                pool.tensor_tensor(wlo[s][:, 0:n], raw[s][:, 0:n], whi[s][:, 0:n].bitcast(F32), ALU.subtract)\
                    .then_inc(lo_done[s].sem, 1)

            for layer in range(DEPTH):
                if layer:
                    pool.wait_ge(xn_ready.sem, xn_ready.at(layer - 1, 4 * X_FFN + 4))
                pool.wait_ge(t_ps.sem, t_ps.at(layer, 4 * X_MIX + 4))
                pool.dma_start(xn[:], mem_rows).then_inc(mem_in.sem, 16)
                for tile, name in ((g_qk[0], "q_gain"), (g_mem, "norm_mem"), (g_qk[1], "k_gain")):
                    pool.dma_start(tile[:], gains[name][layer:layer + 1, :].to_broadcast((P, D)))\
                        .then_inc(s_gain.sem, 16)
                pool.wait_ge(mem_in.sem, mem_in.at(layer, 16))
                pool.wait_ge(s_gain.sem, s_gain.at(layer, 16 * 3))
                pool.wait_ge(xm_scaled.sem, xm_scaled.at(layer, 1))
                pool.tensor_tensor(xn[:], xn[:], g_mem[:].unsqueeze(1).to_broadcast((P, T, D)), ALU.mult)\
                    .then_inc(xm_ready.sem, 1)
                for part in range(2):
                    y = qkv[:, :, part * D:(part + 1) * D]
                    if part == 1:
                        split_lo(layer, POOL_LO[0])
                    pool.wait_ge(scaled.sem, scaled.at(layer, part + 1))
                    if layer == 0 and part == 0:
                        pool.wait_ge(s_sin.sem, 1)
                    own = ROT if part == 0 else ROT[:1]
                    cols = sum(groups * width for groups, width, *_ in own)
                    link(pool.tensor_tensor(y[:, :, 0:cols], y[:, :, 0:cols], g_qk[part][:, 0:cols].unsqueeze(1)
                                            .to_broadcast((P, T, cols)), ALU.mult))
                    for n, rot in enumerate(own):
                        x1, x2, factors, m = rotary(y, rot, rope)
                        for i, (a, b) in enumerate(factors):
                            ins = pool.tensor_tensor(m[i], a, b, ALU.mult)
                        link(ins)
                        pool.tensor_tensor(x1, m[0], m[1], ALU.subtract)
                        ins = pool.tensor_tensor(x2, m[2], m[3], ALU.add)
                        if n < len(own) - 1:
                            link(ins)
                        else:
                            ins.then_inc(roped.sem, 1)
                for tile, name in ((g_cross, "norm_cross"), (g_ffn, "norm_ffn")):
                    pool.dma_start(tile[:], gains[name][layer:layer + 1, :].to_broadcast((P, D)))\
                        .then_inc(s_gain_x.sem, 16)
                if layer + 1 < DEPTH:
                    pool.dma_start(g_mix[:], gains["norm_mix"][layer + 1:layer + 2, :].to_broadcast((P, D)))\
                        .then_inc(s_gmix.sem, 16)
                for u in POOL_LO[1:]:
                    split_lo(layer, u)
                for u in range(U_OUT, U_OUT + 4):
                    split_lo(layer, u)
                for u in (U_MQ, U_MQ + 1):
                    split_lo(layer, u, 4 * MEM_W)
                for u in (U_MO, U_FFN, U_FFN + 1, U_FFN + 2):
                    split_lo(layer, u)
                if layer + 1 < DEPTH:
                    for u in range(2):
                        split_lo(layer + 1, u)

        @block.scalar
        def _(act):
            act.dma_start(g_mix[:], gains["norm_mix"][0:1, :].to_broadcast((P, D))).then_inc(s_gmix0.sem, 16)
            act.dma_start(ident, consts["ident"]).then_inc(s_ident.sem, 16)
            act.dma_start(freqs[:], consts["freqs"]).then_inc(s_freq.sem, 16)

            def split_hi(layer, u, pair=0, n=2048):
                s = u % RING
                act.wait_ge(raw_in[s].sem, raw_level(layer, u, pair))
                if layer or u >= RING:
                    act.wait_ge(used[s].sem, used_before(layer, u, pair))
                act.activation(whi[s][:, 0:n], raw[s][:, 0:n], ACT.Copy).then_inc(hi_done[s].sem, 1)

            def x_hi(layer, b, q):
                act.wait_ge(t_ps.sem, t_ps.at(layer, 4 * b + q + 1))
                act.activation(quarter(thi, q), bank_as_chunks(X_BANKS[b][q]), ACT.Copy).then_inc(t_hi.sem, 1)

            def half_hi(layer, b, h):
                act.wait_ge(h_ps.sem, h_ps.at(layer, 2 * b + h + 1))
                bank = H_BANKS[b][h]
                act.activation(half_of(thi, h), banks(bank, bank + 2), ACT.Copy).then_inc(h_hi.sem, 1)

            def squares_of_x(layer, n, t):
                if layer == 0 and n == 0:
                    act.wait_ge(s_x[t].sem, 16)
                else:
                    act.wait_ge(x_new.sem, x_new.at(layer, 2 * n - 1 + t))
                ins = act.activation(sq[:, t * D:(t + 1) * D], xs[:, t, :], ACT.Square,
                                     accum_out=ss[:, t:t + 1])
                if t == T - 1:
                    ins.then_inc(ss_done.sem, 1)

            for layer in range(DEPTH):
                for t in range(T):
                    if layer == 0 and t == 1:
                        split_hi(0, 0)
                        act.dma_start(table[:], consts["table"]).then_inc(s_table.sem, 16)
                        act.dma_start(small[:].rearrange("p l n -> p (l n)"),
                                      gains["small"].to_broadcast((P, DEPTH * N_SMALL))).then_inc(s_small.sem, 16)
                    for q in (2 * t, 2 * t + 1):
                        x_hi(layer, X_MIX, q)
                if layer == 0:
                    split_hi(0, 1)
                for t in range(T):
                    squares_of_x(layer, 0, t)
                split_hi(layer, 2)
                def chunk_out(c):
                    act.wait_ge(used[(2 * c + 1) % RING].sem, used_after(layer, 2 * c + 1))
                    if c == 0:
                        act.wait_ge(rs_ready.sem, rs_ready.at(layer, 1))
                    for t in range(T):
                        ins = act.activation(qkv[:, t, 512 * c:512 * c + 512], ps[:, 4 + 2 * (c % 2) + t, :],
                                             ACT.Copy, scale=rs[:, 0, t:t + 1])
                    ins.then_inc(proj_out.sem, 1)

                for c in range(NCHUNK - 1):
                    split_hi(layer, 2 * c + 3)
                    if layer == 0 and c == 0:
                        act.wait_ge(mem_in.sem, 16)
                        act.wait_ge(ss_done.sem, 1)
                        for t in range(T):
                            ins = act.activation(sq[:, t * D:(t + 1) * D], xn[:, t, :], ACT.Square,
                                                 accum_out=mem_ss[:, t:t + 1])
                        ins.then_inc(s_memss.sem, 1)
                        act.wait_ge(s_memss.sem, 1)
                    chunk_out(c)
                    if c < 4:
                        act.wait_ge(proj_out.sem, proj_out.at(layer, c + 1))
                        if c >= 2:
                            act.wait_ge(scaled.sem, scaled.at(layer, 1))
                        act.activation(sq[:].rearrange("p (t n) -> p t n", t=T)[:, :, 512 * (c % 2):512 * (c % 2) + 512],
                                       qkv[:, :, 512 * c:512 * c + 512], ACT.Square).then_inc(sqr.sem, 1)
                    split_hi(layer, 2 * c + 4)
                    if c == 1:
                        act.wait_ge(mem_in.sem, mem_in.at(layer, 16))
                        if layer == 0:
                            act.wait_ge(s_memr.sem, 1)
                        for t in range(T):
                            ins = act.activation(xn[:, t, :], xn[:, t, :], ACT.Copy, scale=mem_r[:, t:t + 1])
                        ins.then_inc(xm_scaled.sem, 1)
                    if layer == 0 and c == 0:
                        act.wait_ge(s_cs.sem, 1)
                        act.activation(cs[:], ang[:], ACT.Sin).then_inc(s_sin.sem, 1)
                        act.wait_ge(s_lam.sem, 1)
                        act.activation(lam_exp[:], lam_dot[:], ACT.Exp).then_inc(s_lam.sem, 1)
                for n, dst in enumerate((qT, kT)):
                    act.wait_ge(qkT_ps.sem, qkT_ps.at(layer, 2 * n + 1))
                    act.activation(half_of(dst, 0), banks(0, 2), ACT.Copy).then_inc(qkT_act.sem, 1)

                def exps(n):
                    _, _, rows = SOFTMAXES[n]
                    act.wait_ge(nmax.sem, nmax.at(layer, n + 1))
                    for t, (a, b) in enumerate(((0, P), (P, 3 * P))):
                        ins = act.activation(prob[n % 4][:, a:b], prob[n % 4][:, a:b], ACT.Exp,
                                             bias=nm[:, n, t:t + 1], scale=float(rows) ** -0.5,
                                             accum_out=zs[:, n, t:t + 1])
                    ins.then_inc(probs.sem, 1)

                def probT_out(m):
                    act.wait_ge(pT_ps.sem, pT_ps.at(layer, m + 1))
                    if m >= 3:
                        act.wait_ge(pv.sem, pv.at(layer, m - 2))
                    act.activation(probT[m % 3][:, 0:384], ps[:, 2 + m % 2, 0:384], ACT.Copy)\
                        .then_inc(pT_act.sem, 1)

                for n in range(NS + T_LAG):
                    if n in MEM_AT:
                        half_hi(layer, B_MEM, MEM_AT.index(n))
                    if n < NS:
                        exps(n)
                    if n == V_OUT_AT:
                        chunk_out(NCHUNK - 1)
                    for m in range(0, HEADS, 2):
                        if LAST_OF[m] + T_LAG == n:
                            probT_out(m)
                    if n == NS:
                        act.wait_ge(used[(U_MKV + 1) % RING].sem, used_after(layer, U_MKV + 1))
                        act.activation(kvm[:], ps[:, 6:8, :], ACT.Copy).then_inc(mkv_out.sem, 1)
                    if n in (1, V_OUT_AT + 1):
                        split_hi(layer, 13 if n == 1 else 14)
                half_hi(layer, B_HEADS, 0)
                split_hi(layer, 15)
                split_hi(layer, 16)
                half_hi(layer, B_HEADS, 1)
                split_hi(layer, 17)
                split_hi(layer, 18, n=4 * MEM_W)
                act.wait_ge(kmT_ps.sem, kmT_ps.at(layer, 1))
                act.activation(kmT[:].rearrange("p j n -> p (j n)"), ps[:, 3, :], ACT.Copy)\
                    .then_inc(kmT_out.sem, 1)
                split_hi(layer, 19, n=4 * MEM_W)
                for q in range(2):
                    x_hi(layer, X_CROSS, q)
                squares_of_x(layer, 1, 0)
                split_hi(layer, 20)

                def query_out(t):
                    if t == 0:
                        act.wait_ge(mq_sum.sem, mq_sum.at(layer, 1))
                    else:
                        act.wait_ge(used[(U_MQ + 1) % RING].sem, used_after(layer, U_MQ + 1))
                    act.activation(qm[:, t, :], ps[:, 4 + t, 0:MEM_W], ACT.Copy).then_inc(mq_out.sem, 1)

                def queryT_out(t):
                    act.wait_ge(qmT_ps.sem, qmT_ps.at(layer, t + 1))
                    act.activation(qmT[:, :, t * P:(t + 1) * P], ps[:, 6 + t, 0:SEQ].rearrange("p (j n) -> p j n", j=2),
                                   ACT.Copy).then_inc(qmT_out.sem, 1)

                query_out(0)
                for q in range(2, 4):
                    x_hi(layer, X_CROSS, q)
                squares_of_x(layer, 1, 1)
                queryT_out(0)
                query_out(1)
                queryT_out(1)
                for i in range(4):
                    if i == 2:
                        for n in range(2):
                            act.wait_ge(m_pT_ps.sem, m_pT_ps.at(layer, n + 1))
                            act.activation(m_probT[n], ps[:, 4 + n, :], ACT.Copy).then_inc(m_pT_act.sem, 1)
                    t, j = divmod(i, 2)
                    act.wait_ge(m_max.sem, m_max.at(layer, i + 1))
                    for g in (j, j + 2):
                        a = 256 * (g // 2)
                        ins = act.activation(prob[i][:, a:a + 256], ps[:, i, a:a + 256], ACT.Exp,
                                             bias=nm[:, g, t:t + 1], scale=qscale[:, t, g:g + 1],
                                             accum_out=zs[:, g, t:t + 1])
                    ins.then_inc(m_probs.sem, 1)
                for t in range(T):
                    act.wait_ge(omT_ps.sem, omT_ps.at(layer, t + 1))
                    act.activation(thi[:, 0:2, t * P:(t + 1) * P],
                                   ps[:, 6 + t, SEQ:2 * SEQ].rearrange("p (j n) -> p j n", j=2), ACT.Copy)\
                        .then_inc(om_hi.sem, 1)
                    split_hi(layer, 21 + t)
                for q in range(4):
                    x_hi(layer, X_FFN, q)
                for t in range(T):
                    squares_of_x(layer, 2, t)

                def silu_step(pair, b):
                    act.wait_ge(gate_done.sem, gate_done.at(layer, pair * 2 + b + 1))
                    if not_first(pair):
                        act.wait_ge(glu.sem, glu.at(layer, pair * 2 + b - 1))
                    act.activation(silu_g[b], gate_n[b], ACT.Silu).then_inc(silu_done.sem, 1)

                split_hi(layer, U_FFN + 2)
                silu_step(0, 0)
                split_hi(layer, U_FFN, 1)
                silu_step(0, 1)
                split_hi(layer, U_FFN + 1, 1)
                with act.Fori(1, PAIRS - 1) as i:
                    silu_step(i, 0)
                    split_hi(layer, U_FFN, i + 1)
                    split_hi(layer, U_FFN + 2, i)
                    silu_step(i, 1)
                    split_hi(layer, U_FFN + 1, i + 1)
                silu_step(PAIRS - 1, 0)
                if layer + 1 < DEPTH:
                    split_hi(layer + 1, 0)
                split_hi(layer, U_FFN + 2, PAIRS - 1)
                silu_step(PAIRS - 1, 1)
                if layer + 1 < DEPTH:
                    split_hi(layer + 1, 1)

        @block.vector
        def _(dve):
            links = [0]

            def link(ins):
                links[0] += 1
                ins.then_inc(dve_chain.sem, 1)
                dve.wait_ge(dve_chain.sem, links[0])

            def split_lo(layer, u, pair=0):
                s = u % RING
                dve.wait_ge(hi_done[s].sem, hi_done[s].at(layer, fill(u, pair) + 1))
                dve.tensor_tensor(wlo[s][:], raw[s][:], whi[s][:].bitcast(F32), ALU.subtract)\
                   .then_inc(lo_done[s].sem, 1)

            def rsqrt(n):
                v, h, y, t = (a[:, 0:n] for a in (nv, nh, ny, nt))
                dve.tensor_scalar(h, v, -0.5, None, ALU.mult)
                link(dve.tensor_scalar(y.bitcast(I32), v.bitcast(I32), -0.5, 1597463007.0, ALU.mult, ALU.add))
                for _ in range(3):
                    link(dve.tensor_tensor(t, y, h, ALU.mult))
                    link(dve.tensor_tensor(t, t, y, ALU.mult))
                    link(dve.scalar_tensor_tensor(y, t, 1.5, y, ALU.add, ALU.mult))

            def mean_eps(dst, sums, width):
                link(dve.tensor_scalar(dst, sums, 1.0 / width, EPS, ALU.mult, ALU.add))

            def roots_of_x(layer, n, norm):
                dve.wait_ge(ss_done.sem, ss_done.at(layer, norm + 1))
                mean_eps(nv[:, 0:T], ss[:], D)
                rsqrt(T)
                dve.tensor_copy(rs[:, n, :], ny[:, 0:T]).then_inc(rs_ready.sem, 1)

            def gain_x(gain, q):
                t, h = divmod(q, 2)
                cols = slice(512 * h, 512 * h + 512)
                dve.tensor_tensor(xn[:, t, cols], xs[:, t, cols], gain[:, cols], ALU.mult).then_inc(xn_ready.sem, 1)

            def x_lo(layer, b, q):
                dve.wait_ge(t_hi.sem, t_hi.at(layer, 4 * b + q + 1))
                dve.tensor_tensor(quarter(tlo, q), bank_as_chunks(X_BANKS[b][q]), quarter(thi, q).bitcast(F32),
                                  ALU.subtract).then_inc(t_lo.sem, 1)

            def half_lo(layer, b, h):
                dve.wait_ge(h_hi.sem, h_hi.at(layer, 2 * b + h + 1))
                bank = H_BANKS[b][h]
                dve.tensor_tensor(half_of(tlo, h), banks(bank, bank + 2), half_of(thi, h).bitcast(F32), ALU.subtract)\
                   .then_inc(h_lo.sem, 1)

            def by_head(a, heads):
                return a.rearrange("p t (h d) -> p t h d", h=heads)

            def head_roots(y, squares, heads):
                link(dve.tensor_tensor(squares, y, y, ALU.mult))
                link(dve.tensor_reduce(nh[:, 0:T * heads], squares, AX_X, ALU.add))
                mean_eps(nv[:, 0:T * heads], nh[:, 0:T * heads], HD)
                rsqrt(T * heads)
                return ny[:, 0:T * heads].rearrange("p (t h) -> p t h", t=T)

            def per_head(r, heads):
                return r.unsqueeze(3).to_broadcast((P, T, heads, HD))

            def every_head(gain, heads):
                return gain.unsqueeze(1).unsqueeze(1).to_broadcast((P, T, heads, HD))

            def add_to_x(layer, stage, t, unit, bank, scale=None):
                if t == 0:
                    dve.wait_ge(t0_done.sem, t0_done.at(layer, stage + 1))
                else:
                    dve.wait_ge(used[unit[0] % RING].sem, used_after(layer, *unit))
                for c in range(2):
                    cols = slice(512 * c, 512 * c + 512)
                    if scale is None:
                        ins = dve.tensor_tensor(xs[:, t, cols], ps[:, bank(t, c), :], xs[:, t, cols], ALU.add)
                    else:
                        ins = dve.scalar_tensor_tensor(xs[:, t, cols], ps[:, bank(t, c), :], scale[:, t:t + 1],
                                                       xs[:, t, cols], ALU.mult, ALU.add)
                ins.then_inc(x_new.sem, 1)

            def gain_tile(layer, stage, t, gain):
                dve.wait_ge(x_new.sem, x_new.at(layer, 2 * stage + t + 1))
                for c in range(2):
                    gain_x(gain, 2 * t + c)

            def lambdas():
                dve.wait_ge(s_small.sem, 16)
                for i in range(2):
                    for l in range(DEPTH):
                        link(dve.tensor_tensor_reduce(nt[:, 0:32], lam_in[2 * i][:, l, :], lam_in[2 * i + 1][:, l, :],
                                                      1.0, 0.0, ALU.mult, ALU.add, lam_dot[:, i, l:l + 1]))
                for l in range(DEPTH):
                    ins = dve.tensor_scalar(g_sub[:, l, :], g_sub[:, l, :], 1.0 - lam_init(l), None, ALU.mult)
                    dve.tensor_tensor(g_km[:, l, :], g_km[:, l, :], g_qm[:, l, :], ALU.mult)
                ins = dve.memset(nt[:, 0:32], 0.0)
                ins.then_inc(s_lam.sem, 1)
                dve.wait_ge(s_lam.sem, 2)
                link(dve.tensor_tensor(neg_lam[:], lam_exp[:, 1, :], lam_exp[:, 0, :], ALU.subtract))
                for l in range(DEPTH):
                    ins = dve.tensor_scalar(neg_lam[:, l:l + 1], neg_lam[:, l:l + 1], -lam_init(l), None, ALU.add)
                link(ins)

            dve.memset(ones[:], 1.0).then_inc(s_ones.sem, 1)
            dve.wait_ge(s_gmix0.sem, 16)
            for t in range(T):
                dve.wait_ge(s_x[t].sem, 16)
                for c in range(2):
                    gain_x(g_mix, 2 * t + c)

            for layer in range(DEPTH):
                for q in range(0 if layer == 0 else 2, 4):
                    x_lo(layer, X_MIX, q)
                if layer == 0:
                    split_lo(0, 0)
                    split_lo(0, 1)
                roots_of_x(layer, 0, 0)
                split_lo(layer, 2)

                def reduce_squares(c):
                    h = c % 2
                    dve.wait_ge(sqr.sem, sqr.at(layer, c + 1))
                    link(dve.tensor_reduce(g32[:, :, 16 * h:16 * h + 16],
                                           sq[:].rearrange("p (t g w) -> p t g w", t=T, w=32)[:, :, 16 * h:16 * h + 16, :],
                                           AX_X, ALU.add))

                def scale_qk(part):
                    y = qkv[:, :, part * D:(part + 1) * D]
                    reduce_squares(2 * part + 1)
                    v = nv[:, 0:T * GROUPS].rearrange("p (t g) -> p t g", t=T)
                    dve.tensor_scalar(v[:, :, 0:8], g32[:, :, 0:8], 1.0 / 32, EPS, ALU.mult, ALU.add)
                    two = g32[:, :, 8:32].rearrange("p t (g w) -> p t g w", w=2)
                    link(dve.tensor_tensor(v[:, :, 8:20], two[:, :, :, 0], two[:, :, :, 1], ALU.add))
                    mean_eps(v[:, :, 8:20], v[:, :, 8:20], HD)
                    rsqrt(T * GROUPS)
                    r = ny[:, 0:T * GROUPS].rearrange("p (t g) -> p t g", t=T)
                    for n, (groups, width, _, col, _) in enumerate(ROT):
                        z = y[:, :, col:col + groups * width].rearrange("p t (g w) -> p t g w", w=width)
                        rg = r[:, :, 8 * n:8 * n + groups].unsqueeze(3).to_broadcast((P, T, groups, width))
                        ins = dve.tensor_tensor(z, z, rg, ALU.mult)
                    ins.then_inc(scaled.sem, 1)
                    if part == 1:
                        dve.wait_ge(s_gain.sem, s_gain.at(layer, 16 * 3))
                        dve.wait_ge(scaled.sem, scaled.at(layer, 2))
                        col = ROT[1][3]
                        link(dve.tensor_tensor(y[:, :, col:], y[:, :, col:], g_qk[1][:, col:].unsqueeze(1)
                                               .to_broadcast((P, T, D - col)), ALU.mult))
                        x1, x2, factors, m = rotary(y, ROT[1], rope_dve)
                        if layer == 0:
                            dve.wait_ge(s_sin.sem, 1)
                        for i, (a, b) in enumerate(factors):
                            ins = dve.tensor_tensor(m[i], a, b, ALU.mult)
                        link(ins)
                        dve.tensor_tensor(x1, m[0], m[1], ALU.subtract)
                        dve.tensor_tensor(x2, m[2], m[3], ALU.add).then_inc(roped_dve.sem, 1)

                for c in range(NCHUNK):
                    if 2 * c + 3 not in POOL_LO:
                        split_lo(layer, 2 * c + 3)
                    if c in (0, 2):
                        reduce_squares(c)
                    if c == 3:
                        scale_qk(1)
                    if c < NCHUNK - 1 and 2 * c + 4 not in POOL_LO:
                        split_lo(layer, 2 * c + 4)
                    if c == 1:
                        scale_qk(0)
                    if layer == 0 and c == 0:
                        lambdas()
                        dve.wait_ge(s_memss.sem, 1)
                        mean_eps(nv[:, 0:T], mem_ss[:], D)
                        rsqrt(T)
                        dve.tensor_copy(mem_r[:], ny[:, 0:T]).then_inc(s_memr.sem, 1)
                    if c == 4:
                        dve.wait_ge(qkT_ps.sem, qkT_ps.at(layer, 2))
                        dve.tensor_copy(half_of(qT, 1), banks(2, 4)).then_inc(qkT_dve.sem, 1)
                dve.wait_ge(qkT_ps.sem, qkT_ps.at(layer, 4))
                dve.tensor_copy(half_of(kT, 1), banks(2, 4)).then_inc(qkT_dve.sem, 1)

                def mask_max(n):
                    head, _, rows = SOFTMAXES[n]
                    kind = 1 if DIFF <= head < DIFF + DIL else 0
                    dve.wait_ge(scores.sem, scores.at(layer, n + 1))
                    if layer == n == 0:
                        dve.wait_ge(s_table.sem, 16)
                    if n >= 4:
                        dve.wait_ge(pT_ps.sem, pT_ps.at(layer, SOFTMAXES[n - 4][0] + 1))
                    for t, (a, b) in enumerate(((0, P), (P, 3 * P))):
                        ins = dve.tensor_tensor_reduce(prob[n % 4][:, a:b], ps[:, n % 2, a:b], masks[:, kind, a:b],
                                                       1.0, 3.0 * NEG, ALU.add, ALU.max, mx[:, n, t:t + 1])
                    ins.then_inc(masked.sem, 1)
                    dve.wait_ge(masked.sem, masked.at(layer, n + 1))
                    dve.tensor_scalar(nm[:, n, :], mx[:, n, :], -float(rows) ** -0.5, None, ALU.mult)\
                       .then_inc(nmax.sem, 1)

                def combine(h):
                    n = 2 * h
                    dve.wait_ge(probs.sem, probs.at(layer, n + 2))
                    link(dve.reciprocal(lam_z[:, 0, :], zs[:, n + 1, :]))
                    link(dve.scalar_tensor_tensor(lam_z[:, 1, :], lam_z[:, 0, :], neg_lam[:, layer:layer + 1],
                                                  zs[:, n, :], ALU.mult, ALU.mult))
                    p1, p2 = prob[n % 4], prob[(n + 1) % 4]
                    for t, (a, b) in enumerate(((0, P), (P, 3 * P))):
                        ins = dve.scalar_tensor_tensor(p1[:, a:b], p2[:, a:b], lam_z[:, 1, t:t + 1], p1[:, a:b],
                                                       ALU.mult, ALU.add)
                    ins.then_inc(combined.sem, 1)

                def probT_out(m):
                    dve.wait_ge(pT_ps.sem, pT_ps.at(layer, m + 1))
                    if m >= 3:
                        dve.wait_ge(pv.sem, pv.at(layer, m - 2))
                    dve.tensor_copy(probT[m % 3][:, 0:384], ps[:, 2 + m % 2, 0:384]).then_inc(pT_dve.sem, 1)

                def heads_out(half):
                    dve.wait_ge(pv.sem, pv.at(layer, 8 * half + 8))
                    dve.wait_ge(probs.sem, probs.at(layer, LAST_OF[8 * half + 7] + 1))
                    r = rz[:, 8 * half:8 * half + 8, :]
                    if half == 0:
                        dve.reciprocal(r[:, 0:4, :], zs[:, 0:8:2, :])
                        link(dve.reciprocal(r[:, 4:8, :], zs[:, 8:12, :]))
                    else:
                        link(dve.reciprocal(r, zs[:, 12:20, :]))
                    return dve.tensor_tensor(by_head(xn[:, :, 512 * half:512 * half + 512], 8), by_head(ps[:, 4:6, :], 8),
                                             per_head(r.rearrange("p h t -> p t h"), 8), ALU.mult)

                for n in range(NS + T_LAG + 1):
                    if n < NS:
                        mask_max(n)
                    if n in MEM_AT:
                        half_lo(layer, B_MEM, MEM_AT.index(n))
                    for h in range(HEADS):
                        if h < DIFF and LAST_OF[h] + 1 == n:
                            combine(h)
                        if h % 2 and LAST_OF[h] + T_LAG == n:
                            probT_out(h)
                    if n == HALF_AT:
                        heads_out(0).then_inc(o_read.sem, 1)
                    if n == HALF_AT + 1:
                        dve.wait_ge(o_read.sem, o_read.at(layer, 1))
                        y = by_head(xn[:, :, 0:DIFF * HD], DIFF)
                        r = head_roots(y, by_head(om[:], DIFF), DIFF)
                        link(dve.tensor_tensor(y, y, per_head(r, DIFF), ALU.mult))
                        dve.tensor_tensor(y, y, every_head(g_sub[:, layer, :], DIFF), ALU.mult)\
                           .then_inc(heads_ready.sem, 1)
                half_lo(layer, B_HEADS, 0)
                heads_out(1).then_inc(heads_ready.sem, 1)
                half_lo(layer, B_HEADS, 1)
                dve.wait_ge(mkv_out.sem, mkv_out.at(layer, 1))
                y = by_head(kvm[:, :, 0:MEM_W], MEM_HEADS)
                r = head_roots(y, by_head(om[:], MEM_HEADS), MEM_HEADS)
                link(dve.tensor_tensor(y, y, per_head(r, MEM_HEADS), ALU.mult))
                dve.tensor_tensor(y, y, every_head(g_km[:, layer, :], MEM_HEADS), ALU.mult).then_inc(km_ready.sem, 1)
                dve.wait_ge(s_gain_x.sem, s_gain_x.at(layer, 16 * 2))
                for t in range(T):
                    add_to_x(layer, 0, t, (U_OUT + 3,), lambda t, c: (6, 4)[c] + t)
                    gain_tile(layer, 0, t, g_cross)
                    for q in (2 * t, 2 * t + 1):
                        x_lo(layer, X_CROSS, q)

                dve.wait_ge(ss_done.sem, ss_done.at(layer, 2))
                link(dve.tensor_scalar(var_x[:], ss[:], EPS / D, EPS * EPS, ALU.mult, ALU.add))

                def q_scale(t):
                    dve.wait_ge(mq_out.sem, mq_out.at(layer, t + 1))
                    link(dve.tensor_tensor(om[:, t, :], qm[:, t, :], qm[:, t, :], ALU.mult))
                    link(dve.tensor_reduce(nh[:, 0:4], om[:, t, :].rearrange("p (h d) -> p h d", d=HD), AX_X, ALU.add))
                    link(dve.tensor_scalar(nv[:, 0:4], nh[:, 0:4], 1.0 / HD, var_x[:, t:t + 1], ALU.mult, ALU.add))
                    rsqrt(4)
                    link(dve.tensor_scalar(qscale[:, t, :], ny[:, 0:4], float(HD) ** -0.5, None, ALU.mult))

                def mem_max(i):
                    t, j = divmod(i, 2)
                    dve.wait_ge(m_scores.sem, m_scores.at(layer, i + 1))
                    link(dve.tensor_reduce(mx[:, j:j + 3:2, t], ps[:, i, :].rearrange("p (g n) -> p g n", g=2),
                                           AX_X, ALU.max))
                    dve.scalar_tensor_tensor(nm[:, j:j + 3:2, t], mx[:, j:j + 3:2, t], -1.0,
                                             qscale[:, t, j:j + 3:2], ALU.mult, ALU.mult).then_inc(m_max.sem, 1)

                def mem_probT(i):
                    dve.wait_ge(m_pT_ps.sem, m_pT_ps.at(layer, i + 1))
                    dve.tensor_copy(m_probT[i], ps[:, 4 + i % 2, :]).then_inc(m_pT_dve.sem, 1)

                def mem_out(t):
                    dve.wait_ge(m_probs.sem, m_probs.at(layer, 2 * t + 2))
                    link(dve.reciprocal(rz[:, 0:MEM_HEADS, t], zs[:, 0:MEM_HEADS, t]))
                    dve.wait_ge(m_pv.sem, m_pv.at(layer, 2 * t + 2))
                    dve.tensor_tensor(om[:, t, :].rearrange("p (h d) -> p h d", d=HD),
                                      ps[:, 6 + t, 0:MEM_W].rearrange("p (h d) -> p h d", d=HD),
                                      rz[:, 0:MEM_HEADS, t].unsqueeze(2).to_broadcast((P, MEM_HEADS, HD)), ALU.mult)\
                       .then_inc(om_ready.sem, 1)

                def mem_lo(t):
                    dve.wait_ge(om_hi.sem, om_hi.at(layer, t + 1))
                    tok = slice(t * P, (t + 1) * P)
                    dve.tensor_tensor(tlo[:, 0:2, tok], ps[:, 6 + t, SEQ:2 * SEQ].rearrange("p (j n) -> p j n", j=2),
                                      thi[:, 0:2, tok].bitcast(F32), ALU.subtract).then_inc(om_lo.sem, 1)

                for t in range(T):
                    q_scale(t)
                    mem_max(2 * t)
                    mem_max(2 * t + 1)
                mem_out(0)
                mem_probT(2)
                mem_probT(3)
                mem_lo(0)
                mem_out(1)
                mem_lo(1)
                for t in range(T):
                    add_to_x(layer, 1, t, (U_MO,), lambda t, c: (2, 0)[t] + c)
                    gain_tile(layer, 1, t, g_ffn)

                for q in range(4):
                    x_lo(layer, X_FFN, q)
                roots_of_x(layer, 1, 2)
                dve.wait_ge(rs_ready.sem, rs_ready.at(layer, 2))
                for t in range(T):
                    ins = dve.tensor_scalar(rs_diag[:, t * P:(t + 1) * P], ident, rs[:, 1, t:t + 1], None, ALU.mult)
                ins.then_inc(diag_ready.sem, 1)
                dve.wait_ge(row_ps.sem, row_ps.at(layer, 1))
                dve.tensor_copy(rs_row, ps[:, 2, 0:SEQ]).then_inc(row_out.sem, 1)
                dve.wait_ge(row_out.sem, row_out.at(layer, 1))

                def gate_step(pair, b):
                    dve.wait_ge(used[(U_FFN + b) % RING].sem, used_after(layer, U_FFN + b, pair))
                    if not_first(pair):
                        dve.wait_ge(silu_done.sem, silu_done.at(layer, pair * 2 + b - 1))
                    dve.tensor_tensor(gate_n[b], ps[:, b, 0:256], rs_row, ALU.mult).then_inc(gate_done.sem, 1)

                def glu_step(pair, b):
                    f = pair * 2 + b
                    dve.wait_ge(silu_done.sem, silu_done.at(layer, f + 1))
                    dve.tensor_tensor(act_f[b], ps[:, b, 256:512], silu_g[b], ALU.mult).then_inc(glu.sem, 1)
                    dve.wait_ge(glu.sem, glu.at(layer, f + 1))
                    if not_first(pair):
                        if b == 0:
                            dve.wait_ge(down_even.sem, down_even.at(layer, pair))
                        else:
                            dve.wait_ge(used[(U_FFN + 2) % RING].sem, used_after(layer, U_FFN + 2, pair - 1))
                    dve.tensor_copy(ahi[b][:], act_f[b]).then_inc(act_hi.sem, 1)
                    dve.wait_ge(act_hi.sem, act_hi.at(layer, f + 1))
                    dve.tensor_tensor(alo[b][:], act_f[b], ahi[b][:].bitcast(F32), ALU.subtract)\
                       .then_inc(act_lo.sem, 1)

                gate_step(0, 0)
                glu_step(0, 0)
                split_lo(layer, U_FFN, 1)
                gate_step(0, 1)
                glu_step(0, 1)
                split_lo(layer, U_FFN + 1, 1)
                with dve.Fori(1, PAIRS - 1) as i:
                    gate_step(i, 0)
                    glu_step(i, 0)
                    split_lo(layer, U_FFN, i + 1)
                    split_lo(layer, U_FFN + 2, i)
                    gate_step(i, 1)
                    glu_step(i, 1)
                    split_lo(layer, U_FFN + 1, i + 1)
                gate_step(PAIRS - 1, 0)
                glu_step(PAIRS - 1, 0)
                split_lo(layer, U_FFN + 2, PAIRS - 1)
                gate_step(PAIRS - 1, 1)
                glu_step(PAIRS - 1, 1)
                for t in range(T):
                    add_to_x(layer, 2, t, (U_FFN + 2, PAIRS - 1), lambda t, c: 4 + 2 * c + t, rs[:, 1, :])
                    if layer + 1 < DEPTH:
                        if t == 0:
                            dve.wait_ge(s_gmix.sem, s_gmix.at(layer, 16))
                        else:
                            for q in range(2):
                                x_lo(layer + 1, X_MIX, q)
                        gain_tile(layer, 2, t, g_mix)

        @block.tensor
        def _(pe):
            def build_x(layer, b, q):
                t, h = divmod(q, 2)
                pe.wait_ge(xn_ready.sem, xn_ready.at(layer, 4 * b + q + 1))
                for k in range(4):
                    ins = pe.transpose(ps[:, X_BANKS[b][q], k * P:(k + 1) * P],
                                       xn[:, t, (4 * h + k) * P:(4 * h + k + 1) * P], ident)
                ins.then_inc(t_ps.sem, 1)

            def build_half(layer, b, h):
                for k in range(4):
                    for t in range(T):
                        a = k * SEQ + t * P
                        ins = pe.transpose(ps[:, H_BANKS[b][h] + a // 512, a % 512:a % 512 + P],
                                           xn[:, t, (4 * h + k) * P:(4 * h + k + 1) * P], ident)
                ins.then_inc(h_ps.sem, 1)

            def products(layer, u, tiles, acc, chunks=4, k0=0, first=False, last=False, built=None, done=True, cols=512):
                s = u % RING
                pe.wait_ge(hi_done[s].sem, hi_done[s].at(layer, fill(u) + 1))
                n = min(cols, 512)
                if built is not None:
                    pe.wait_ge(built[0].sem, built[0].at(layer, built[2]))
                parts = [(thi, whi), (thi, wlo), (tlo, whi)]
                if layer == 0 and u < 2:
                    parts = [(thi, whi), (tlo, whi), (thi, wlo)]
                for part, (x_part, w_part) in enumerate(parts):
                    if x_part is tlo and built is not None:
                        pe.wait_ge(built[1].sem, built[1].at(layer, built[2]))
                    if w_part is wlo:
                        pe.wait_ge(lo_done[s].sem, lo_done[s].at(layer, fill(u) + 1))
                    for k in range(chunks):
                        for t in tiles:
                            for c in range(cols // n):
                                a = k * cols + c * n
                                ins = pe.matmul(acc(t, c), x_part[:, k0 + k, t * P:(t + 1) * P], w_part[s][:, a:a + n],
                                                start=first and k == 0 and part == 0,
                                                stop=last and k == chunks - 1 and part == 2)
                if done:
                    ins.then_inc(used[s].sem, 1)
                return ins

            pe.wait_ge(s_ident.sem, 16)
            for layer in range(DEPTH):
                for q in range(2):
                    build_x(layer, X_MIX, q)

                def transpose_qk(part, half, bank):
                    for j in range(4 * half, 4 * half + 4):
                        for t in range(T):
                            a = (j % 4) * SEQ + t * P
                            ins = pe.transpose(ps[:, bank + a // 512, a % 512:a % 512 + P],
                                               qkv[:, t, part * D + j * P:part * D + (j + 1) * P], ident)
                    ins.then_inc(qkT_ps.sem, 1)

                for c in range(NCHUNK):
                    if c >= 2:
                        pe.wait_ge(proj_out.sem, proj_out.at(layer, c - 1))
                    if c == 5:
                        pe.wait_ge(roped.sem, roped.at(layer, 1))
                        for half in range(2):
                            transpose_qk(0, half, 2 * half)

                    def acc(t, _):
                        return ps[:, 4 + 2 * (c % 2) + t, :]

                    if c == 0:
                        if layer == 0:
                            for q in range(2, 4):
                                build_x(layer, X_MIX, q)
                            for h in range(2):
                                products(layer, U_QKV + h, range(T), acc, k0=4 * h, first=h == 0, last=h == 1,
                                         built=(t_hi, t_lo, 4 * X_MIX + 4))
                            continue
                        for t in range(T):
                            for h in range(2):
                                if t == 0 and h == 1:
                                    for q in range(2, 4):
                                        build_x(layer, X_MIX, q)
                                products(layer, U_QKV + h, (t,), acc, k0=4 * h, first=h == 0, last=h == 1,
                                         built=(t_hi, t_lo, 4 * X_MIX + 2 * t + h + 1), done=t == 1)
                        continue
                    for h in range(2):
                        if c == 5 and h == 1:
                            pe.wait_ge(roped.sem, roped.at(layer, 2))
                            pe.wait_ge(roped_dve.sem, roped_dve.at(layer, 1))
                            pe.wait_ge(qkT_act.sem, qkT_act.at(layer, 1))
                            pe.wait_ge(qkT_dve.sem, qkT_dve.at(layer, 1))
                            for half in range(2):
                                transpose_qk(1, half, 2 * half)
                            continue
                        products(layer, U_QKV + 2 * c + h, range(T), acc, k0=4 * h, first=h == 0, last=h == 1)

                def score(n):
                    h, base, rows = SOFTMAXES[n]
                    if n >= 2:
                        pe.wait_ge(masked.sem, masked.at(layer, n - 1))
                    j = h // 2
                    q, k = qT[base:base + rows, j, :], kT[base:base + rows, j, :]
                    pe.matmul(ps[:, n % 2, 0:P], q[:, 0:P], k[:, 0:P], start=True, stop=True)
                    pe.matmul(ps[:, n % 2, P:3 * P], q[:, P:2 * P], k, start=True, stop=True)\
                      .then_inc(scores.sem, 1)

                def transpose_p(m):
                    n = 2 * m if m < DIFF else m + DIFF
                    if m < DIFF:
                        pe.wait_ge(combined.sem, combined.at(layer, m + 1))
                    else:
                        pe.wait_ge(probs.sem, probs.at(layer, n + 1))
                    if m >= 2:
                        if m % 2:
                            pe.wait_ge(pT_dve.sem, pT_dve.at(layer, m // 2))
                        else:
                            pe.wait_ge(pT_act.sem, pT_act.at(layer, m // 2))
                    for b in range(3):
                        ins = pe.transpose(ps[:, 2 + m % 2, b * P:(b + 1) * P], prob[n % 4][:, b * P:(b + 1) * P], ident)
                    ins.then_inc(pT_ps.sem, 1)

                def weigh_v(m):
                    if m % 2:
                        pe.wait_ge(pT_dve.sem, pT_dve.at(layer, m // 2 + 1))
                    else:
                        pe.wait_ge(pT_act.sem, pT_act.at(layer, m // 2 + 1))
                    if m == 8:
                        pe.wait_ge(o_read.sem, o_read.at(layer, 1))
                        pe.wait_ge(proj_out.sem, proj_out.at(layer, NCHUNK))
                    p = probT[m % 3]
                    a = (m % 8) * HD
                    v = qkv[:, :, 2 * D + m * HD:2 * D + (m + 1) * HD]
                    pe.matmul(ps[:, 4, a:a + HD], p[:, 0:P], v[:, 0, :], start=True, stop=True)
                    pe.matmul(ps[:, 5, a:a + HD], p[:, P:2 * P], v[:, 0, :], start=True, stop=False)
                    pe.matmul(ps[:, 5, a:a + HD], p[:, 2 * P:3 * P], v[:, 1, :], start=False, stop=True)\
                      .then_inc(pv.sem, 1)

                def qkv_piece(i):
                    u = U_MKV - 1
                    s = u % RING
                    k, t = HALF + i // 2, i % 2
                    if i == 0:
                        pe.wait_ge(lo_done[s].sem, lo_done[s].at(layer, fill(u) + 1))
                    cols = slice((k % 4) * 512, (k % 4) * 512 + 512)
                    tok = slice(t * P, (t + 1) * P)
                    acc = ps[:, 6 + t, :]
                    pe.matmul(acc, thi[:, k, tok], whi[s][:, cols], start=False, stop=False)
                    pe.matmul(acc, thi[:, k, tok], wlo[s][:, cols], start=False, stop=False)
                    ins = pe.matmul(acc, tlo[:, k, tok], whi[s][:, cols], start=False, stop=(k == KC - 1))
                    if i == 7:
                        ins.then_inc(used[s].sem, 1)

                def mem_piece(i):
                    k, t = i // 2, i % 2
                    u = U_MKV + k // 4
                    s = u % RING
                    if i % 8 == 0:
                        pe.wait_ge(lo_done[s].sem, lo_done[s].at(layer, fill(u) + 1))
                    if i == 0:
                        pe.wait_ge(h_lo.sem, h_lo.at(layer, 2 * B_MEM + 2))
                    cols = slice((k % 4) * 512, (k % 4) * 512 + 512)
                    tok = slice(t * P, (t + 1) * P)
                    acc = ps[:, 6 + t, :]
                    pe.matmul(acc, thi[:, k, tok], whi[s][:, cols], start=(k == 0), stop=False)
                    pe.matmul(acc, thi[:, k, tok], wlo[s][:, cols], start=False, stop=False)
                    ins = pe.matmul(acc, tlo[:, k, tok], whi[s][:, cols], start=False, stop=(k == KC - 1))
                    if i % 8 == 7:
                        ins.then_inc(used[s].sem, 1)

                pe.wait_ge(qkT_act.sem, qkT_act.at(layer, 2))
                for n in range(NS + V_LAG[1] + 1):
                    if n < NS and SOFTMAXES[n][0] == 8:
                        pe.wait_ge(qkT_dve.sem, qkT_dve.at(layer, 2))
                    if n < NS:
                        score(n)
                    for i in range(QKV_PIECES[n], QKV_PIECES[n + 1]):
                        qkv_piece(i)
                    if n == MEM_AT[0]:
                        pe.wait_ge(xm_ready.sem, xm_ready.at(layer, 1))
                        pe.wait_ge(proj_out.sem, proj_out.at(layer, NCHUNK))
                        build_half(layer, B_MEM, 0)
                    if n == MEM_AT[1]:
                        pe.wait_ge(h_lo.sem, h_lo.at(layer, 2 * B_MEM + 1))
                        build_half(layer, B_MEM, 1)
                    for i in range(MEM_PIECES[n], MEM_PIECES[n + 1]):
                        mem_piece(i)
                    if n == NS + 1:
                        pe.wait_ge(heads_ready.sem, heads_ready.at(layer, 1))
                        pe.wait_ge(masked.sem, masked.at(layer, NS))
                        build_half(layer, B_HEADS, 0)
                    for m in range(HEADS):
                        if LAST_OF[m] + T_LAG == n:
                            transpose_p(m)
                        if LAST_OF[m] + V_LAG[m // 8] == n:
                            weigh_v(m)

                def out_acc(c):
                    return lambda t, _: ps[:, (6, 4)[c] + t, :]

                pe.wait_ge(mkv_out.sem, mkv_out.at(layer, 1))
                products(layer, U_OUT, range(T), out_acc(0), first=True, built=(h_hi, h_lo, 2 * B_HEADS + 1))
                pe.wait_ge(heads_ready.sem, heads_ready.at(layer, 2))
                pe.wait_ge(pT_dve.sem, pT_dve.at(layer, HEADS // 2))
                build_half(layer, B_HEADS, 1)
                products(layer, U_OUT + 1, range(T), out_acc(1), first=True)
                products(layer, U_OUT + 2, (0,), out_acc(0), k0=4, last=True, built=(h_hi, h_lo, 2 * B_HEADS + 2),
                         done=False)
                products(layer, U_OUT + 3, (0,), out_acc(1), k0=4, last=True, done=False).then_inc(t0_done.sem, 1)
                pe.wait_ge(km_ready.sem, km_ready.at(layer, 1))
                for j in range(2):
                    for t in range(T):
                        a = j * SEQ + t * P
                        ins = pe.transpose(ps[:, 3, a:a + P], kvm[:, t, j * P:(j + 1) * P], ident)
                ins.then_inc(kmT_ps.sem, 1)
                products(layer, U_OUT + 2, (1,), out_acc(0), k0=4, last=True)
                for q in range(2):
                    build_x(layer, X_CROSS, q)
                products(layer, U_OUT + 3, (1,), out_acc(1), k0=4, last=True)

                def transpose_pair(src, t, bank, col, sig):
                    for j in range(2):
                        ins = pe.transpose(ps[:, bank, col + j * P:col + (j + 1) * P], src[:, t, j * P:(j + 1) * P], ident)
                    ins.then_inc(sig.sem, 1)

                for t in range(T):
                    if t == 1:
                        pe.wait_ge(kmT_out.sem, kmT_out.at(layer, 1))
                        for q in range(2, 4):
                            build_x(layer, X_CROSS, q)
                        pe.wait_ge(mq_out.sem, mq_out.at(layer, 1))
                        transpose_pair(qm, 0, 6, 0, qmT_ps)
                    for h in range(2):
                        ins = products(layer, U_MQ + h, (t,), lambda t, _: ps[:, 4 + t, 0:MEM_W], k0=4 * h,
                                       first=h == 0, last=h == 1, done=False, cols=MEM_W,
                                       built=(t_hi, t_lo, 4 * X_CROSS + 2 * t + h + 1))
                        if t == 1:
                            ins.then_inc(used[(U_MQ + h) % RING].sem, 1)
                        elif h == 1:
                            ins.then_inc(mq_sum.sem, 1)

                def mem_score(t):
                    pe.wait_ge(qmT_out.sem, qmT_out.at(layer, t + 1))
                    for i in (2 * t, 2 * t + 1):
                        for g in (i % 2, i % 2 + 2):
                            base, j = (g % 2) * HD, g // 2
                            ins = pe.matmul(ps[:, i, 256 * j:256 * j + 256],
                                            qmT[base:base + HD, j, t * P:(t + 1) * P], kmT[base:base + HD, j, :],
                                            start=True, stop=True)
                        ins.then_inc(m_scores.sem, 1)

                def mem_transpose_p(i):
                    pe.wait_ge(m_probs.sem, m_probs.at(layer, i + 1))
                    if i >= 2:
                        pe.wait_ge(m_pT_act.sem, m_pT_act.at(layer, i - 1))
                    for a in range(0, 512, P):
                        ins = pe.transpose(ps[:, 4 + i % 2, a:a + P], prob[i][:, a:a + P], ident)
                    ins.then_inc(m_pT_ps.sem, 1)

                def mem_weigh_v(i):
                    if i < 2:
                        pe.wait_ge(m_pT_act.sem, m_pT_act.at(layer, i + 1))
                    else:
                        pe.wait_ge(m_pT_dve.sem, m_pT_dve.at(layer, i - 1))
                    t = i // 2
                    for g in (i % 2, i % 2 + 2):
                        for k in range(T):
                            a = (g // 2) * 256 + k * P
                            ins = pe.matmul(ps[:, 6 + t, g * HD:(g + 1) * HD], m_probT[i][:, a:a + P],
                                            kvm[:, k, MEM_W + g * HD:MEM_W + (g + 1) * HD],
                                            start=(k == 0), stop=(k == T - 1))
                    ins.then_inc(m_pv.sem, 1)

                mem_score(0)
                pe.wait_ge(mq_out.sem, mq_out.at(layer, 2))
                transpose_pair(qm, 1, 7, 0, qmT_ps)
                mem_score(1)
                mem_transpose_p(0)
                mem_transpose_p(1)
                mem_weigh_v(0)
                mem_weigh_v(1)
                mem_transpose_p(2)
                mem_transpose_p(3)
                pe.wait_ge(om_ready.sem, om_ready.at(layer, 1))
                transpose_pair(om, 0, 6, SEQ, omT_ps)
                mem_weigh_v(2)
                mem_weigh_v(3)

                def mo_acc(t, c):
                    return ps[:, (2, 0)[t] + c, :]

                pe.wait_ge(om_ready.sem, om_ready.at(layer, 2))
                transpose_pair(om, 1, 7, SEQ, omT_ps)
                products(layer, U_MO, (0,), mo_acc, chunks=2, first=True, last=True, done=False, cols=D,
                         built=(om_hi, om_lo, 1)).then_inc(t0_done.sem, 1)
                products(layer, U_MO, (1,), mo_acc, chunks=2, first=True, last=True, cols=D, built=(om_hi, om_lo, 2))

                for q in range(4):
                    build_x(layer, X_FFN, q)

                def gate_up(pair, b):
                    s = (U_FFN + b) % RING
                    pe.wait_ge(hi_done[s].sem, hi_done[s].at(layer, fill(U_FFN + b, pair) + 1))
                    if not_first(pair):
                        pe.wait_ge(glu.sem, glu.at(layer, pair * 2 + b - 1))
                    for j in range(2):
                        acc = ps[:, b, 256 * j:256 * j + 256]
                        for part, (w_part, x_part) in enumerate(((whi, thi), (wlo, thi), (whi, tlo))):
                            if part == 1 and j == 0:
                                pe.wait_ge(lo_done[s].sem, lo_done[s].at(layer, fill(U_FFN + b, pair) + 1))
                            if part == 2 and j == b == 0 and not not_first(pair):
                                pe.wait_ge(t_lo.sem, t_lo.at(layer, 4 * X_FFN + 4))
                            for k in range(KC):
                                a = (2 * k + j) * P
                                ins = pe.matmul(acc, w_part[s][:, a:a + P], x_part[:, k, :],
                                                start=(k == 0 and part == 0), stop=(k == KC - 1 and part == 2))
                    ins.then_inc(used[s].sem, 1)

                def down(pair, b, first=False, last=False):
                    s = (U_FFN + 2) % RING
                    if b == 0:
                        pe.wait_ge(lo_done[s].sem, lo_done[s].at(layer, fill(U_FFN + 2, pair) + 1))
                    pe.wait_ge(act_lo.sem, act_lo.at(layer, pair * 2 + b + 1))
                    for t in range(T):
                        for c in range(2):
                            a = b * D + c * 512
                            acc = ps[:, 4 + 2 * c + t, :]
                            tok = slice(t * P, (t + 1) * P)
                            pe.matmul(acc, ahi[b][:, tok], whi[s][:, a:a + 512], start=first, stop=False)
                            pe.matmul(acc, ahi[b][:, tok], wlo[s][:, a:a + 512], start=False, stop=False)
                            ins = pe.matmul(acc, alo[b][:, tok], whi[s][:, a:a + 512], start=False, stop=last)
                        if last and t == 0:
                            ins.then_inc(t0_done.sem, 1)
                    ins.then_inc((down_even.sem, used[s].sem)[b], 1)

                pe.wait_ge(t_hi.sem, t_hi.at(layer, 4 * X_FFN + 4))
                gate_up(0, 0)
                if layer == 0:
                    pe.wait_ge(s_ones.sem, 1)
                pe.wait_ge(diag_ready.sem, diag_ready.at(layer, 1))
                pe.matmul(ps[:, 2, 0:SEQ], ones[:], rs_diag, start=True, stop=True).then_inc(row_ps.sem, 1)
                gate_up(0, 1)
                down(0, 0, first=True)
                with pe.Fori(1, PAIRS) as i:
                    gate_up(i, 0)
                    down(i - 1, 1)
                    gate_up(i, 1)
                    down(i, 0)
                down(PAIRS - 1, 1, last=True)


X_BANKS = {X_MIX: (0, 1, 2, 3), X_CROSS: (0, 1, 2, 3), X_FFN: (6, 7, 4, 5)}
H_BANKS = {B_MEM: (6, 6), B_HEADS: (0, 2)}
QKV_PIECES = [min(2 * n, 8) for n in range(NS + 6)]
MEM_AT = (7, 8)
MEM_PIECES = [min(max((n - 9) * 16 // 12, 0), 16) for n in range(NS + 6)]
V_OUT_AT = 5
POOL_LO = (10, 12, 13)
T_LAG, V_LAG = 2, (3, 4)
HALF_AT = LAST_OF[7] + V_LAG[0] + 1
N_SMALL = 3 * HD + 4 * 32
N_TABLE = 6 * P


def not_first(pair):
    return not isinstance(pair, int) or pair > 0


def lam_init(layer):
    return 0.8 - 0.6 * math.exp(-0.3 * layer)


def split_two_pi():
    parts, left = [], 2.0 * math.pi
    for bits in (5, 13, 21):
        c = math.floor(left * 2.0 ** bits) / 2.0 ** bits
        parts.append(c)
        left -= c
    return parts + [left]


TWO_PI = split_two_pi()


def mask_table():
    q = np.arange(SEQ)[:, None]
    k = np.arange(SEQ)[None, :]
    d = q - k
    count = [(d >= 0).astype(np.float64),
             (((d >= 0) & (d <= 128)).astype(np.float64) + ((d >= 0) & (d % 4 == 0)) + ((d >= 0) & (d % 16 == 0)))]
    table = np.full((P, 2, 3 * P), NEG, np.float32)
    for kind, c in enumerate(count):
        m = np.where(c > 0, np.log(np.maximum(c, 1.0)) * math.sqrt(HD), NEG).astype(np.float32)
        table[:, kind, 0:P] = m[0:P, 0:P]
        table[:, kind, P:3 * P] = m[P:2 * P, :]
    return table


def freq_table():
    parts = [THETA ** (-np.arange(half, dtype=np.float32) / np.float32(half)) for half in (4, 8)]
    return np.tile(np.concatenate(parts).astype(np.float32), (P, 1))


WEIGHTS = ("w_in", "w_out", "w_mq", "w_mkv", "w_mo", "w_gate_up", "w_down")
GAINS = ("norm_mix", "norm_cross", "norm_mem", "norm_ffn")
SMALL = ("subln_diff", "qn_mem", "kn_mem", "lambda_q1", "lambda_k1", "lambda_q2", "lambda_k2")


def kernel(**inputs):
    import concourse.bacc as bacc
    from concourse.bass_utils import run_bass_kernel_spmd

    nc = bacc.Bacc("TRN2", target_bir_lowering=False, num_devices=1)
    arrays = {}

    def put(name, a):
        a = np.ascontiguousarray(a)
        arrays[f"in_{name}"] = a
        return nc.dram_tensor(f"in_{name}", a.shape, mybir.dt.from_np(a.dtype), kind="ExternalInput").ap()

    def tiled(kind):
        parts = [np.tile(np.asarray(inputs[f"{kind}_{n}"]), (1, reps))
                 for n, reps in (("diff", 2 * DIFF), ("dil", DIL), ("moba", MOBA))]
        return np.concatenate(parts, axis=1)

    x = put("x", inputs["x"])
    mem = put("mem", inputs["mem"])
    positions = put("positions", inputs["positions"])
    w = {n: put(n, inputs[n]) for n in WEIGHTS}
    gains = {n: put(n, inputs[n]) for n in GAINS}
    gains["q_gain"] = put("q_gain", tiled("qn"))
    gains["k_gain"] = put("k_gain", tiled("kn"))
    gains["small"] = put("small", np.concatenate([np.asarray(inputs[n]) for n in SMALL], axis=1).reshape(1, -1))
    consts = {"table": put("table", mask_table().reshape(P, -1)), "freqs": put("freqs", freq_table()),
              "ident": put("ident", np.eye(P, dtype=np.float32))}
    out = nc.dram_tensor("out", (1, SEQ, D), F32, kind="ExternalOutput").ap()
    trunk(nc, x, mem, positions, w, gains, consts, out)
    r = run_bass_kernel_spmd(nc, [arrays], core_ids=[0])
    return r.results[0]["out"]
```
